# Optimizing a Trainium2 kernel written in Bass

```python
import math
import jax, jax.numpy as jnp
from jax import lax
import numpy as np

D_MODEL = 1024
BATCH = 1
SEQ = 512
DEPTH = 2

HEAD_DIM = 64
BLOCK = 128
DIL_GROUPS = ((128, 1), (512, 4), (2048, 16))
N_GROUPS = 3
A_HEADS_PER_GROUP = 4
A_HEADS = N_GROUPS * A_HEADS_PER_GROUP
A_WIDTH = A_HEADS * HEAD_DIM
A_OUT = A_HEADS_PER_GROUP * HEAD_DIM
SB_HEADS = 4
SB_HEAD_DIM = 128
SB_WIDTH = SB_HEADS * SB_HEAD_DIM
RET_HEADS = 4
RET_DK = 64
RET_DV = 128
RET_QK_WIDTH = RET_HEADS * RET_DK
RET_V_WIDTH = RET_HEADS * RET_DV
RET_CHUNK = 128
ROPE_BASE = 10000.0
REL_BUCKETS = 32
REL_MAX_DIST = 2048
N_BRANCH = 3
D_FF = 2816
CONV_WIDTH = 3
EPS = 1e-6

IN_SIZES = (A_WIDTH,) * 3 + (SB_WIDTH,) * 3 + (RET_QK_WIDTH,) * 2 + (RET_V_WIDTH,) * 2 + (N_BRANCH * D_MODEL,)
IN_WIDTH = 3 * A_WIDTH + 3 * SB_WIDTH + 2 * RET_QK_WIDTH + 2 * RET_V_WIDTH + N_BRANCH * D_MODEL

kernel_name = "hybrid_dilated_stickbreak_retention_convffn"

def rms_norm(x, w):
    xf = x.astype(jnp.float32)
    y = xf * lax.rsqrt(jnp.mean(xf * xf, axis=-1, keepdims=True) + EPS)
    return (y * w.astype(jnp.float32)).astype(x.dtype)

def t5_causal_bucket(dist):
    max_exact = REL_BUCKETS // 2
    n = np.maximum(dist, 0)
    large = max_exact + (np.log(np.maximum(n, 1) / max_exact) / np.log(REL_MAX_DIST / max_exact)
                         * (REL_BUCKETS - max_exact)).astype(np.int64)
    large = np.minimum(large, REL_BUCKETS - 1)
    return np.where(n < max_exact, n, large).astype(np.int32)

def dilated_window_attention(q, k, v, bias_hd, window, dilation):
    b, s, h, hd = q.shape
    n_steps = window // dilation
    span = dilation * BLOCK
    sp = -(-s // span) * span
    L = sp // dilation
    nb = L // BLOCK

    def to_blocks(t):
        t = jnp.pad(t, ((0, 0), (0, sp - s), (0, 0), (0, 0))).reshape(b, L, dilation, h, hd)
        return t.transpose(0, 2, 1, 3, 4).reshape(b, dilation, nb, BLOCK, h, hd)

    def with_prev(t):
        prev = jnp.pad(t, ((0, 0), (0, 0), (1, 0), (0, 0), (0, 0), (0, 0)))[:, :, :-1]
        return jnp.concatenate([prev, t], axis=3)

    qb = to_blocks(q)
    kw = with_prev(to_blocks(k))
    vw = with_prev(to_blocks(v))

    a_idx = np.arange(BLOCK)[:, None]
    c_idx = np.arange(2 * BLOCK)[None, :]
    steps = a_idx + BLOCK - c_idx
    in_band = (steps >= 0) & (steps <= n_steps)
    valid = in_band[None] & ((np.arange(nb)[:, None, None] > 0) | (c_idx[None] >= BLOCK))
    bucket = t5_causal_bucket(steps * dilation)
    bias = jnp.take(bias_hd.astype(jnp.float32), jnp.asarray(bucket), axis=0).transpose(2, 0, 1)

    logits = jnp.einsum('bdnqhc,bdnkhc->bdnhqk', qb, kw).astype(jnp.float32) * (hd ** -0.5) + bias
    logits = jnp.where(valid[None, None, :, None], logits, -jnp.inf)
    lse = jax.nn.logsumexp(logits, axis=-1)
    p = jnp.exp(logits - lse[..., None])
    out = jnp.einsum('bdnhqk,bdnkhc->bdnqhc', p.astype(v.dtype), vw)

    out = out.reshape(b, dilation, L, h, hd).transpose(0, 2, 1, 3, 4).reshape(b, sp, h, hd)[:, :s]
    lse = lse.transpose(0, 1, 2, 4, 3).reshape(b, dilation, L, h).transpose(0, 2, 1, 3).reshape(b, sp, h)[:, :s]
    return out, lse

def stick_breaking_attention(q, k, v):
    b, s, h, hd = q.shape
    nb = s // BLOCK
    scale = hd ** -0.5
    kb = k.reshape(b, nb, BLOCK, h, hd)
    vb = v.reshape(b, nb, BLOCK, h, hd)
    tri_in = jnp.asarray(np.arange(BLOCK)[:, None] > np.arange(BLOCK)[None, :], jnp.float32)
    diag_mask = np.arange(BLOCK)[None, :] < np.arange(BLOCK)[:, None]
    outs = []
    for i in range(nb):
        n = i + 1
        qi = q[:, i * BLOCK:(i + 1) * BLOCK]
        z = jnp.einsum('bqhc,bnkhc->bhqnk', qi, kb[:, :n]).astype(jnp.float32) * scale
        mask_np = np.ones((BLOCK, n, BLOCK), dtype=bool)
        mask_np[:, -1, :] = diag_mask
        mask = jnp.asarray(mask_np)
        log_keep = jnp.where(mask, jax.nn.log_sigmoid(-z), 0.0)
        later_in = jnp.einsum('bhqnk,kj->bhqnj', log_keep, tri_in)
        tri_blk = jnp.asarray(np.arange(n)[:, None] > np.arange(n)[None, :], jnp.float32)
        later_blk = jnp.einsum('bhqm,mn->bhqn', jnp.sum(log_keep, axis=-1), tri_blk)
        log_w = jnp.where(mask, log_keep + z + later_in + later_blk[..., None], -jnp.inf)
        w = jnp.exp(log_w)
        outs.append(jnp.einsum('bhqnk,bnkhc->bqhc', w.astype(v.dtype), vb[:, :n]))
    return jnp.concatenate(outs, axis=1)

def rotary(x, pos):
    half = x.shape[-1] // 2
    inv = ROPE_BASE ** (-jnp.arange(half, dtype=jnp.float32) / half)
    ang = pos.astype(jnp.float32)[:, None] * inv[None, :]
    cos = jnp.cos(ang)[None, :, None, :]
    sin = jnp.sin(ang)[None, :, None, :]
    x1 = x[..., :half].astype(jnp.float32)
    x2 = x[..., half:].astype(jnp.float32)
    return jnp.concatenate([x1 * cos - x2 * sin, x1 * sin + x2 * cos], axis=-1)

def retention(q, k, v):
    b, s, h, dk = q.shape
    dv = v.shape[-1]
    C = RET_CHUNK
    nc = s // C
    log_gamma = jnp.log1p(-jnp.exp2(-5.0 - jnp.arange(h, dtype=jnp.float32)))
    pos = jnp.arange(s, dtype=jnp.int32)
    qc = rotary(q, pos).reshape(b, nc, C, h, dk)
    kc = (rotary(k, pos) * (dk ** -0.5)).reshape(b, nc, C, h, dk)
    vc = v.astype(jnp.float32).reshape(b, nc, C, h, dv)

    n = jnp.arange(C, dtype=jnp.float32)
    diff = n[:, None] - n[None, :]
    decay_intra = jnp.where(diff >= 0, jnp.exp(diff[None] * log_gamma[:, None, None]), 0.0)
    intra = jnp.einsum('bnqhd,bnkhd->bnhqk', qc, kc) * decay_intra
    o_intra = jnp.einsum('bnhqk,bnkhe->bnqhe', intra, vc)

    zeta = jnp.exp((C - 1 - n)[:, None] * log_gamma[None, :])
    kv = jnp.einsum('bnkhd,bnkhe->bnhde', kc * zeta[None, None, :, :, None], vc)
    chunk_decay = jnp.exp(C * log_gamma)[:, None, None]

    def step(r, kv_i):
        return r * chunk_decay + kv_i, r

    _, r_prev = lax.scan(step, jnp.zeros((b, h, dk, dv), jnp.float32), kv.transpose(1, 0, 2, 3, 4))
    r_prev = r_prev.transpose(1, 0, 2, 3, 4)
    xi = jnp.exp((n + 1)[:, None] * log_gamma[None, :])
    o_cross = jnp.einsum('bnqhd,bnhde->bnqhe', qc * xi[None, None, :, :, None], r_prev)
    return (o_intra + o_cross).reshape(b, s, h, dv)

def conv_ffn(h, w_up, w_gate, conv_w, conv_b, w_down):
    u = h @ w_up
    u = lax.conv_general_dilated(u, conv_w[:, None, :].astype(u.dtype), window_strides=(1,),
                                 padding=((CONV_WIDTH - 1, 0),),
                                 dimension_numbers=('NWC', 'WIO', 'NWC'),
                                 feature_group_count=D_FF) + conv_b
    return (jax.nn.gelu(u) * (h @ w_gate)) @ w_down

def setup_inputs(seed: int = 0) -> dict:
    key = jax.random.key(seed)
    ks = jax.random.split(key, 20)
    f32 = jnp.float32
    nrm = lambda k, shape, fan: jax.random.normal(k, shape, f32) * (fan ** -0.5)
    return {
        "x": jax.random.normal(ks[0], (BATCH, SEQ, D_MODEL), f32),
        "rel_bias": jax.random.normal(ks[1], (REL_BUCKETS, A_HEADS), f32) * 0.5,
        "norm_mix_w": 1.0 + 0.01 * jax.random.normal(ks[2], (DEPTH, D_MODEL), f32),
        "w_in": nrm(ks[3], (DEPTH, D_MODEL, IN_WIDTH), D_MODEL),
        "b_gate": 0.1 * jax.random.normal(ks[4], (DEPTH, N_BRANCH, D_MODEL), f32),
        "ret_norm_w": 1.0 + 0.01 * jax.random.normal(ks[5], (DEPTH, RET_V_WIDTH), f32),
        "w_proj_a": nrm(ks[6], (DEPTH, A_OUT, D_MODEL), A_OUT),
        "w_proj_b": nrm(ks[7], (DEPTH, SB_WIDTH, D_MODEL), SB_WIDTH),
        "w_proj_c": nrm(ks[8], (DEPTH, RET_V_WIDTH, D_MODEL), RET_V_WIDTH),
        "w_out": nrm(ks[9], (DEPTH, D_MODEL, D_MODEL), D_MODEL),
        "norm_ffn_w": 1.0 + 0.01 * jax.random.normal(ks[10], (DEPTH, D_MODEL), f32),
        "w_up": nrm(ks[11], (DEPTH, D_MODEL, D_FF), D_MODEL),
        "w_gate": nrm(ks[12], (DEPTH, D_MODEL, D_FF), D_MODEL),
        "conv_w": nrm(ks[13], (DEPTH, CONV_WIDTH, D_FF), CONV_WIDTH),
        "conv_b": 0.01 * jax.random.normal(ks[14], (DEPTH, D_FF), f32),
        "w_down": nrm(ks[15], (DEPTH, D_FF, D_MODEL), D_FF),
        "final_norm_w": 1.0 + 0.01 * jax.random.normal(ks[16], (D_MODEL,), f32),
    }

def reference(x, rel_bias, norm_mix_w, w_in, b_gate, ret_norm_w, w_proj_a, w_proj_b, w_proj_c,
              w_out, norm_ffn_w, w_up, w_gate, conv_w, conv_b, w_down, final_norm_w):
    b, s, _ = x.shape
    offsets = np.cumsum(IN_SIZES)[:-1].tolist()
    for l in range(DEPTH):
        h = rms_norm(x, norm_mix_w[l])
        proj = h @ w_in[l]
        (a_q, a_k, a_v, sb_q, sb_k, sb_v, r_q, r_k, r_v, r_g, gate_in) = jnp.split(proj, offsets, axis=-1)

        a_q = a_q.reshape(b, s, N_GROUPS, A_HEADS_PER_GROUP, HEAD_DIM)
        a_k = a_k.reshape(b, s, N_GROUPS, A_HEADS_PER_GROUP, HEAD_DIM)
        a_v = a_v.reshape(b, s, N_GROUPS, A_HEADS_PER_GROUP, HEAD_DIM)
        outs, lses = [], []
        for g, (window, dilation) in enumerate(DIL_GROUPS):
            bias_g = rel_bias[:, g * A_HEADS_PER_GROUP:(g + 1) * A_HEADS_PER_GROUP]
            o_g, lse_g = dilated_window_attention(a_q[:, :, g], a_k[:, :, g], a_v[:, :, g], bias_g, window, dilation)
            outs.append(o_g)
            lses.append(lse_g)
        wts = jax.nn.softmax(jnp.stack(lses), axis=0)
        y_a = jnp.einsum('gbsh,gbshc->bshc', wts.astype(x.dtype), jnp.stack(outs)).reshape(b, s, A_OUT)

        y_b = stick_breaking_attention(sb_q.reshape(b, s, SB_HEADS, SB_HEAD_DIM),
                                       sb_k.reshape(b, s, SB_HEADS, SB_HEAD_DIM),
                                       sb_v.reshape(b, s, SB_HEADS, SB_HEAD_DIM)).reshape(b, s, SB_WIDTH)

        o_r = retention(r_q.reshape(b, s, RET_HEADS, RET_DK), r_k.reshape(b, s, RET_HEADS, RET_DK),
                        r_v.reshape(b, s, RET_HEADS, RET_DV))
        mu = jnp.mean(o_r, axis=-1, keepdims=True)
        var = jnp.mean(jnp.square(o_r - mu), axis=-1, keepdims=True)
        o_r = ((o_r - mu) * lax.rsqrt(var + EPS)).reshape(b, s, RET_V_WIDTH) * ret_norm_w[l].astype(jnp.float32)
        y_c = jax.nn.silu(r_g) * o_r.astype(x.dtype)

        gates = jax.nn.sigmoid(gate_in.reshape(b, s, N_BRANCH, D_MODEL) + b_gate[l])
        merged = (gates[:, :, 0] * (y_a @ w_proj_a[l]) + gates[:, :, 1] * (y_b @ w_proj_b[l])
                  + gates[:, :, 2] * (y_c @ w_proj_c[l]))
        x = x + merged @ w_out[l]

        h = rms_norm(x, norm_ffn_w[l])
        x = x + conv_ffn(h, w_up[l], w_gate[l], conv_w[l], conv_b[l], w_down[l])
    return rms_norm(x, final_norm_w)


_drawn_inputs = setup_inputs


def setup_inputs(seed=0):
    import zlib

    import numpy as np

    out = dict(_drawn_inputs(seed))
    spreads = {}
    factors = {'norm_mix_w': 4.589,
     'ret_norm_w': 8.0,
     'norm_ffn_w': 5.247,
     'conv_b': 7.553,
     'final_norm_w': 5.728}
    for name, (base, spread) in spreads.items():
        noise = np.random.default_rng([zlib.crc32(name.encode()), seed]).standard_normal(out[name].shape)
        drawn = base * np.exp(spread * noise) if base else spread * noise
        out[name] = __import__('jax').numpy.asarray(drawn.astype(out[name].dtype))
    for name, factor in factors.items():
        out[name] = (out[name] * factor).astype(out[name].dtype)
    return out
```

```python
from contextlib import ExitStack

import numpy as np

import concourse.bass as bass
from concourse import mybir
from concourse.alu_op_type import AluOpType as ALU

F32 = mybir.dt.float32
F32R = mybir.dt.float32r
ACT = mybir.ActivationFunctionType
AX_X = mybir.AxisListType.X

P = 128
D_MODEL, SEQ, DEPTH = 1024, 512, 2
KD = D_MODEL // P
NT = SEQ // P
GROUPS, SLOTS = 3, 4
HD = 64
D_FF = 2816
KF = D_FF // P
KHALF = KF // 2
REL_BUCKETS, REL_MAX_DIST = 32, 2048
EPS = 1e-6
MASKED = -1e30
SB_SCALE = 128.0 ** -0.5
NLE = "natural_log_exp_and_others"

A_CHUNKS, B_CHUNKS, C_CHUNKS = 18, 12, 12
S_M = A_CHUNKS + B_CHUNKS + C_CHUNKS
S_O = S_M + 4 * KD
S_F = S_O + KD
S_D = S_F + 2 * KF
SLABS = S_D + 2 * KD
K_PROJ = 10
SLAB_MAX = KHALF * P
GATE_BANKS = (0, 2, 3)

LINE1, LINE2 = 1024, 256
LINE = LINE1 + 2 * LINE2
EXT = SEQ + 3
TABLE = EXT + 2 * P

V_NORM, V_BGATE = 0, (2 * DEPTH + 1) * KD
V_CONV = V_BGATE + DEPTH * 3 * KD
V_RET = V_CONV + DEPTH * 4 * KF
VECS = V_RET + DEPTH * 4

DVE_STEPS, ACT_STEPS = 174, 38

COUNTS = {
    "raw_in0": (16 * (SLABS // 2), 0), "raw_in1": (16 * (SLABS // 2), 0),
    "hi_ready": (SLABS, 0), "split_done": (SLABS, 2), "slab_used": (SLABS, 2),
    "ms_ready": (2, 0), "y0_ready": (2, 0),
    "hf_ready": (2 * KD, 0), "h_hi_ready": (2 * KD, 0), "h_ready": (2 * KD, 0),
    "x_new": (2 * KD, 2), "sq_ready": (2 * KD, KD), "sum_added": (2 * KD, KD),
    "sum_cleared": (2, 0),
    "chunk_out": (S_M, 0), "vt_ready": (14, 0), "v_ready": (14, 0),
    "s_ready": (16, 0), "l_ready": (16, 0), "p_ready": (16, 0), "t_ready": (16, 0),
    "pt_ready": (16, 0), "o_ready": (16, 0), "o_used": (16, 0),
    "yt_ready": (4, 0), "ya_hi_ready": (4, 0), "ya_ready": (4, 0),
    "z_ready": (16, 0), "zs_ready": (16, 0), "e_ready": (16, 0), "sp_ready": (16, 0),
    "sfx_ready": (16, 0), "lw_ready": (16, 0), "w_ready": (16, 0),
    "yb_mm": (4, 0), "yb_hi_ready": (4, 0), "yb_ready": (4, 0),
    "rx_ready": (4, 0), "rot_ready": (4, 0),
    "st_ready": (16, 0), "decay_ready": (16, 0), "ret_ready": (4, 0), "ret_copied": (4, 0),
    "mu_ready": (4, 0), "cen_ready": (4, 0), "csq_ready": (4, 0), "var_ready": (4, 0),
    "cy0_ready": (4, 0), "yc_ready": (4, 0), "yc_hi_ready": (4, 0), "yc_split": (4, 0),
    "gate_ready": (3 * KD, 3), "m_ready": (KD, 1), "m_hi_ready": (KD, 0), "m_split": (KD, 1),
    "cv_ready": (KF, 0), "conv_done": (KF, 1), "gelu_ready": (KF, 0), "af_ready": (KF, 1),
    "af_hi_ready": (KF, 0), "af_split": (KF, 1),
    "dve_step": (DVE_STEPS, 0), "act_step": (ACT_STEPS, 0),
}
GRANTED = {"split_done": 2, "slab_used": 2, "x_new": 2, "gate_ready": 3, "m_ready": 1,
           "conv_done": 1, "af_ready": 1, "m_split": 1, "af_split": 1}


def trunk_program(nc, x_t, vectors, rel_bias, onehot, mats, decay, cos_sin, w_qkv, w_gates,
                  w_proj, w_o, w_upgate, w_down, line_dram, out_t):
    with ExitStack() as ctx:
        def sb(stack, name, shape, dtype=F32):
            return stack.enter_context(nc.sbuf_tensor(name, shape, dtype))

        x = sb(ctx, "x", [P, KD, SEQ])
        h_hi = sb(ctx, "h_hi", [P, KD, SEQ], F32R)
        h_lo = sb(ctx, "h_lo", [P, KD, SEQ], F32R)
        raw = [sb(ctx, f"raw{p}", [P, SLAB_MAX]) for p in range(2)]
        w_hi = [sb(ctx, f"w_hi{p}", [P, SLAB_MAX], F32R) for p in range(2)]
        w_lo = [sb(ctx, f"w_lo{p}", [P, SLAB_MAX], F32R) for p in range(2)]
        table = sb(ctx, "table", [P, SLOTS, TABLE])
        decays = sb(ctx, "decays", [P, 4, SEQ])
        rope = sb(ctx, "rope", [P, 2, SEQ])
        consts = sb(ctx, "consts", [P, 7, P])
        vecs = sb(ctx, "vecs", [P, VECS])
        stat = sb(ctx, "stat", [P, 4, 4])
        eps = sb(ctx, "eps", [P, 1])
        ones, ones_model, ones_head, tri, ident, rotate, neg_mask = (consts[:, i, :] for i in range(7))
        with ExitStack() as z:
            hf = [sb(z, f"hf{p}", [P, SEQ]) for p in range(2)]
            sumsq = sb(z, "sumsq", [P, SEQ])
            y0 = sb(z, "y0", [P, SEQ])
            rs = sb(z, "rs", [P, SEQ])
        square = hf
        with ExitStack() as z:
            cv = sb(z, "cv", [P, SEQ])
            af = sb(z, "af", [P, SEQ])
        with ExitStack() as z:
            vs = [sb(z, f"vs{p}", [P, SEQ]) for p in range(2)]
            acc = [sb(z, f"acc{p}", [P, SEQ]) for p in range(2)]
            ytile = [sb(z, f"ytile{p}", [P, 2 * P]) for p in range(2)]
        ctx.enter_context(nc.sbuf_tensor("scratch", [P, 5, SEQ], F32))

        with ExitStack() as mix:
            ya_hi, ya_lo = (sb(mix, f"ya_{n}", [P, 2, SEQ], F32R) for n in ("hi", "lo"))
            yb_hi, yb_lo = (sb(mix, f"yb_{n}", [P, 4, SEQ], F32R) for n in ("hi", "lo"))
            yc_hi, yc_lo = (sb(mix, f"yc_{n}", [P, 4, SEQ], F32R) for n in ("hi", "lo"))
            with ExitStack() as z:
                aq = sb(z, "aq", [P, 6, SEQ])
                ak = sb(z, "ak", [P, 6, SEQ])
                av = sb(z, "av", [P, GROUPS, NT, SLOTS * HD])
                logits = [sb(z, f"logits{p}", [P, 6 * P]) for p in range(2)]
                probs_t = [sb(z, f"probs_t{p}", [P, 6 * P]) for p in range(2)]
            with ExitStack() as z:
                bv = sb(z, "bv", [P, NT, 4 * P])
                bq = sb(z, "bq", [P, 4, SEQ])
                bk = sb(z, "bk", [P, 4, SEQ])
                zs = [sb(z, f"zs{p}", [P, SEQ]) for p in range(3)]
                ez = [sb(z, f"ez{p}", [P, SEQ]) for p in range(2)]
                sp_keep = [sb(z, f"sp_keep{p}", [P, SEQ]) for p in range(2)]
                wts = sb(z, "wts", [P, 10 * P])
            with ExitStack() as z:
                cvv = sb(z, "cvv", [P, NT, 4 * P])
                cq = sb(z, "cq", [P, 4, SEQ])
                cg = sb(z, "cg", [P, 4, SEQ])
                dcy = [sb(z, f"dcy{p}", [P, 10 * P]) for p in range(2)]
                ret = [sb(z, f"ret{p}", [P, SEQ]) for p in range(2)]
                cen = [sb(z, f"cen{p}", [P, SEQ]) for p in range(2)]
                csq = sb(z, "csq", [P, SEQ])
                cy = sb(z, "cy", [P, SEQ])
                ct = sb(z, "ct", [P, SEQ])
            with ExitStack() as z:
                m_hi, m_lo = (sb(z, f"m_{n}", [P, KD, SEQ], F32R) for n in ("hi", "lo"))
                sg = [sb(z, f"sg{p}", [P, SEQ]) for p in range(3)]
                mt = [sb(z, f"mt{p}", [P, SEQ]) for p in range(2)]
        with ExitStack() as ffn:
            act_hi, act_lo = (sb(ffn, f"act_{n}", [P, KF, SEQ], F32R) for n in ("hi", "lo"))
        with ExitStack() as z:
            rel_ext = sb(z, "rel_ext", [REL_BUCKETS + 1, 12])
            one_hot = sb(z, "one_hot", [REL_BUCKETS + 1, LINE])
            lines = sb(z, "lines", [12, LINE])
            flip = sb(z, "flip", [P, P])
            table_rev = sb(z, "table_rev", [P, SLOTS, TABLE])
        ctx.enter_context(nc.sbuf_tensor("layer_area", [P, 2 * KF * SEQ], F32))

        ps = ctx.enter_context(nc.psum_tensor("ps", [P, 8, SEQ], F32))

        sem = {name: ctx.enter_context(nc.semaphore(name)) for name in COUNTS}
        raw_in = [sem["raw_in0"], sem["raw_in1"]]
        const_in = ctx.enter_context(nc.semaphore("const_in"))
        x_in = ctx.enter_context(nc.semaphore("x_in"))
        memset_done = ctx.enter_context(nc.semaphore("memset_done"))
        line_mm = ctx.enter_context(nc.semaphore("line_mm"))
        line_copied = ctx.enter_context(nc.semaphore("line_copied"))
        line_out = ctx.enter_context(nc.semaphore("line_out"))
        table_in = ctx.enter_context(nc.semaphore("table_in"))
        table_mm = ctx.enter_context(nc.semaphore("table_mm"))
        table_ready = ctx.enter_context(nc.semaphore("table_ready"))
        out_ready = ctx.enter_context(nc.semaphore("out_ready"))
        out_done = ctx.enter_context(nc.semaphore("out_done"))
        block = ctx.enter_context(nc.Block())

        def nth(name, L, k):
            per_layer, before = COUNTS[name]
            return L * per_layer + (k + before)

        def grant(eng, *names):
            for name in names:
                eng.sem_inc(sem[name], GRANTED[name])

        def bank(b, a=0, z=SEQ):
            return ps[:, b, a:z]

        class Steps:

            def __init__(self, name):
                self.name, self.k, self.turn = name, 0, 0

            def next(self, L):
                self.k += 1
                return nth(self.name, L, self.turn + self.k)

            def enter(self, i, per_turn):
                self.turn, self.first, self.per_turn = i * per_turn, self.k, per_turn

            def leave(self, turns):
                assert self.k - self.first == self.per_turn, (self.name, self.k - self.first)
                self.k, self.turn = self.first + turns * self.per_turn, 0

            def end(self):
                assert self.k == COUNTS[self.name][0], (self.name, self.k)

        def elements(s):
            if S_M <= s < S_O:
                return (K_PROJ if (s - S_M) % 4 == 3 else KD) * P
            return KHALF * P if s >= S_D else KD * P

        @block.sync
        def _(sp):
            for dst, src in ((vecs[:], vectors), (consts[:], mats[:, 0:7, :]), (flip[:], mats[:, 7, :]),
                             (rel_ext[0:REL_BUCKETS, :], rel_bias), (one_hot[:], onehot),
                             (decays[:], decay), (rope[:], cos_sin)):
                sp.dma_start(dst, src).then_inc(const_in, 16)
            sp.dma_start(x[:], x_t).then_inc(x_in, 16)
            sp.wait_ge(line_copied, 3)
            sp.dma_start(line_dram, lines[:]).then_inc(line_out, 16)
            sp.wait_ge(line_out, 16)
            for h in range(SLOTS):
                for g, at, step, n in ((0, 0, 4, EXT), (1, LINE1, 1, P), (2, LINE1 + LINE2, 1, P)):
                    to = 0 if g == 0 else EXT + (g - 1) * P
                    src = bass.AP(tensor=line_dram.tensor, offset=(SLOTS * g + h) * LINE + at,
                                  ap=[[step, P], [1, n]])
                    sp.dma_start(table_rev[:, h, to:to + n], src).then_inc(table_in, 16)

            def load(L, s, p, src, n):
                sp.wait_ge(sem["split_done"], nth("split_done", L, s - 1))
                sp.dma_start(raw[p][:, 0:n], src).then_inc(raw_in[p], 16)

            with sp.Fori(0, DEPTH) as L:
                with sp.Fori(0, S_M // 2) as i:
                    for p in range(2):
                        load(L, 2 * i + p, p, w_qkv[L * S_M + 2 * i + p], KD * P)
                with sp.Fori(0, KD) as j:
                    for b in range(3):
                        load(L, 4 * j + (S_M + b), b % 2, w_gates[L * (3 * KD) + 3 * j + b], KD * P)
                    load(L, 4 * j + (S_M + 3), 1, w_proj[L * KD + j], K_PROJ * P)
                for first, src, n, per in ((S_O, w_o, KD // 2, KD * P), (S_F, w_upgate, KF, KD * P),
                                           (S_D, w_down, KD, KHALF * P)):
                    with sp.Fori(0, n) as i:
                        for p in range(2):
                            load(L, 2 * i + (first + p), p, src[L * (2 * n) + 2 * i + p], per)

            for k in range(KD):
                sp.wait_ge(out_ready, k + 1)
                sp.dma_start(out_t[:, k, :], x[:, k, :]).then_inc(out_done, 16)
            sp.wait_ge(out_done, 16 * KD)

        @block.tensor
        def _(pe):
            grant(pe, "slab_used")

            def slab(L, s, p, products):
                pe.wait_ge(sem["split_done"], nth("split_done", L, s + 1))
                at = 0
                for b, blocks, first, hi, lo, starts, ends in products:
                    for k in range(blocks):
                        w = slice((at + k) * P, (at + k + 1) * P)
                        for n, (a, y) in enumerate(((w_hi[p], hi), (w_hi[p], lo), (w_lo[p], hi))):
                            mm = pe.matmul(bank(b), a[:, w], y[:, first + k, :],
                                           start=starts and k == 0 and n == 0,
                                           stop=ends and k == blocks - 1 and n == 2)
                    at += blocks
                mm.then_inc(sem["slab_used"], 1)

            def from_h(b):
                return [(b, KD, 0, h_hi, h_lo, True, True)]

            def mean_square(L, n):
                pe.wait_ge(sem["sum_added"], nth("sum_added", L, KD * (n - 1)))
                pe.matmul(bank(6), ones_model, sumsq[:], start=True, stop=True)\
                  .then_inc(sem["ms_ready"], 1)

            def section(L, first, chunks, v_chunks, v_before):
                straight = v_chunks + 2
                for c in range(straight):
                    s = first + c
                    if s >= 2:
                        pe.wait_ge(sem["chunk_out"], nth("chunk_out", L, s - 1))
                    slab(L, s, s % 2, from_h(s % 2))
                    if 1 <= c <= v_chunks:
                        v = v_before + c - 1
                        pe.wait_ge(sem["chunk_out"], nth("chunk_out", L, s))
                        if v >= 2:
                            pe.wait_ge(sem["v_ready"], nth("v_ready", L, v - 1))
                        for t in range(NT):
                            mm = pe.transpose(bank(2 + v % 2, t * P, (t + 1) * P),
                                              vs[v % 2][:, t * P:(t + 1) * P], ident)
                        mm.then_inc(sem["vt_ready"], 1)
                with pe.Fori(0, (chunks - straight) // 2) as i:
                    for p in range(2):
                        s = 2 * i + (first + straight + p)
                        pe.wait_ge(sem["chunk_out"], nth("chunk_out", L, s - 1))
                        slab(L, s, p, from_h(p))
                pe.wait_ge(sem["chunk_out"], nth("chunk_out", L, first + chunks))
                pe.wait_ge(sem["v_ready"], nth("v_ready", L, v_before + v_chunks))

            def windows(L):
                def scores(i):
                    r, h = divmod(i, SLOTS)
                    if i >= 2:
                        pe.wait_ge(sem["l_ready"], nth("l_ready", L, i - 1))
                    rows = slice(HD * (h % 2), HD * (h % 2) + HD)
                    for g in range(GROUPS):
                        q = aq[rows, 2 * g + h // 2, r * P:(r + 1) * P]
                        k = ak[rows, 2 * g + h // 2, :]
                        if g == 0:
                            mm = pe.matmul(bank(2 + 2 * (i % 2)), q, k, start=True, stop=True)
                        else:
                            mm = pe.matmul(bank(3 + 2 * (i % 2), (g - 1) * P, g * P), q,
                                           k[:, r * P:(r + 1) * P], start=True, stop=True)
                    mm.then_inc(sem["s_ready"], 1)

                def turned_y(r):
                    pe.wait_ge(sem["o_used"], nth("o_used", L, SLOTS * (r + 1)))
                    pe.wait_ge(sem["pt_ready"], nth("pt_ready", L, min(SLOTS * (r + 1) + 1, 16)))
                    for c in range(2):
                        mm = pe.transpose(bank(6, c * P, (c + 1) * P), ytile[r % 2][:, c * P:(c + 1) * P],
                                          ident)
                    mm.then_inc(sem["yt_ready"], 1)

                scores(0)
                scores(1)
                for i in range(16):
                    r, h = divmod(i, SLOTS)
                    pe.wait_ge(sem["p_ready"], nth("p_ready", L, i + 1))
                    if i >= 1:
                        pe.wait_ge(sem["pt_ready"], nth("pt_ready", L, i))
                    if i >= 5 and h == 1:
                        pe.wait_ge(sem["ya_ready"], nth("ya_ready", L, r))
                    for kb in range(6):
                        mm = pe.transpose(bank(6 + kb // 4, kb % 4 * P, (kb % 4 + 1) * P),
                                          logits[i % 2][:, kb * P:(kb + 1) * P], ident)
                    mm.then_inc(sem["t_ready"], 1)
                    if i + 2 < 16:
                        scores(i + 2)
                    pe.wait_ge(sem["pt_ready"], nth("pt_ready", L, i + 1))
                    if i >= 2:
                        pe.wait_ge(sem["o_used"], nth("o_used", L, i - 1))
                    for kb in range(6):
                        g, t = (0, kb) if kb < 4 else (kb - 3, r)
                        mm = pe.matmul(bank(i % 2, 0, HD), probs_t[i % 2][:, kb * P:(kb + 1) * P],
                                       av[:, g, t, h * HD:(h + 1) * HD], start=kb == 0, stop=kb == 5)
                    mm.then_inc(sem["o_ready"], 1)
                    if h == 0 and r >= 1:
                        turned_y(r - 1)
                turned_y(3)
                pe.wait_ge(sem["ya_ready"], nth("ya_ready", L, 4))

            def stick_breaking(L):
                turns = [(h, n) for h in range(4) for n in (3, 2, 1, 0)]

                def scores(t):
                    h, n = turns[t]
                    if t >= 2:
                        pe.wait_ge(sem["zs_ready"], nth("zs_ready", L, t - 1))
                    pe.matmul(bank(2 + t % 2, n * P), bk[:, h, n * P:(n + 1) * P], bq[:, h, n * P:],
                              start=True, stop=True).then_inc(sem["z_ready"], 1)

                def output(h):
                    pe.wait_ge(sem["w_ready"], nth("w_ready", L, 4 * h + 4))
                    if h >= 2:
                        pe.wait_ge(sem["yb_ready"], nth("yb_ready", L, h - 1))
                    for n in range(4):
                        at = (4 - n) * (3 - n) // 2 * P
                        mm = pe.matmul(bank(6 + h % 2, n * P), bv[:, n, h * P:(h + 1) * P],
                                       wts[:, at:at + (4 - n) * P], start=n == 0, stop=True,
                                       skip_group_check=True)
                    mm.then_inc(sem["yb_mm"], 1)

                scores(0)
                scores(1)
                for t, (h, n) in enumerate(turns):
                    pe.wait_ge(sem["sp_ready"], nth("sp_ready", L, t + 1))
                    if t >= 2:
                        pe.wait_ge(sem["lw_ready"], nth("lw_ready", L, t - 1))
                    mm = pe.matmul(bank(4 + t % 2, n * P), tri, sp_keep[t % 2][:, n * P:],
                                   start=True, stop=True)
                    if n < 3:
                        mm = pe.matmul(bank(4 + t % 2, (n + 1) * P), ones,
                                       acc[(n + 1) % 2][:, (n + 1) * P:], start=False, stop=True,
                                       skip_group_check=True)
                    mm.then_inc(sem["sfx_ready"], 1)
                    if t + 2 < 16:
                        scores(t + 2)
                    if n == 3 and h >= 1:
                        output(h - 1)
                output(3)
                pe.wait_ge(sem["yb_ready"], nth("yb_ready", L, 4))

            def retention(L):
                for c in range(4):
                    if c >= 2:
                        pe.wait_ge(sem["rot_ready"], nth("rot_ready", L, c - 1))
                    pe.matmul(bank(4 + c % 2), rotate, cq[:, c, :], start=True, stop=True)\
                      .then_inc(sem["rx_ready"], 1)
                pe.wait_ge(sem["rot_ready"], nth("rot_ready", L, 4))

                def scores(h):
                    rows = slice(HD * (h % 2), HD * (h % 2) + HD)
                    for n in range(4):
                        if h >= 1:
                            pe.wait_ge(sem["decay_ready"], nth("decay_ready", L, 4 * (h - 1) + n + 1))
                        pe.matmul(bank(2 + n, n * P), cq[rows, 2 + h // 2, n * P:(n + 1) * P],
                                  cq[rows, h // 2, n * P:], start=True, stop=True)\
                          .then_inc(sem["st_ready"], 1)

                def mix(h):
                    pe.wait_ge(sem["decay_ready"], nth("decay_ready", L, 4 * h + 4))
                    if h >= 1:
                        pe.wait_ge(sem["ret_copied"], nth("ret_copied", L, h))
                    for n in range(4):
                        at = (4 - n) * (3 - n) // 2 * P
                        mm = pe.matmul(bank(6, n * P), cvv[:, n, h * P:(h + 1) * P],
                                       dcy[h % 2][:, at:at + (4 - n) * P], start=n == 0, stop=True,
                                       skip_group_check=True)
                    mm.then_inc(sem["ret_ready"], 1)

                def mean(h):
                    pe.wait_ge(sem["ret_copied"], nth("ret_copied", L, h + 1))
                    if h >= 1:
                        pe.wait_ge(sem["cen_ready"], nth("cen_ready", L, h))
                    pe.matmul(bank(7), ones_head, ret[h % 2][:], start=True, stop=True)\
                      .then_inc(sem["mu_ready"], 1)

                def variance(h):
                    pe.wait_ge(sem["csq_ready"], nth("csq_ready", L, h + 1))
                    if h >= 1:
                        pe.wait_ge(sem["yc_ready"], nth("yc_ready", L, h))
                    pe.matmul(bank(1), ones_head, csq[:], start=True, stop=True)\
                      .then_inc(sem["var_ready"], 1)

                scores(0)
                for h in range(4):
                    mix(h)
                    if h < 3:
                        scores(h + 1)
                    mean(h)
                    if h >= 1:
                        variance(h - 1)
                variance(3)
            pe.wait_ge(const_in, 16 * 7)
            pe.wait_ge(memset_done, 2)
            for n in range(3):
                pe.matmul(ps[0:12, n, :], rel_ext[:, :], one_hot[:, n * SEQ:(n + 1) * SEQ],
                          start=True, stop=True).then_inc(line_mm, 1)
            pe.wait_ge(table_in, 16 * 12)
            for h in range(SLOTS):
                if h >= 2:
                    pe.wait_ge(table_ready, 2 * (h - 1))
                for half in range(2):
                    a, z = (0, SEQ) if half == 0 else (SEQ, TABLE)
                    pe.matmul(bank(3 + 2 * (h % 2) + half, 0, z - a), flip[:], table_rev[:, h, a:z],
                              start=True, stop=True).then_inc(table_mm, 1)
            pe.wait_ge(table_ready, 2 * SLOTS)

            with pe.Fori(0, DEPTH) as L:
                mean_square(L, 1)
                pe.wait_ge(sem["h_ready"], nth("h_ready", L, KD))
                section(L, 0, A_CHUNKS, 6, 0)
                windows(L)
                section(L, A_CHUNKS, B_CHUNKS, 4, 6)
                stick_breaking(L)
                section(L, A_CHUNKS + B_CHUNKS, C_CHUNKS, 4, 10)
                retention(L)
                with pe.Fori(0, KD) as j:
                    for b in range(3):
                        pe.wait_ge(sem["gate_ready"], nth("gate_ready", L, 3 * j + (b - 2)))
                        slab(L, 4 * j + (S_M + b), b % 2, from_h(GATE_BANKS[b]))
                    pe.wait_ge(sem["yc_split"], nth("yc_split", L, 4))
                    pe.wait_ge(sem["m_ready"], nth("m_ready", L, j))
                    slab(L, 4 * j + (S_M + 3), 1,
                         [(1, 2, 0, ya_hi, ya_lo, True, True), (4, 4, 0, yb_hi, yb_lo, True, True),
                          (5, 4, 0, yc_hi, yc_lo, True, True)])
                with pe.Fori(0, KD // 2) as i:
                    for p in range(2):
                        pe.wait_ge(sem["m_split"], nth("m_split", L, KD))
                        pe.wait_ge(sem["x_new"], nth("x_new", L, 2 * i + (p - 1)))
                        slab(L, 2 * i + (S_O + p), p, [(p, KD, 0, m_hi, m_lo, True, True)])
                mean_square(L, 2)
                with pe.Fori(0, KF) as c:
                    pe.wait_ge(sem["h_ready"], nth("h_ready", L, 2 * KD))
                    pe.wait_ge(sem["conv_done"], nth("conv_done", L, c))
                    slab(L, 2 * c + S_F, 0, from_h(0))
                    pe.wait_ge(sem["af_ready"], nth("af_ready", L, c))
                    slab(L, 2 * c + (S_F + 1), 1, from_h(1))
                with pe.Fori(0, KD // 2) as i:
                    for b in range(2):
                        for p in range(2):
                            pe.wait_ge(sem["af_split"], nth("af_split", L, (p + 1) * KHALF))
                            if p == 0:
                                pe.wait_ge(sem["conv_done"], nth("conv_done", L, KF))
                                pe.wait_ge(sem["x_new"], nth("x_new", L, 2 * i + (KD + b - 1)))
                            slab(L, 4 * i + (S_D + 2 * b + p), p,
                                 [(b, KHALF, p * KHALF, act_hi, act_lo, p == 0, p == 1)])
            mean_square(DEPTH, 1)

        @block.scalar
        def _(act):
            grant(act, "gate_ready")

            def high(L, s, p, turn, n):
                act.wait_ge(sem[f"raw_in{p}"], nth(f"raw_in{p}", L, 16 * turn))
                act.wait_ge(sem["slab_used"], nth("slab_used", L, s - 1))
                act.activation(w_hi[p][:, 0:n], raw[p][:, 0:n], ACT.Copy).then_inc(sem["hi_ready"], 1)

            def high_at(L, s):
                high(L, s, s % 2, s // 2 + 1, elements(s))

            def norm(L, n, steps):
                act.wait_ge(sem["ms_ready"], nth("ms_ready", L, n))
                act.activation(y0[:], bank(6), ACT.Ln, bias=eps[:]).then_inc(sem["act_step"], 1)
                act.wait_ge(sem["act_step"], steps.next(L))
                act.activation(y0[:], y0[:], ACT.Exp, scale=-0.5).then_inc(sem["y0_ready"], 1)

            def norm_high(L, n):
                for k in range(KD):
                    act.wait_ge(sem["hf_ready"], nth("hf_ready", L, KD * (n - 1) + k + 1))
                    act.activation(h_hi[:, k, :], hf[k % 2][:], ACT.Copy).then_inc(sem["h_hi_ready"], 1)

            def by_class(t):
                return t.rearrange("p (u r) -> p r u", r=4)

            def section(L, first, places):
                for c, (dst, permuted, scale, func, v) in enumerate(places):
                    s = first + c
                    high_at(L, s + 2)
                    act.wait_ge(sem["slab_used"], nth("slab_used", L, s + 1))
                    if v is not None and v >= 2:
                        act.wait_ge(sem["vt_ready"], nth("vt_ready", L, v - 1))
                    src = bank(s % 2)
                    if permuted:
                        dst, src = dst.rearrange("p (r u) -> p r u", r=4), by_class(src)
                    act.activation(dst, src, func, scale=scale).then_inc(sem["chunk_out"], 1)

            def turned(v0, n):
                return [(vs[v % 2][:], v0 == 0 and v >= 2, 1.0, ACT.Copy, v) for v in range(v0, v0 + n)]

            def windows(L):
                def probs(i):
                    act.wait_ge(sem["l_ready"], nth("l_ready", L, i + 1))
                    act.activation(logits[i % 2][:], logits[i % 2][:], ACT.Exp,
                                   bias=stat[:, 1, i % 4:i % 4 + 1],
                                   accum_out=stat[:, 2, i % 4:i % 4 + 1]).then_inc(sem["p_ready"], 1)

                def y_high(r):
                    act.wait_ge(sem["yt_ready"], nth("yt_ready", L, r + 1))
                    act.activation(ya_hi[:, :, r::4], ps[:, 6, 0:2 * P].rearrange("p (c u) -> p c u", c=2),
                                   ACT.Copy).then_inc(sem["ya_hi_ready"], 1)

                probs(0)
                for i in range(16):
                    if i + 1 < 16:
                        probs(i + 1)
                    act.wait_ge(sem["t_ready"], nth("t_ready", L, i + 1))
                    if i >= 2:
                        act.wait_ge(sem["o_ready"], nth("o_ready", L, i - 1))
                    act.activation(probs_t[i % 2][:, :], ps[:, 6:8, :].rearrange("p b n -> p (b n)")[:, 0:6 * P],
                                   ACT.Copy).then_inc(sem["pt_ready"], 1)
                    if i % SLOTS == 0 and i:
                        y_high(i // SLOTS - 1)
                y_high(3)

            def stick_breaking(L, steps):
                turns = [(h, n) for h in range(4) for n in (3, 2, 1, 0)]

                def log_part(t):
                    n = turns[t][1]
                    e, z = ez[t % 2][:, n * P:], zs[t % 3][:, n * P:]
                    act.wait_ge(sem["zs_ready"], nth("zs_ready", L, t + 1))
                    act.activation(e, z, ACT.Abs).then_inc(sem["act_step"], 1)
                    act.wait_ge(sem["act_step"], steps.next(L))
                    act.activation(e, e, ACT.Exp, scale=-1.0).then_inc(sem["act_step"], 1)
                    act.wait_ge(sem["act_step"], steps.next(L))
                    act.activation(e, e, ACT.Ln, bias=1.0).then_inc(sem["e_ready"], 1)

                def weights(t):
                    h, n = turns[t]
                    at = (4 - n) * (3 - n) // 2 * P
                    act.wait_ge(sem["lw_ready"], nth("lw_ready", L, t + 1))
                    if n == 3 and h >= 1:
                        act.wait_ge(sem["yb_mm"], nth("yb_mm", L, h))
                    act.activation(wts[:, at:at + (4 - n) * P], zs[t % 3][:, n * P:], ACT.Exp)\
                       .then_inc(sem["w_ready"], 1)

                def y_high(h):
                    act.wait_ge(sem["yb_mm"], nth("yb_mm", L, h + 1))
                    act.activation(yb_hi[:, h, :], bank(6 + h % 2), ACT.Copy)\
                       .then_inc(sem["yb_hi_ready"], 1)

                for t in range(16):
                    log_part(t)
                    if t >= 1:
                        weights(t - 1)
                    if t % 4 == 1 and t > 4:
                        y_high(t // 4 - 1)
                weights(15)
                y_high(3)

            def retention(L, steps):
                def start_root(h):
                    act.wait_ge(sem["var_ready"], nth("var_ready", L, h + 1))
                    if h >= 1:
                        act.wait_ge(sem["yc_ready"], nth("yc_ready", L, h))
                    act.activation(cy[:], bank(1), ACT.Ln, bias=eps[:]).then_inc(sem["act_step"], 1)
                    act.wait_ge(sem["act_step"], steps.next(L))
                    act.activation(cy[:], cy[:], ACT.Exp, scale=-0.5).then_inc(sem["cy0_ready"], 1)

                def y_high(h):
                    act.wait_ge(sem["yc_ready"], nth("yc_ready", L, h + 1))
                    act.activation(yc_hi[:, h, :], ct[:], ACT.Copy).then_inc(sem["yc_hi_ready"], 1)

                for h in range(4):
                    act.wait_ge(sem["ret_ready"], nth("ret_ready", L, h + 1))
                    if h >= 2:
                        act.wait_ge(sem["cen_ready"], nth("cen_ready", L, h - 1))
                    act.activation(ret[h % 2][:], bank(6), ACT.Copy).then_inc(sem["ret_copied"], 1)
                    if h >= 1:
                        start_root(h - 1)
                    act.wait_ge(sem["cen_ready"], nth("cen_ready", L, h + 1))
                    act.activation(csq[:], cen[h % 2][:], ACT.Square).then_inc(sem["csq_ready"], 1)
                    if h >= 1:
                        y_high(h - 1)
                start_root(3)
                y_high(3)

            def square_of(L, j, p, n):
                act.wait_ge(sem["x_new"], nth("x_new", L, n))
                act.activation(square[p][:], x[:, j, :], ACT.Square).then_inc(sem["sq_ready"], 1)

            act.preload_act_table_set(NLE)
            act.wait_ge(x_in, 16)
            for k in range(KD):
                if k >= 2:
                    act.wait_ge(sem["sum_added"], k - 1)
                act.activation(square[k % 2][:], x[:, k, :], ACT.Square).then_inc(sem["sq_ready"], 1)
            act.wait_ge(memset_done, 2)
            act.wait_ge(const_in, 16 * 7)

            with act.Fori(0, DEPTH) as L:
                steps = Steps("act_step")
                act.preload_act_table_set(NLE)
                high_at(L, 0)
                high_at(L, 1)
                norm(L, 1, steps)
                norm_high(L, 1)
                section(L, 0, turned(0, 6)
                        + [(aq[:, c, :], True, HD ** -0.5, ACT.Copy, None) for c in range(6)]
                        + [(ak[:, c, :], c >= 2, 1.0, ACT.Copy, None) for c in range(6)])
                windows(L)
                section(L, A_CHUNKS, turned(6, 4)
                        + [(bq[:, c, :], False, 1.0, ACT.Copy, None) for c in range(4)]
                        + [(bk[:, c, :], False, 1.0, ACT.Copy, None) for c in range(4)])
                stick_breaking(L, steps)
                section(L, A_CHUNKS + B_CHUNKS, turned(10, 4)
                        + [(cq[:, c, :], False, 1.0 if c < 2 else HD ** -0.5, ACT.Copy, None)
                           for c in range(4)]
                        + [(cg[:, c, :], False, 1.0, ACT.Silu, None) for c in range(4)])
                act.preload_act_table_set(NLE)
                retention(L, steps)
                with act.Fori(0, KD) as j:
                    for b in range(4):
                        s = 4 * j + (S_M + b)
                        high(L, s + 2, b % 2, 2 * j + (S_M // 2 + b // 2 + 2),
                             (K_PROJ if b == 1 else KD) * P)
                        if b < 3:
                            act.wait_ge(sem["slab_used"], nth("slab_used", L, s + 1))
                            act.wait_ge(sem["m_ready"], nth("m_ready", L, j))
                            act.activation(sg[b][:], bank(GATE_BANKS[b]), ACT.Sigmoid,
                                           bias=vecs[:, bass.ds(V_BGATE + L * (3 * KD) + 3 * j + b, 1)])\
                               .then_inc(sem["gate_ready"], 1)
                    act.wait_ge(sem["m_ready"], nth("m_ready", L, j + 1))
                    act.activation(m_hi[:, j, :], mt[0][:], ACT.Copy).then_inc(sem["m_hi_ready"], 1)
                act.preload_act_table_set(NLE)
                with act.Fori(0, KD // 2) as i:
                    for p in range(2):
                        high(L, 2 * i + (S_O + p + 2), p, i + (S_O // 2 + 2), KD * P)
                        square_of(L, 2 * i + p, p, 2 * i + (p + 1))
                norm(L, 2, steps)
                norm_high(L, 2)

                def ffn_block(c, n, turn):
                    high(L, 2 * c + (S_F + 2), 0, turn, n)
                    act.wait_ge(sem["slab_used"], nth("slab_used", L, 2 * c + (S_F + 1)))
                    act.wait_ge(sem["af_ready"], nth("af_ready", L, c))
                    at = V_CONV + L * (4 * KF) + 4 * c
                    act.activation(cv[:], bank(0), ACT.Identity, bias=vecs[:, bass.ds(at + 3, 1)],
                                   scale=vecs[:, bass.ds(at + 2, 1)]).then_inc(sem["cv_ready"], 1)
                    act.wait_ge(sem["conv_done"], nth("conv_done", L, c + 1))
                    act.activation(cv[:], cv[:], ACT.Gelu_apprx_tanh).then_inc(sem["gelu_ready"], 1)
                    high(L, 2 * c + (S_F + 3), 1, turn, n)
                    act.wait_ge(sem["af_ready"], nth("af_ready", L, c + 1))
                    act.activation(act_hi[:, c, :], af[:], ACT.Copy).then_inc(sem["af_hi_ready"], 1)

                act.preload_act_table(ACT.Gelu_apprx_tanh)
                with act.Fori(0, KF - 1) as c:
                    ffn_block(c, KD * P, c + (S_F // 2 + 2))
                ffn_block(KF - 1, KHALF * P, KF - 1 + S_F // 2 + 2)

                def down_pair(i, last):
                    for b in range(2):
                        for p in range(2):
                            if not (last and b == 1):
                                high(L, 4 * i + (S_D + 2 * b + p + 2), p, 2 * i + (S_D // 2 + b + 2),
                                     KHALF * P)
                        square_of(L, 2 * i + b, b, 2 * i + (KD + b + 1))

                with act.Fori(0, KD // 2 - 1) as i:
                    down_pair(i, False)
                down_pair(KD // 2 - 1, True)
                steps.end()
            act.preload_act_table_set(NLE)
            steps = Steps("act_step")
            norm(DEPTH, 1, steps)

        @block.vector
        def _(dve):
            grant(dve, "split_done", "x_new", "m_ready", "conv_done", "af_ready", "m_split", "af_split")

            def low(L, s, p, n):
                dve.wait_ge(sem["hi_ready"], nth("hi_ready", L, s + 1))
                dve.tensor_tensor(w_lo[p][:, 0:n], raw[p][:, 0:n], w_hi[p][:, 0:n].bitcast(F32),
                                  ALU.subtract).then_inc(sem["split_done"], 1)

            def low_at(L, s):
                low(L, s, s % 2, elements(s))

            def root(L, n, steps):
                dve.wait_ge(sem["y0_ready"], nth("y0_ready", L, n))
                dve.tensor_tensor(rs[:], y0[:], y0[:], ALU.mult).then_inc(sem["dve_step"], 1)
                dve.wait_ge(sem["dve_step"], steps.next(L))
                dve.scalar_tensor_tensor(rs[:], bank(6), EPS, rs[:], ALU.add, ALU.mult)\
                   .then_inc(sem["dve_step"], 1)
                dve.wait_ge(sem["dve_step"], steps.next(L))
                dve.tensor_scalar(rs[:], rs[:], -0.5, 1.5, ALU.mult, ALU.add)\
                   .then_inc(sem["dve_step"], 1)
                dve.wait_ge(sem["dve_step"], steps.next(L))
                dve.tensor_tensor(rs[:], rs[:], y0[:], ALU.mult).then_inc(sem["dve_step"], 1)
                dve.wait_ge(sem["dve_step"], steps.next(L))

            def norm(L, n, steps):
                root(L, n, steps)

                def scaled(k):
                    if k >= 2:
                        dve.wait_ge(sem["h_ready"], nth("h_ready", L, KD * (n - 1) + k - 1))
                    dve.scalar_tensor_tensor(hf[k % 2][:], x[:, k, :],
                                             vecs[:, bass.ds(V_NORM + L * (2 * KD) + ((n - 1) * KD + k), 1)],
                                             rs[:], ALU.mult, ALU.mult).then_inc(sem["hf_ready"], 1)

                scaled(0)
                for k in range(KD):
                    if k + 1 < KD:
                        scaled(k + 1)
                    dve.wait_ge(sem["h_hi_ready"], nth("h_hi_ready", L, KD * (n - 1) + k + 1))
                    dve.tensor_tensor(h_lo[:, k, :], hf[k % 2][:], h_hi[:, k, :].bitcast(F32),
                                      ALU.subtract).then_inc(sem["h_ready"], 1)

            def section(L, first, chunks, v_chunks, v_before, store):
                for c in range(chunks):
                    s = first + c
                    low_at(L, s + 2)
                    if 1 <= c <= v_chunks:
                        v = v_before + c - 1
                        dve.wait_ge(sem["vt_ready"], nth("vt_ready", L, v + 1))
                        dve.tensor_copy(store(c - 1), bank(2 + v % 2).rearrange("p (t n) -> p t n", t=NT))\
                           .then_inc(sem["v_ready"], 1)

            def windows(L, steps):
                def logit(i):
                    r, h = divmod(i, SLOTS)
                    dve.wait_ge(sem["s_ready"], nth("s_ready", L, i + 1))
                    b, to = 2 + 2 * (i % 2), logits[i % 2]
                    dve.tensor_tensor(to[:, 0:SEQ], bank(b), table[:, h, 3 - r:3 - r + SEQ], ALU.add)\
                       .then_inc(sem["dve_step"], 1)
                    dve.wait_ge(sem["dve_step"], steps.next(L))
                    dve.tensor_tensor(to[:, SEQ:6 * P], bank(b + 1, 0, 2 * P), table[:, h, EXT:TABLE],
                                      ALU.add).then_inc(sem["dve_step"], 1)
                    dve.wait_ge(sem["dve_step"], steps.next(L))
                    a = i % 4
                    dve.reduce_max(stat[:, 0, a:a + 1], to[:], AX_X).then_inc(sem["dve_step"], 1)
                    dve.wait_ge(sem["dve_step"], steps.next(L))
                    dve.tensor_scalar(stat[:, 1, a:a + 1], stat[:, 0, a:a + 1], -1.0, None, ALU.mult)\
                       .then_inc(sem["l_ready"], 1)

                def divide(i):
                    r, h = divmod(i, SLOTS)
                    a = i % 4
                    dve.wait_ge(sem["p_ready"], nth("p_ready", L, i + 1))
                    dve.reciprocal(stat[:, 3, a:a + 1], stat[:, 2, a:a + 1])\
                       .then_inc(sem["dve_step"], 1)
                    dve.wait_ge(sem["dve_step"], steps.next(L))
                    dve.wait_ge(sem["o_ready"], nth("o_ready", L, i + 1))
                    if h == 0 and r >= 2:
                        dve.wait_ge(sem["yt_ready"], nth("yt_ready", L, r - 1))
                    dve.tensor_scalar(ytile[r % 2][:, h * HD:(h + 1) * HD], bank(i % 2, 0, HD),
                                      stat[:, 3, a:a + 1], None, ALU.mult).then_inc(sem["o_used"], 1)

                def y_low(r):
                    dve.wait_ge(sem["ya_hi_ready"], nth("ya_hi_ready", L, r + 1))
                    dve.tensor_tensor(ya_lo[:, :, r::4], ps[:, 6, 0:2 * P].rearrange("p (c u) -> p c u", c=2),
                                      ya_hi[:, :, r::4].bitcast(F32), ALU.subtract)\
                       .then_inc(sem["ya_ready"], 1)

                logit(0)
                logit(1)
                for i in range(16):
                    if i + 2 < 16:
                        logit(i + 2)
                    divide(i)
                    if i % SLOTS == 0 and i:
                        y_low(i // SLOTS - 1)
                y_low(3)

            def stick_breaking(L, steps):
                turns = [(h, n) for h in range(4) for n in (3, 2, 1, 0)]

                def scaled(t):
                    n = turns[t][1]
                    dve.wait_ge(sem["z_ready"], nth("z_ready", L, t + 1))
                    if t >= 3:
                        dve.wait_ge(sem["w_ready"], nth("w_ready", L, t - 2))
                    z, b = zs[t % 3], 2 + t % 2
                    if n < 3:
                        dve.tensor_scalar(z[:, (n + 1) * P:], bank(b, (n + 1) * P), SB_SCALE, None, ALU.mult)
                    dve.scalar_tensor_tensor(z[:, n * P:(n + 1) * P], bank(b, n * P, (n + 1) * P), SB_SCALE,
                                             neg_mask, ALU.mult, ALU.add).then_inc(sem["zs_ready"], 1)

                def softplus(t):
                    n = turns[t][1]
                    dve.wait_ge(sem["e_ready"], nth("e_ready", L, t + 1))
                    dve.scalar_tensor_tensor(sp_keep[t % 2][:, n * P:], zs[t % 3][:, n * P:], 0.0,
                                             ez[t % 2][:, n * P:], ALU.max, ALU.add)\
                       .then_inc(sem["sp_ready"], 1)

                def log_weight(t):
                    n = turns[t][1]
                    z = zs[t % 3][:, n * P:]
                    dve.wait_ge(sem["sfx_ready"], nth("sfx_ready", L, t + 1))
                    dve.tensor_tensor(z, z, bank(4 + t % 2, n * P), ALU.subtract)\
                       .then_inc(sem["lw_ready"], 1)

                def accumulate(t):
                    n = turns[t][1]
                    if n == 0:
                        return
                    dve.wait_ge(sem["sp_ready"], nth("sp_ready", L, t + 1))
                    own, keep = slice(n * P, (n + 1) * P), sp_keep[t % 2]
                    if n < 3:
                        later = slice((n + 1) * P, SEQ)
                        dve.tensor_tensor(acc[n % 2][:, later], acc[(n + 1) % 2][:, later],
                                          keep[:, later], ALU.add)\
                           .then_inc(sem["dve_step"], 1)
                        dve.wait_ge(sem["dve_step"], steps.next(L))
                    dve.tensor_copy(acc[n % 2][:, own], keep[:, own]).then_inc(sem["dve_step"], 1)
                    dve.wait_ge(sem["dve_step"], steps.next(L))

                def y_low(h):
                    dve.wait_ge(sem["yb_hi_ready"], nth("yb_hi_ready", L, h + 1))
                    dve.tensor_tensor(yb_lo[:, h, :], bank(6 + h % 2), yb_hi[:, h, :].bitcast(F32),
                                      ALU.subtract).then_inc(sem["yb_ready"], 1)

                scaled(0)
                for t in range(16):
                    if t + 1 < 16:
                        scaled(t + 1)
                    softplus(t)
                    if t >= 1:
                        log_weight(t - 1)
                    accumulate(t)
                    if t % 4 == 2 and t > 4:
                        y_low(t // 4 - 1)
                log_weight(15)
                y_low(3)

            def retention(L, steps):
                for c in range(4):
                    dve.wait_ge(sem["rx_ready"], nth("rx_ready", L, c + 1))
                    own, partner = dcy[c % 2][:, 0:SEQ], dcy[c % 2][:, SEQ:2 * SEQ]
                    dve.tensor_tensor(own, cq[:, c, :], rope[:, 0, :], ALU.mult)\
                       .then_inc(sem["dve_step"], 1)
                    dve.wait_ge(sem["dve_step"], steps.next(L))
                    dve.tensor_tensor(partner, bank(4 + c % 2), rope[:, 1, :], ALU.mult)\
                       .then_inc(sem["dve_step"], 1)
                    dve.wait_ge(sem["dve_step"], steps.next(L))
                    dve.tensor_tensor(cq[:, c, :], own, partner, ALU.add).then_inc(sem["rot_ready"], 1)
                dve.wait_ge(sem["rot_ready"], nth("rot_ready", L, 4))

                def decay_of(h):
                    if h >= 2:
                        dve.wait_ge(sem["ret_ready"], nth("ret_ready", L, h - 1))
                    for n in range(4):
                        at, w = (4 - n) * (3 - n) // 2 * P, (4 - n) * P
                        dve.wait_ge(sem["st_ready"], nth("st_ready", L, 4 * h + n + 1))
                        dve.tensor_tensor(dcy[h % 2][:, at:at + w], bank(2 + n, n * P), decays[:, h, 0:w],
                                          ALU.mult).then_inc(sem["decay_ready"], 1)

                def centre(h):
                    dve.wait_ge(sem["mu_ready"], nth("mu_ready", L, h + 1))
                    dve.tensor_tensor(cen[h % 2][:], ret[h % 2][:], bank(7), ALU.subtract)\
                       .then_inc(sem["cen_ready"], 1)

                def finish(h):
                    dve.wait_ge(sem["cy0_ready"], nth("cy0_ready", L, h + 1))
                    if h >= 1:
                        dve.wait_ge(sem["yc_split"], nth("yc_split", L, h))
                    dve.tensor_tensor(ct[:], cy[:], cy[:], ALU.mult).then_inc(sem["dve_step"], 1)
                    dve.wait_ge(sem["dve_step"], steps.next(L))
                    dve.scalar_tensor_tensor(ct[:], bank(1), EPS, ct[:], ALU.add, ALU.mult)\
                       .then_inc(sem["dve_step"], 1)
                    dve.wait_ge(sem["dve_step"], steps.next(L))
                    dve.tensor_scalar(ct[:], ct[:], -0.5, 1.5, ALU.mult, ALU.add)\
                       .then_inc(sem["dve_step"], 1)
                    dve.wait_ge(sem["dve_step"], steps.next(L))
                    dve.tensor_tensor(ct[:], ct[:], cy[:], ALU.mult).then_inc(sem["dve_step"], 1)
                    dve.wait_ge(sem["dve_step"], steps.next(L))
                    dve.tensor_tensor(ct[:], ct[:], cen[h % 2][:], ALU.mult)\
                       .then_inc(sem["dve_step"], 1)
                    dve.wait_ge(sem["dve_step"], steps.next(L))
                    dve.scalar_tensor_tensor(ct[:], ct[:], vecs[:, bass.ds(V_RET + L * 4 + h, 1)],
                                             cg[:, h, :], ALU.mult, ALU.mult).then_inc(sem["yc_ready"], 1)

                def y_low(h):
                    dve.wait_ge(sem["yc_hi_ready"], nth("yc_hi_ready", L, h + 1))
                    dve.tensor_tensor(yc_lo[:, h, :], ct[:], yc_hi[:, h, :].bitcast(F32), ALU.subtract)\
                       .then_inc(sem["yc_split"], 1)

                decay_of(0)
                for h in range(4):
                    if h < 3:
                        decay_of(h + 1)
                    centre(h)
                    if h >= 1:
                        finish(h - 1)
                        y_low(h - 1)
                finish(3)
                y_low(3)

            def add_block(L, j, b, slab_end):
                dve.wait_ge(sem["slab_used"], nth("slab_used", L, slab_end))
                dve.tensor_tensor(x[:, j, :], x[:, j, :], bank(b), ALU.add).then_inc(sem["x_new"], 1)

            def add_square(L, p, n, norm):
                dve.wait_ge(sem["sq_ready"], nth("sq_ready", L, n))
                dve.wait_ge(sem["sum_added"], nth("sum_added", L, n - 1))
                dve.wait_ge(sem["sum_cleared"], nth("sum_cleared", L, norm))
                dve.tensor_tensor(sumsq[:], sumsq[:], square[p][:], ALU.add).then_inc(sem["sum_added"], 1)

            dve.memset(eps[:], EPS).then_inc(memset_done, 1)
            dve.memset(rel_ext[REL_BUCKETS:REL_BUCKETS + 1, :], MASKED).then_inc(memset_done, 1)
            for k in range(KD):
                dve.wait_ge(sem["sq_ready"], k + 1)
                if k >= 1:
                    dve.wait_ge(sem["sum_added"], k)
                    dve.tensor_tensor(sumsq[:], sumsq[:], square[k % 2][:], ALU.add)\
                       .then_inc(sem["sum_added"], 1)
                else:
                    dve.tensor_copy(sumsq[:], square[0][:]).then_inc(sem["sum_added"], 1)
            for n in range(3):
                dve.wait_ge(line_mm, n + 1)
                dve.tensor_copy(lines[:, n * SEQ:(n + 1) * SEQ], ps[0:12, n, :]).then_inc(line_copied, 1)
            for h in range(SLOTS):
                for half, (a, z) in enumerate(((0, SEQ), (SEQ, TABLE))):
                    dve.wait_ge(table_mm, 2 * h + half + 1)
                    dve.tensor_copy(table[:, h, a:z], bank(3 + 2 * (h % 2) + half, 0, z - a))\
                       .then_inc(table_ready, 1)
            dve.wait_ge(const_in, 16 * 7)
            dve.wait_ge(table_ready, 2 * SLOTS)

            with dve.Fori(0, DEPTH) as L:
                steps = Steps("dve_step")
                low_at(L, 0)
                low_at(L, 1)
                norm(L, 1, steps)
                section(L, 0, A_CHUNKS, 6, 0,
                        lambda c: av[:, c // 2, :, c % 2 * P:(c % 2 + 1) * P])
                windows(L, steps)
                section(L, A_CHUNKS, B_CHUNKS, 4, 6, lambda c: bv[:, :, c * P:(c + 1) * P])
                stick_breaking(L, steps)
                section(L, A_CHUNKS + B_CHUNKS, C_CHUNKS, 4, 10, lambda c: cvv[:, :, c * P:(c + 1) * P])
                retention(L, steps)
                with dve.Fori(0, KD) as j:
                    steps.enter(j, 4)
                    for b in range(4):
                        low(L, 4 * j + (S_M + b + 2), b % 2, (K_PROJ if b == 1 else KD) * P)
                    dve.wait_ge(sem["slab_used"], nth("slab_used", L, 4 * j + (S_M + 4)))
                    dve.wait_ge(sem["gate_ready"], nth("gate_ready", L, 3 * j + 3))
                    dve.wait_ge(sem["m_split"], nth("m_split", L, j))
                    dve.tensor_tensor(mt[0][:], bank(1), sg[0][:], ALU.mult)\
                       .then_inc(sem["dve_step"], 1)
                    dve.wait_ge(sem["dve_step"], steps.next(L))
                    dve.tensor_tensor(mt[1][:], bank(4), sg[1][:], ALU.mult)\
                       .then_inc(sem["dve_step"], 1)
                    dve.wait_ge(sem["dve_step"], steps.next(L))
                    dve.tensor_tensor(mt[0][:], mt[0][:], mt[1][:], ALU.add)\
                       .then_inc(sem["dve_step"], 1)
                    dve.wait_ge(sem["dve_step"], steps.next(L))
                    dve.tensor_tensor(mt[1][:], bank(5), sg[2][:], ALU.mult)\
                       .then_inc(sem["dve_step"], 1)
                    dve.wait_ge(sem["dve_step"], steps.next(L))
                    dve.tensor_tensor(mt[0][:], mt[0][:], mt[1][:], ALU.add).then_inc(sem["m_ready"], 1)
                    dve.wait_ge(sem["m_hi_ready"], nth("m_hi_ready", L, j + 1))
                    dve.tensor_tensor(m_lo[:, j, :], mt[0][:], m_hi[:, j, :].bitcast(F32), ALU.subtract)\
                       .then_inc(sem["m_split"], 1)
                steps.leave(KD)
                dve.memset(sumsq[:], 0.0).then_inc(sem["sum_cleared"], 1)
                with dve.Fori(0, KD // 2) as i:
                    for p in range(2):
                        low(L, 2 * i + (S_O + p + 2), p, KD * P)
                        add_block(L, 2 * i + p, p, 2 * i + (S_O + p + 1))
                        add_square(L, p, 2 * i + (p + 1), 1)
                norm(L, 2, steps)

                def ffn_block(c, n):
                    low(L, 2 * c + (S_F + 2), 0, n)
                    dve.wait_ge(sem["cv_ready"], nth("cv_ready", L, c + 1))
                    at = V_CONV + L * (4 * KF) + 4 * c
                    dve.scalar_tensor_tensor(cv[:, 1:], bank(0, 0, SEQ - 1),
                                             vecs[:, bass.ds(at + 1, 1)], cv[:, 1:],
                                             ALU.mult, ALU.add)\
                       .then_inc(sem["dve_step"], 1)
                    dve.wait_ge(sem["dve_step"], steps.next(L))
                    dve.scalar_tensor_tensor(cv[:, 2:], bank(0, 0, SEQ - 2), vecs[:, bass.ds(at, 1)],
                                             cv[:, 2:], ALU.mult, ALU.add).then_inc(sem["conv_done"], 1)
                    low(L, 2 * c + (S_F + 3), 1, n)
                    dve.wait_ge(sem["gelu_ready"], nth("gelu_ready", L, c + 1))
                    dve.wait_ge(sem["slab_used"], nth("slab_used", L, 2 * c + (S_F + 2)))
                    dve.wait_ge(sem["af_split"], nth("af_split", L, c))
                    dve.tensor_tensor(af[:], bank(1), cv[:], ALU.mult).then_inc(sem["af_ready"], 1)
                    dve.wait_ge(sem["af_hi_ready"], nth("af_hi_ready", L, c + 1))
                    dve.tensor_tensor(act_lo[:, c, :], af[:], act_hi[:, c, :].bitcast(F32),
                                      ALU.subtract).then_inc(sem["af_split"], 1)

                with dve.Fori(0, KF - 1) as c:
                    steps.enter(c, 1)
                    ffn_block(c, KD * P)
                steps.leave(KF - 1)
                ffn_block(KF - 1, KHALF * P)
                dve.memset(sumsq[:], 0.0).then_inc(sem["sum_cleared"], 1)

                def down_pair(i, last):
                    for b in range(2):
                        for p in range(2):
                            if not (last and b == 1):
                                low(L, 4 * i + (S_D + 2 * b + p + 2), p, KHALF * P)
                        add_block(L, 2 * i + b, b, 4 * i + (S_D + 2 * b + 2))
                        add_square(L, b, 2 * i + (KD + b + 1), 2)

                with dve.Fori(0, KD // 2 - 1) as i:
                    down_pair(i, False)
                down_pair(KD // 2 - 1, True)
                steps.end()
            root(DEPTH, 1, Steps("dve_step"))
            for k in range(KD):
                at = V_NORM + 2 * DEPTH * KD + k
                dve.scalar_tensor_tensor(x[:, k, :], x[:, k, :], vecs[:, at:at + 1], rs[:],
                                         ALU.mult, ALU.mult).then_inc(out_ready, 1)


def bucket(distance):
    exact = REL_BUCKETS // 2
    n = np.maximum(distance, 0)
    large = exact + (np.log(np.maximum(n, 1) / exact) / np.log(REL_MAX_DIST / exact)
                     * (REL_BUCKETS - exact)).astype(np.int64)
    return np.where(n < exact, n, np.minimum(large, REL_BUCKETS - 1)).astype(np.int64)


def bias_lines():
    i1, i2 = np.arange(LINE1), np.arange(LINE2)
    d1, d2 = 511 - i1, 127 - i2
    parts = [(bucket(d1), (d1 >= 0) & (d1 <= 128)), (bucket(4 * d2), d2 >= 0),
             (bucket(4 * d2), (d2 >= 0) & (d2 % 4 == 0))]
    rows = np.concatenate([np.where(ok, b, REL_BUCKETS) for b, ok in parts])
    return (np.arange(REL_BUCKETS + 1)[:, None] == rows[None, :]).astype(np.float32)


def matrices():
    a, b = np.arange(P)[:, None], np.arange(P)[None, :]
    one = np.ones((P, P), np.float32)
    turn = np.where((b % HD < HD // 2) & (a == b + HD // 2), -1.0, 0.0)
    turn = np.where((b % HD >= HD // 2) & (a == b - HD // 2), 1.0, turn)
    return np.stack([one, one / D_MODEL, one / P, (a >= b) * one, (a == b) * one, turn * one,
                     np.where(a < b, 0.0, MASKED) * one, (a + b == P - 1) * one], 1).astype(np.float32)


def decay_tables():
    gamma = np.log1p(-np.exp2(-5.0 - np.arange(4, dtype=np.float64)))
    d = np.arange(SEQ)[None, :] - np.arange(P)[:, None]
    return np.stack([np.where(d >= 0, np.exp(np.maximum(d, 0) * g), 0.0) for g in gamma], 1)\
        .astype(np.float32)


def rope_tables():
    half = HD // 2
    inv = (np.float32(10000.0) ** (-np.arange(half, dtype=np.float32) / np.float32(half))).astype(np.float32)
    angle = np.arange(SEQ, dtype=np.float32)[None, :] * inv[:, None]
    angle = np.tile(angle.astype(np.float64), (P // half, 1))
    return np.stack([np.cos(angle), np.sin(angle)], 1).astype(np.float32)


def slabs(w, order=None):
    n, rows, columns = w.shape
    w = w.reshape(n, rows // P, P, columns // P, P).transpose(0, 3, 2, 1, 4)
    if order is not None:
        w = w[:, order]
    return w.reshape(n, -1, P, rows)


def halves(w):
    n, c, p, e = w.shape
    return w.reshape(n, c, p, 2, e // 2).transpose(0, 1, 3, 2, 4).reshape(n, 2 * c, p, e // 2)


def columns(v):
    return v.reshape(-1, P).T


def kernel(x, rel_bias, norm_mix_w, w_in, b_gate, ret_norm_w, w_proj_a, w_proj_b, w_proj_c,
           w_out, norm_ffn_w, w_up, w_gate, conv_w, conv_b, w_down, final_norm_w):
    import concourse.bacc as bacc
    from concourse.bass_utils import run_bass_kernel_spmd

    a = {k: np.asarray(v) for k, v in locals().items() if k not in ("bacc", "run_bass_kernel_spmd")}
    order = (list(range(12, 18)) + list(range(12)) + list(range(26, 30)) + list(range(18, 26))
             + list(range(34, 38)) + list(range(30, 34)) + list(range(38, 42)))
    gates = slabs(a["w_in"][:, :, S_M * P:]).reshape(DEPTH, 3, KD, P, KD * P).transpose(0, 2, 1, 3, 4)
    upgate = np.stack([slabs(a["w_up"]), slabs(a["w_gate"])], 2)
    norms = np.concatenate([np.stack([a["norm_mix_w"], a["norm_ffn_w"]], 1).ravel(), a["final_norm_w"]])
    conv = np.concatenate([a["conv_w"], a["conv_b"][:, None]], 1).reshape(DEPTH, 4, KF, P)
    arrays = {
        "x_t": a["x"][0].reshape(SEQ, KD, P).transpose(2, 1, 0),
        "vectors": np.concatenate([
            columns(norms), columns(a["b_gate"].reshape(DEPTH, 3, KD, P).transpose(0, 2, 1, 3)),
            columns(conv.transpose(0, 2, 1, 3)), columns(a["ret_norm_w"])], 1),
        "rel_bias": a["rel_bias"],
        "onehot": bias_lines(), "mats": matrices(), "decay": decay_tables(), "cos_sin": rope_tables(),
        "w_qkv": slabs(a["w_in"][:, :, :S_M * P], order).reshape(-1, P, KD * P),
        "w_gates": gates.reshape(-1, P, KD * P),
        "w_proj": np.concatenate([slabs(a["w_proj_a"]), slabs(a["w_proj_b"]), slabs(a["w_proj_c"])], 3)
        .reshape(-1, P, K_PROJ * P),
        "w_o": slabs(a["w_out"]).reshape(-1, P, KD * P),
        "w_upgate": upgate.reshape(-1, P, KD * P),
        "w_down": halves(slabs(a["w_down"])).reshape(-1, P, KHALF * P),
    }
    arrays = {k: np.ascontiguousarray(v) for k, v in arrays.items()}
    nc = bacc.Bacc("TRN2", target_bir_lowering=False, num_devices=1)
    args = [nc.dram_tensor(k, v.shape, F32, kind="ExternalInput").ap() for k, v in arrays.items()]
    line = nc.dram_tensor("line_dram", (12, LINE), F32, kind="Internal").ap()
    out = nc.dram_tensor("out_t", (P, KD, SEQ), F32, kind="ExternalOutput").ap()
    trunk_program(nc, *args, line, out)
    result = run_bass_kernel_spmd(nc, [arrays], core_ids=[0]).results[0]["out_t"]
    return result.transpose(2, 1, 0).reshape(1, SEQ, D_MODEL)
```

```python
from contextlib import ExitStack

import numpy as np

import concourse.bass as bass
from concourse import mybir
from concourse.alu_op_type import AluOpType as ALU

F32 = mybir.dt.float32
F32R = mybir.dt.float32r
ACT = mybir.ActivationFunctionType
AX_X = mybir.AxisListType.X

P = 128
D_MODEL, SEQ, DEPTH = 1024, 512, 2
KD = D_MODEL // P
NT = SEQ // P
GROUPS, SLOTS = 3, 4
HD = 64
D_FF = 2816
KF = D_FF // P
KHALF = KF // 2
PER_HEAD = 8.0
REL_BUCKETS, REL_MAX_DIST = 32, 2048
EPS = 1e-6
MASKED = -1e30
SB_SCALE = 128.0 ** -0.5
NLE = "natural_log_exp_and_others"

A_CHUNKS, B_CHUNKS, C_CHUNKS = 18, 12, 12
V_A, V_B, V_C = 6, 4, 4
S_M = A_CHUNKS + B_CHUNKS + C_CHUNKS
S_O = S_M + 4 * KD
S_F = S_O + KD
S_D = S_F + 2 * KF
SLABS = S_D + 2 * KD
K_PROJ = 10
SLAB_MAX = KHALF * P
GATE_BANKS = (0, 4, 5)

LINE1, LINE2 = 1024, 256
LINE = LINE1 + 2 * LINE2
EXT = SEQ + 3
TABLE = EXT + 2 * P

V_NORM, V_BGATE = 0, (2 * DEPTH + 1) * KD
V_CONV = V_BGATE + DEPTH * 3 * KD
V_RET = V_CONV + DEPTH * 4 * KF
VECS = V_RET + DEPTH * 4

DVE_STEPS, ACT_STEPS = 158, 38

COUNTS = {
    "raw_in0": (16 * (SLABS // 2), 0), "raw_in1": (16 * (SLABS // 2), 0),
    "hi_ready": (SLABS, 0), "split_done": (SLABS, 2), "slab_used": (SLABS, 2),
    "ms_ready": (2, 0), "y0_ready": (2, 0),
    "hf_ready": (2 * KD, 0), "h_hi_ready": (2 * KD, 0), "h_ready": (2 * KD, 0),
    "x_new": (2 * KD, 2), "sq_ready": (2 * KD, KD), "sum_added": (2 * KD, KD),
    "sum_cleared": (2, 0),
    "chunk_out": (S_M, 0), "vt_ready": (14, 0), "v_ready": (14, 0),
    "s_ready": (16, 0), "s_used": (16, 0), "l_ready": (16, 0), "p_ready": (16, 0), "diag_ready": (16, 0),
    "t_ready": (16, 0), "pt_ready": (16, 0), "o_ready": (16, 0),
    "ya_hi_ready": (4, 0), "ya_ready": (4, 0),
    "z_ready": (16, 0), "zs_ready": (16, 0), "e_ready": (16, 0), "sp_ready": (16, 0),
    "sfx_ready": (16, 0), "lw_ready": (16, 0), "w_ready": (16, 0),
    "yb_mm": (4, 0), "yb_hi_ready": (4, 0), "yb_ready": (4, 0),
    "rx_ready": (4, 0), "rot_ready": (4, 0),
    "st_ready": (16, 0), "decay_ready": (16, 0), "ret_ready": (4, 1), "table_in": (16 * 12, 0), "swish_ready": (1, 0), "ret_copied": (4, 0),
    "mu_ready": (4, 0), "cen_ready": (4, 0), "csq_ready": (4, 0), "var_ready": (4, 0),
    "cy0_ready": (4, 0), "yc_ready": (4, 0), "yc_hi_ready": (4, 0), "yc_split": (4, 0),
    "gate_ready": (3 * KD, 3), "m_ready": (KD, 1), "m_hi_ready": (KD, 0), "m_split": (KD, 1),
    "cv_ready": (KF, 0), "conv_done": (KF, 1), "gelu_ready": (KF, 0), "af_ready": (KF, 1),
    "af_hi_ready": (KF, 0), "af_split": (KF, 1),
    "dve_step": (DVE_STEPS, 0), "act_step": (ACT_STEPS, 0),
}
GRANTED = {"split_done": 2, "slab_used": 2, "x_new": 2, "gate_ready": 3, "m_ready": 1,
           "conv_done": 1, "af_ready": 1, "m_split": 1, "af_split": 1, "ret_ready": 1}


def trunk_program(nc, x_t, vectors, rel_bias, onehot, mats, decay, cos_sin, w_qkv, w_gates,
                  w_proj, w_o, w_upgate, w_down, line_dram, out_t):
    with ExitStack() as ctx:
        def sb(stack, name, shape, dtype=F32):
            return stack.enter_context(nc.sbuf_tensor(name, shape, dtype))

        x = sb(ctx, "x", [P, KD, SEQ])
        h_hi = sb(ctx, "h_hi", [P, KD, SEQ], F32R)
        h_lo = sb(ctx, "h_lo", [P, KD, SEQ], F32R)
        raw = [sb(ctx, f"raw{p}", [P, SLAB_MAX]) for p in range(2)]
        w_hi = [sb(ctx, f"w_hi{p}", [P, SLAB_MAX], F32R) for p in range(2)]
        w_lo = [sb(ctx, f"w_lo{p}", [P, SLAB_MAX], F32R) for p in range(2)]
        with ExitStack() as z:
            cvv = sb(z, "cvv", [P, NT, 4 * P])
        table = sb(ctx, "table", [P, SLOTS, TABLE])
        decays = sb(ctx, "decays", [P, 4, SEQ])
        rope = sb(ctx, "rope", [P, 2, SEQ])
        consts = sb(ctx, "consts", [P, 7, P])
        vecs = sb(ctx, "vecs", [P, VECS])
        stat = sb(ctx, "stat", [P, 4, 4])
        eps = sb(ctx, "eps", [P, 1])
        ones, ones_model, tri, ident, rotate, neg_mask, flip = (
            consts[:, i, :] for i in range(7))
        with ExitStack() as z:
            hf = [sb(z, f"hf{p}", [P, SEQ]) for p in range(2)]
            sumsq = sb(z, "sumsq", [P, SEQ])
            y0 = sb(z, "y0", [P, SEQ])
            rs = sb(z, "rs", [P, SEQ])
        square = hf
        with ExitStack() as z:
            cv = sb(z, "cv", [P, SEQ])
            af = sb(z, "af", [P, SEQ])
        with ExitStack() as z:
            vs = [sb(z, f"vs{p}", [P, SEQ]) for p in range(2)]
            acc = [sb(z, f"acc{p}", [P, SEQ]) for p in range(2)]
            diag = [sb(z, f"diag{p}", [P, P]) for p in range(2)]
        ctx.enter_context(nc.sbuf_tensor("scratch", [P, 5, SEQ], F32))

        def spare(stack, name, kib):
            sb(stack, name, [P, kib * 256])

        with ExitStack() as mix:
            ya_hi, ya_lo = (sb(mix, f"ya_{n}", [P, 2, SEQ], F32R) for n in ("hi", "lo"))
            with ExitStack() as z:
                aq = sb(z, "aq", [P, 6, SEQ])
                ak = sb(z, "ak", [P, 6, SEQ])
                av = sb(z, "av", [P, GROUPS, NT, SLOTS * HD])
                logits = [sb(z, f"logits{p}", [P, 6 * P]) for p in range(2)]
                probs_t = [sb(z, f"probs_t{p}", [P, 6 * P]) for p in range(2)]
                bv = sb(z, "bv", [P, NT, 4 * P])
                bq = sb(z, "bq", [P, 4, SEQ])
                bk = sb(z, "bk", [P, 4, SEQ])
            with ExitStack() as z:
                zs = [sb(z, f"zs{p}", [P, SEQ]) for p in range(3)]
                ez = [sb(z, f"ez{p}", [P, SEQ]) for p in range(2)]
                sp_keep = [sb(z, f"sp_keep{p}", [P, SEQ]) for p in range(2)]
                wts = sb(z, "wts", [P, 10 * P])
            with ExitStack() as z:
                dcy = [sb(z, f"dcy{p}", [P, 10 * P]) for p in range(2)]
                ret = [sb(z, f"ret{p}", [P, SEQ]) for p in range(2)]
                cen = [sb(z, f"cen{p}", [P, SEQ]) for p in range(2)]
                spare(z, "spare26", 1)
                yb_hi, yb_lo = (sb(z, f"yb_{n}", [P, 4, SEQ], F32R) for n in ("hi", "lo"))
                with ExitStack() as y:
                    cq = sb(y, "cq", [P, 4, SEQ])
                    csq = sb(y, "csq", [P, SEQ])
                    cy = sb(y, "cy", [P, SEQ])
                sg = [sb(z, f"sg{p}", [P, SEQ]) for p in range(3)]
                mt = [sb(z, f"mt{p}", [P, SEQ]) for p in range(2)]
                spare(z, "spare53", 3)
                yc_hi, yc_lo = (sb(z, f"yc_{n}", [P, 4, SEQ], F32R) for n in ("hi", "lo"))
                with ExitStack() as y:
                    ct = sb(y, "ct", [P, SEQ])
                    spare(y, "spare74", 6)
                    cg = sb(y, "cg", [P, 4, SEQ])
                m_lo = sb(z, "m_lo", [P, KD, SEQ], F32R)
            m_hi = sb(mix, "m_hi", [P, KD, SEQ], F32R)
        with ExitStack() as ffn:
            act_hi, act_lo = (sb(ffn, f"act_{n}", [P, KF, SEQ], F32R) for n in ("hi", "lo"))
        with ExitStack() as z:
            rel_ext = sb(z, "rel_ext", [REL_BUCKETS + 1, 12])
            one_hot = sb(z, "one_hot", [REL_BUCKETS + 1, LINE])
            lines = sb(z, "lines", [12, LINE])
        ctx.enter_context(nc.sbuf_tensor("layer_area", [P, 2 * KF * SEQ], F32))

        ps = ctx.enter_context(nc.psum_tensor("ps", [P, 8, SEQ], F32))

        sem = {name: ctx.enter_context(nc.semaphore(name)) for name in COUNTS}
        raw_in = [sem["raw_in0"], sem["raw_in1"]]
        const_in = ctx.enter_context(nc.semaphore("const_in"))
        late_in = ctx.enter_context(nc.semaphore("late_in"))
        x_in = ctx.enter_context(nc.semaphore("x_in"))
        memset_done = ctx.enter_context(nc.semaphore("memset_done"))
        line_mm = ctx.enter_context(nc.semaphore("line_mm"))
        line_copied = ctx.enter_context(nc.semaphore("line_copied"))
        line_out = ctx.enter_context(nc.semaphore("line_out"))
        out_ready = ctx.enter_context(nc.semaphore("out_ready"))
        out_done = ctx.enter_context(nc.semaphore("out_done"))
        block = ctx.enter_context(nc.Block())

        def nth(name, L, k):
            per_layer, before = COUNTS[name]
            return L * per_layer + (k + before)

        def grant(eng, *names):
            for name in names:
                eng.sem_inc(sem[name], GRANTED[name])

        def bank(b, a=0, z=SEQ):
            return ps[:, b, a:z]

        class Steps:

            def __init__(self, name):
                self.name, self.k, self.turn = name, 0, 0

            def next(self, L):
                self.k += 1
                return nth(self.name, L, self.turn + self.k)

            def enter(self, i, per_turn):
                self.turn, self.first, self.per_turn = i * per_turn, self.k, per_turn

            def leave(self, turns):
                assert self.k - self.first == self.per_turn, (self.name, self.k - self.first)
                self.k, self.turn = self.first + turns * self.per_turn, 0

            def end(self):
                assert self.k == COUNTS[self.name][0], (self.name, self.k)

        def elements(s):
            if S_M <= s < S_O:
                return (K_PROJ if (s - S_M) % 4 == 3 else KD) * P
            return KHALF * P if s >= S_D else KD * P

        @block.sync
        def _(sp):
            sp.dma_start(x[:], x_t).then_inc(x_in, 16)
            for dst, src in ((rel_ext[0:REL_BUCKETS, :], rel_bias), (one_hot[:], onehot),
                             (vecs[:], vectors), (consts[:], mats)):
                sp.dma_start(dst, src).then_inc(const_in, 16)
            sp.dma_start(decays[:], decay).then_inc(late_in, 16)
            sp.dma_start(rope[:], cos_sin).then_inc(late_in, 16)

            def load(L, s, p, src, n):
                sp.wait_ge(sem["split_done"], nth("split_done", L, s - 1))
                sp.dma_start(raw[p][:, 0:n], src).then_inc(raw_in[p], 16)

            with sp.Fori(0, DEPTH) as L:
                with sp.Fori(0, 2) as i:
                    for p in range(2):
                        load(L, 2 * i + p, p, w_qkv[L * S_M + 2 * i + p], KD * P)
                sp.wait_ge(line_out, 16)
                sp.wait_ge(sem["ret_ready"], nth("ret_ready", L, 0))
                for h in range(SLOTS):
                    for g, at, step, n in ((0, 0, 4, EXT), (1, LINE1, 1, P), (2, LINE1 + LINE2, 1, P)):
                        to = 0 if g == 0 else EXT + (g - 1) * P
                        src = bass.AP(tensor=line_dram.tensor, offset=(SLOTS * g + h) * LINE + at,
                                      ap=[[step, P], [1, n]])
                        sp.dma_start(table[:, h, to:to + n], src).then_inc(sem["table_in"], 16)
                with sp.Fori(2, S_M // 2) as i:
                    for p in range(2):
                        load(L, 2 * i + p, p, w_qkv[L * S_M + 2 * i + p], KD * P)
                with sp.Fori(0, KD) as j:
                    for b in range(3):
                        load(L, 4 * j + (S_M + b), b % 2, w_gates[L * (3 * KD) + 3 * j + b], KD * P)
                    load(L, 4 * j + (S_M + 3), 1, w_proj[L * KD + j], K_PROJ * P)
                for first, src, n, per in ((S_O, w_o, KD // 2, KD * P), (S_F, w_upgate, KF, KD * P),
                                           (S_D, w_down, KD, KHALF * P)):
                    with sp.Fori(0, n) as i:
                        for p in range(2):
                            load(L, 2 * i + (first + p), p, src[L * (2 * n) + 2 * i + p], per)

            for k in range(KD):
                sp.wait_ge(out_ready, k + 1)
                sp.dma_start(out_t[:, k, :], x[:, k, :]).then_inc(out_done, 16)
            sp.wait_ge(out_done, 16 * KD)

        @block.gpsimd
        def _(pool):
            pool.wait_ge(line_copied, 3)
            pool.dma_start(line_dram, lines[:]).then_inc(line_out, 16)

        @block.tensor
        def _(pe):
            grant(pe, "slab_used", "ret_ready")

            def slab(L, s, p, products, split=None):
                pe.wait_ge(sem["split_done"], nth("split_done", L, s + 1))
                at = 0
                for b, blocks, first, hi, lo, starts, ends in products:
                    for k in range(blocks):
                        w = slice((at + k) * P, (at + k + 1) * P)
                        if split:
                            pe.wait_ge(sem[split[0]], nth(split[0], L, split[1] + k + 1))
                        for n, (a, y) in enumerate(((w_hi[p], hi), (w_hi[p], lo), (w_lo[p], hi))):
                            mm = pe.matmul(bank(b), a[:, w], y[:, first + k, :],
                                           start=starts and k == 0 and n == 0,
                                           stop=ends and k == blocks - 1 and n == 2)
                    at += blocks
                mm.then_inc(sem["slab_used"], 1)

            def from_h(b):
                return [(b, KD, 0, h_hi, h_lo, True, True)]

            def mean_square(L, n):
                pe.wait_ge(sem["sum_added"], nth("sum_added", L, KD * (n - 1)))
                pe.matmul(bank(6), ones_model, sumsq[:], start=True, stop=True)\
                  .then_inc(sem["ms_ready"], 1)

            def row_block(L, s, p, b, k):
                w = slice(k * P, (k + 1) * P)
                for n, (a, y) in enumerate(((w_hi[p], h_hi), (w_hi[p], h_lo), (w_lo[p], h_hi))):
                    mm = pe.matmul(bank(b), a[:, w], y[:, k, :], start=k == 0 and n == 0,
                                   stop=k == KD - 1 and n == 2)
                return mm

            def chunk_block(L, first, c, k, v_chunks, v_before, v_bank):
                s = first + c
                if k == 0:
                    pe.wait_ge(sem["split_done"], nth("split_done", L, s + 1))
                    if s >= 2:
                        pe.wait_ge(sem["chunk_out"], nth("chunk_out", L, s - 1))
                if s == 0:
                    pe.wait_ge(sem["h_ready"], nth("h_ready", L, k + 1))
                mm = row_block(L, s, s % 2, s % 2, k)
                if k < KD - 1:
                    return
                mm.then_inc(sem["slab_used"], 1)
                if 1 <= c <= v_chunks:
                    v = v_before + c - 1
                    pe.wait_ge(sem["chunk_out"], nth("chunk_out", L, s))
                    if v >= 1:
                        pe.wait_ge(sem["v_ready"], nth("v_ready", L, v))
                    for t in range(NT):
                        mm = pe.transpose(bank(v_bank, t * P, (t + 1) * P),
                                          vs[v % 2][:, t * P:(t + 1) * P], ident)
                    mm.then_inc(sem["vt_ready"], 1)

            def first_section(L):
                for c in range(V_A + 2):
                    for k in range(KD):
                        chunk_block(L, 0, c, k, V_A, 0, 2)
                with pe.Fori(0, (A_CHUNKS - V_A - 2) // 2) as i:
                    for p in range(2):
                        s = 2 * i + (V_A + 2 + p)
                        pe.wait_ge(sem["chunk_out"], nth("chunk_out", L, s - 1))
                        slab(L, s, p, from_h(p))
                pe.wait_ge(sem["chunk_out"], nth("chunk_out", L, A_CHUNKS))
                pe.wait_ge(sem["v_ready"], nth("v_ready", L, V_A))

            def b_blocks(L, start, n):
                for a in range(start, start + n):
                    chunk_block(L, A_CHUNKS, a // KD, a % KD, V_B, V_A, 4)

            def c_blocks(L, start, n):
                for a in range(start, start + n):
                    chunk_block(L, A_CHUNKS + B_CHUNKS, a // KD, a % KD, V_C, V_A + V_B, 7)

            def gate_blocks(L, start, n):
                for a in range(start, start + n):
                    b, k = divmod(a, KD)
                    if k == 0:
                        pe.wait_ge(sem["split_done"], nth("split_done", L, S_M + b + 1))
                    mm = row_block(L, S_M + b, b, GATE_BANKS[b], k)
                    if k == KD - 1:
                        mm.then_inc(sem["slab_used"], 1)

            def windows(L):
                def scores(i):
                    r, h = divmod(i, SLOTS)
                    if i >= 1:
                        pe.wait_ge(sem["s_used"], nth("s_used", L, i))
                    rows = slice(HD * (h % 2), HD * (h % 2) + HD)
                    for g in range(GROUPS):
                        q = aq[rows, 2 * g + h // 2, r * P:(r + 1) * P]
                        k = ak[rows, 2 * g + h // 2, :]
                        if g == 0:
                            mm = pe.matmul(bank(2), q, k, start=True, stop=True)
                        else:
                            mm = pe.matmul(bank(3, (g - 1) * P, g * P), q,
                                           k[:, r * P:(r + 1) * P], start=True, stop=True)
                    mm.then_inc(sem["s_ready"], 1)

                scores(0)
                scores(1)
                for i in range(16):
                    r, h = divmod(i, SLOTS)
                    pe.wait_ge(sem["diag_ready"], nth("diag_ready", L, i + 1))
                    if i >= 1:
                        pe.wait_ge(sem["pt_ready"], nth("pt_ready", L, i))
                    for kb in range(6):
                        mm = pe.matmul(bank(6 + kb // 4, kb % 4 * P, (kb % 4 + 1) * P),
                                       logits[i % 2][:, kb * P:(kb + 1) * P], diag[i % 2][:],
                                       start=True, stop=True)
                    mm.then_inc(sem["t_ready"], 1)
                    b_blocks(L, 6 * i, 2)
                    if i + 2 < 16:
                        scores(i + 2)
                    b_blocks(L, 6 * i + 2, 2)
                    pe.wait_ge(sem["pt_ready"], nth("pt_ready", L, i + 1))
                    if h == 0 and r >= 1:
                        pe.wait_ge(sem["ya_ready"], nth("ya_ready", L, r))
                    out = ps[HD * (h % 2):HD * (h % 2) + HD, 5, h // 2 * P:(h // 2 + 1) * P]
                    for kb in range(6):
                        g, t = (0, kb) if kb < 4 else (kb - 3, r)
                        mm = pe.matmul(out, av[:, g, t, h * HD:(h + 1) * HD],
                                       probs_t[i % 2][:, kb * P:(kb + 1) * P], start=kb == 0,
                                       stop=kb == 5)
                    mm.then_inc(sem["o_ready"], 1)
                    b_blocks(L, 6 * i + 4, 2)
                pe.wait_ge(sem["ya_ready"], nth("ya_ready", L, 4))
                pe.wait_ge(sem["chunk_out"], nth("chunk_out", L, A_CHUNKS + B_CHUNKS))
                pe.wait_ge(sem["v_ready"], nth("v_ready", L, V_A + V_B))

            def stick_breaking(L):
                turns = [(h, n) for h in range(4) for n in (3, 2, 1, 0)]

                def scores(t):
                    h, n = turns[t]
                    if t >= 2:
                        pe.wait_ge(sem["zs_ready"], nth("zs_ready", L, t - 1))
                    pe.matmul(bank(2 + t % 2, n * P), bk[:, h, n * P:(n + 1) * P], bq[:, h, n * P:],
                              start=True, stop=True).then_inc(sem["z_ready"], 1)

                def output(h):
                    pe.wait_ge(sem["w_ready"], nth("w_ready", L, 4 * h + 4))
                    if h >= 1:
                        pe.wait_ge(sem["yb_ready"], nth("yb_ready", L, h))
                    for n in range(4):
                        at = (4 - n) * (3 - n) // 2 * P
                        mm = pe.matmul(bank(6, n * P), bv[:, n, h * P:(h + 1) * P],
                                       wts[:, at:at + (4 - n) * P], start=n == 0, stop=True,
                                       skip_group_check=True)
                    mm.then_inc(sem["yb_mm"], 1)

                scores(0)
                scores(1)
                for t, (h, n) in enumerate(turns):
                    c_blocks(L, 6 * t, 3)
                    pe.wait_ge(sem["sp_ready"], nth("sp_ready", L, t + 1))
                    if t >= 2:
                        pe.wait_ge(sem["lw_ready"], nth("lw_ready", L, t - 1))
                    mm = pe.matmul(bank(4 + t % 2, n * P), tri, sp_keep[t % 2][:, n * P:],
                                   start=True, stop=True)
                    if n < 3:
                        mm = pe.matmul(bank(4 + t % 2, (n + 1) * P), ones,
                                       acc[(n + 1) % 2][:, (n + 1) * P:], start=False, stop=True,
                                       skip_group_check=True)
                    mm.then_inc(sem["sfx_ready"], 1)
                    if t + 2 < 16:
                        scores(t + 2)
                    if n == 3 and h >= 1:
                        output(h - 1)
                    c_blocks(L, 6 * t + 3, 3)
                output(3)
                pe.wait_ge(sem["yb_ready"], nth("yb_ready", L, 4))
                pe.wait_ge(sem["chunk_out"], nth("chunk_out", L, S_M))
                pe.wait_ge(sem["v_ready"], nth("v_ready", L, V_A + V_B + V_C))

            def retention(L):
                for c in range(4):
                    if c >= 2:
                        pe.wait_ge(sem["rot_ready"], nth("rot_ready", L, c - 1))
                    pe.matmul(bank(4 + c % 2), rotate, cq[:, c, :], start=True, stop=True)\
                      .then_inc(sem["rx_ready"], 1)
                    gate_blocks(L, 2 * c, 2)
                pe.wait_ge(sem["rot_ready"], nth("rot_ready", L, 4))

                def scores(h):
                    rows = slice(HD * (h % 2), HD * (h % 2) + HD)
                    for n in range(4):
                        if 4 * h + n >= 2:
                            pe.wait_ge(sem["decay_ready"], nth("decay_ready", L, 4 * h + n - 1))
                        pe.matmul(bank(2 + n % 2, n * P), cq[rows, 2 + h // 2, n * P:(n + 1) * P],
                                  cq[rows, h // 2, n * P:], start=True, stop=True)\
                          .then_inc(sem["st_ready"], 1)

                def mix(h):
                    pe.wait_ge(sem["decay_ready"], nth("decay_ready", L, 4 * h + 4))
                    if h >= 1:
                        pe.wait_ge(sem["ret_copied"], nth("ret_copied", L, h))
                    for n in range(4):
                        at = (4 - n) * (3 - n) // 2 * P
                        mm = pe.matmul(bank(6, n * P), cvv[:, n, h * P:(h + 1) * P],
                                       dcy[h % 2][:, at:at + (4 - n) * P], start=n == 0, stop=True,
                                       skip_group_check=True)
                    mm.then_inc(sem["ret_ready"], 1)

                def mean(h):
                    pe.wait_ge(sem["ret_copied"], nth("ret_copied", L, h + 1))
                    if h >= 1:
                        pe.wait_ge(sem["cen_ready"], nth("cen_ready", L, h))
                    pe.matmul(bank(7), ones_model, ret[h % 2][:], start=True, stop=True)\
                      .then_inc(sem["mu_ready"], 1)

                def variance(h):
                    pe.wait_ge(sem["csq_ready"], nth("csq_ready", L, h + 1))
                    if h >= 1:
                        pe.wait_ge(sem["yc_ready"], nth("yc_ready", L, h))
                    pe.matmul(bank(1), ones_model, csq[:], start=True, stop=True)\
                      .then_inc(sem["var_ready"], 1)

                scores(0)
                for h in range(4):
                    mix(h)
                    if h < 3:
                        scores(h + 1)
                    gate_blocks(L, KD + 2 * h, 2)
                    mean(h)
                    if h >= 1:
                        variance(h - 1)
                variance(3)
            pe.wait_ge(const_in, 16 * 4)
            pe.wait_ge(memset_done, 2)
            for n in range(3):
                pe.matmul(ps[0:12, n, :], rel_ext[:, :], one_hot[:, n * SEQ:(n + 1) * SEQ],
                          start=True, stop=True).then_inc(line_mm, 1)
            with pe.Fori(0, DEPTH) as L:
                mean_square(L, 1)
                first_section(L)
                windows(L)
                stick_breaking(L)
                retention(L)
                def gate(L, j, b):
                    pe.wait_ge(sem["gate_ready"], nth("gate_ready", L, 3 * j + (b - 2)))
                    slab(L, 4 * j + (S_M + b), b % 2, from_h(GATE_BANKS[b]))

                def branches(L, j):
                    pe.wait_ge(sem["m_ready"], nth("m_ready", L, j))
                    slab(L, 4 * j + (S_M + 3), 1,
                         [(1, 2, 0, ya_hi, ya_lo, True, True), (2, 4, 0, yb_hi, yb_lo, True, True),
                          (3, 4, 0, yc_hi, yc_lo, True, True)])

                gate(L, 0, 2)
                pe.wait_ge(sem["yc_split"], nth("yc_split", L, 4))
                branches(L, 0)
                with pe.Fori(1, KD) as j:
                    for b in range(3):
                        gate(L, j, b)
                    branches(L, j)
                with pe.Fori(0, KD // 2) as i:
                    for p in range(2):
                        pe.wait_ge(sem["x_new"], nth("x_new", L, 2 * i + (p - 1)))
                        slab(L, 2 * i + (S_O + p), p, [(p, KD, 0, m_hi, m_lo, True, True)],
                             ("m_split", 0))
                mean_square(L, 2)
                with pe.Fori(0, KF) as c:
                    pe.wait_ge(sem["conv_done"], nth("conv_done", L, c))
                    slab(L, 2 * c + S_F, 0, from_h(0), ("h_ready", KD))
                    pe.wait_ge(sem["af_ready"], nth("af_ready", L, c))
                    slab(L, 2 * c + (S_F + 1), 1, from_h(1))
                with pe.Fori(0, KD // 2) as i:
                    for b in range(2):
                        for p in range(2):
                            pe.wait_ge(sem["af_split"], nth("af_split", L, (p + 1) * KHALF))
                            if p == 0:
                                pe.wait_ge(sem["conv_done"], nth("conv_done", L, KF))
                                pe.wait_ge(sem["x_new"], nth("x_new", L, 2 * i + (KD + b - 1)))
                            slab(L, 4 * i + (S_D + 2 * b + p), p,
                                 [(b, KHALF, p * KHALF, act_hi, act_lo, p == 0, p == 1)])
            mean_square(DEPTH, 1)

        @block.scalar
        def _(act):
            grant(act, "gate_ready")

            def high(L, s, p, turn, n):
                act.wait_ge(sem[f"raw_in{p}"], nth(f"raw_in{p}", L, 16 * turn))
                act.wait_ge(sem["slab_used"], nth("slab_used", L, s - 1))
                act.activation(w_hi[p][:, 0:n], raw[p][:, 0:n], ACT.Copy).then_inc(sem["hi_ready"], 1)

            def high_at(L, s):
                high(L, s, s % 2, s // 2 + 1, elements(s))

            def norm(L, n, steps):
                act.wait_ge(sem["ms_ready"], nth("ms_ready", L, n))
                act.activation(y0[:], bank(6), ACT.Ln, bias=eps[:]).then_inc(sem["act_step"], 1)
                act.wait_ge(sem["act_step"], steps.next(L))
                act.activation(y0[:], y0[:], ACT.Exp, scale=-0.5).then_inc(sem["y0_ready"], 1)

            def norm_high(L, n):
                for k in range(KD):
                    act.wait_ge(sem["hf_ready"], nth("hf_ready", L, KD * (n - 1) + k + 1))
                    act.activation(h_hi[:, k, :], hf[k % 2][:], ACT.Copy).then_inc(sem["h_hi_ready"], 1)

            def by_class(t):
                return t.rearrange("p (u r) -> p r u", r=4)

            def take(L, s, dst, order=0, scale=1.0, v=None):
                high_at(L, s + 2)
                act.wait_ge(sem["slab_used"], nth("slab_used", L, s + 1))
                if v is not None and v >= 2:
                    act.wait_ge(sem["vt_ready"], nth("vt_ready", L, v - 1))
                src = bank(s % 2)
                if order:
                    dst, src = dst.rearrange("p (r u) -> p r u", r=4)[:, :, ::order], by_class(src)
                act.activation(dst, src, ACT.Copy, scale=scale).then_inc(sem["chunk_out"], 1)

            def take_b(L, c):
                if c < V_B:
                    take(L, A_CHUNKS + c, vs[(V_A + c) % 2][:], v=V_A + c)
                else:
                    take(L, A_CHUNKS + c, bq[:, c - 4, :] if c < 8 else bk[:, c - 8, :])

            def take_c(L, c):
                s = A_CHUNKS + B_CHUNKS + c
                if c < V_C:
                    take(L, s, vs[(V_A + V_B + c) % 2][:], v=V_A + V_B + c)
                elif c < 8:
                    take(L, s, cq[:, c - 4, :], scale=1.0 if c < 6 else HD ** -0.5)
                else:
                    take(L, s, cg[:, c - 8, :])

            def windows(L):
                def probs(i):
                    act.wait_ge(sem["l_ready"], nth("l_ready", L, i + 1))
                    act.activation(logits[i % 2][:], logits[i % 2][:], ACT.Exp,
                                   bias=stat[:, 1, i % 4:i % 4 + 1],
                                   accum_out=stat[:, 2, i % 4:i % 4 + 1]).then_inc(sem["p_ready"], 1)

                def y_high(r):
                    act.wait_ge(sem["o_ready"], nth("o_ready", L, SLOTS * (r + 1)))
                    act.activation(ya_hi[:, :, r::4], ps[:, 5, 0:2 * P].rearrange("p (c u) -> p c u", c=2),
                                   ACT.Copy).then_inc(sem["ya_hi_ready"], 1)

                probs(0)
                for i in range(16):
                    if i + 1 < 16:
                        probs(i + 1)
                    act.wait_ge(sem["t_ready"], nth("t_ready", L, i + 1))
                    if i >= 2:
                        act.wait_ge(sem["o_ready"], nth("o_ready", L, i - 1))
                    act.activation(probs_t[i % 2][:, :], ps[:, 6:8, :].rearrange("p b n -> p (b n)")[:, 0:6 * P],
                                   ACT.Copy).then_inc(sem["pt_ready"], 1)
                    if i % SLOTS == 0 and i:
                        y_high(i // SLOTS - 1)
                    if i >= 1 and i % 4 != 1:
                        take_b(L, 3 * ((i - 1) // 4) + (i - 2) % 4)
                take_b(L, B_CHUNKS - 1)
                y_high(3)

            def stick_breaking(L, steps):
                turns = [(h, n) for h in range(4) for n in (3, 2, 1, 0)]

                def log_part(t):
                    n = turns[t][1]
                    e, z = ez[t % 2][:, n * P:], zs[t % 3][:, n * P:]
                    act.wait_ge(sem["zs_ready"], nth("zs_ready", L, t + 1))
                    act.activation(e, z, ACT.Abs).then_inc(sem["act_step"], 1)
                    act.wait_ge(sem["act_step"], steps.next(L))
                    act.activation(e, e, ACT.Exp, scale=-1.0).then_inc(sem["act_step"], 1)
                    act.wait_ge(sem["act_step"], steps.next(L))
                    act.activation(e, e, ACT.Ln, bias=1.0).then_inc(sem["e_ready"], 1)

                def weights(t):
                    h, n = turns[t]
                    at = (4 - n) * (3 - n) // 2 * P
                    act.wait_ge(sem["lw_ready"], nth("lw_ready", L, t + 1))
                    if n == 3 and h >= 1:
                        act.wait_ge(sem["yb_mm"], nth("yb_mm", L, h))
                    act.activation(wts[:, at:at + (4 - n) * P], zs[t % 3][:, n * P:], ACT.Exp)\
                       .then_inc(sem["w_ready"], 1)

                def y_high(h):
                    act.wait_ge(sem["yb_mm"], nth("yb_mm", L, h + 1))
                    act.activation(yb_hi[:, h, :], bank(6), ACT.Copy)\
                       .then_inc(sem["yb_hi_ready"], 1)

                for t in range(16):
                    log_part(t)
                    if t >= 1:
                        weights(t - 1)
                    if t % 4 == 1 and t > 4:
                        y_high(t // 4 - 1)
                    if t >= 1 and t % 4 != 1:
                        take_c(L, 3 * ((t - 1) // 4) + (t - 2) % 4)
                take_c(L, C_CHUNKS - 1)
                weights(15)
                y_high(3)

            def retention(L, steps):
                def start_root(h):
                    act.wait_ge(sem["var_ready"], nth("var_ready", L, h + 1))
                    if h >= 1:
                        act.wait_ge(sem["yc_ready"], nth("yc_ready", L, h))
                    act.activation(cy[:], bank(1), ACT.Ln, bias=eps[:], scale=PER_HEAD).then_inc(sem["act_step"], 1)
                    act.wait_ge(sem["act_step"], steps.next(L))
                    act.activation(cy[:], cy[:], ACT.Exp, scale=-0.5).then_inc(sem["cy0_ready"], 1)

                def y_high(h):
                    act.wait_ge(sem["yc_ready"], nth("yc_ready", L, h + 1))
                    act.activation(yc_hi[:, h, :], ct[:], ACT.Copy).then_inc(sem["yc_hi_ready"], 1)

                for h in range(4):
                    act.wait_ge(sem["ret_ready"], nth("ret_ready", L, h + 1))
                    if h >= 2:
                        act.wait_ge(sem["cen_ready"], nth("cen_ready", L, h - 1))
                    act.activation(ret[h % 2][:], bank(6), ACT.Copy).then_inc(sem["ret_copied"], 1)
                    if h >= 1:
                        start_root(h - 1)
                    act.wait_ge(sem["cen_ready"], nth("cen_ready", L, h + 1))
                    act.activation(csq[:], cen[h % 2][:], ACT.Square).then_inc(sem["csq_ready"], 1)
                    if h >= 1:
                        y_high(h - 1)
                start_root(3)
                y_high(3)

            def square_of(L, j, p, n):
                act.wait_ge(sem["x_new"], nth("x_new", L, n))
                act.activation(square[p][:], x[:, j, :], ACT.Square).then_inc(sem["sq_ready"], 1)

            act.preload_act_table_set(NLE)
            act.wait_ge(x_in, 16)
            for k in range(KD):
                if k >= 2:
                    act.wait_ge(sem["sum_added"], k - 1)
                act.activation(square[k % 2][:], x[:, k, :], ACT.Square).then_inc(sem["sq_ready"], 1)
            act.wait_ge(memset_done, 2)
            act.wait_ge(const_in, 16 * 4)
            act.wait_ge(line_out, 16)

            with act.Fori(0, DEPTH) as L:
                steps = Steps("act_step")
                act.preload_act_table_set(NLE)
                high_at(L, 0)
                high_at(L, 1)
                norm(L, 1, steps)
                norm_high(L, 1)
                for v in range(V_A):
                    take(L, v, vs[v % 2][:], v >= 2, v=v)
                for c in range(6):
                    take(L, V_A + c, aq[:, c, :], -1, HD ** -0.5)
                for c in range(6):
                    take(L, V_A + 6 + c, ak[:, c, :], c >= 2)
                windows(L)
                stick_breaking(L, steps)
                act.activation(cg[:], cg[:], ACT.Silu).then_inc(sem["swish_ready"], 1)
                act.preload_act_table_set(NLE)
                retention(L, steps)
                with act.Fori(0, KD) as j:
                    for b in range(4):
                        s = 4 * j + (S_M + b)
                        high(L, s + 2, b % 2, 2 * j + (S_M // 2 + b // 2 + 2),
                             (K_PROJ if b == 1 else KD) * P)
                        if b < 3:
                            act.wait_ge(sem["slab_used"], nth("slab_used", L, s + 1))
                            act.wait_ge(sem["m_ready"], nth("m_ready", L, j))
                            act.activation(sg[b][:], bank(GATE_BANKS[b]), ACT.Sigmoid,
                                           bias=vecs[:, bass.ds(V_BGATE + L * (3 * KD) + 3 * j + b, 1)])\
                               .then_inc(sem["gate_ready"], 1)
                    act.wait_ge(sem["m_ready"], nth("m_ready", L, j + 1))
                    act.activation(m_hi[:, j, :], mt[0][:], ACT.Copy).then_inc(sem["m_hi_ready"], 1)
                act.preload_act_table_set(NLE)
                with act.Fori(0, KD // 2) as i:
                    for p in range(2):
                        high(L, 2 * i + (S_O + p + 2), p, i + (S_O // 2 + 2), KD * P)
                        square_of(L, 2 * i + p, p, 2 * i + (p + 1))
                norm(L, 2, steps)
                norm_high(L, 2)

                def ffn_block(c, n, turn):
                    high(L, 2 * c + (S_F + 2), 0, turn, n)
                    act.wait_ge(sem["slab_used"], nth("slab_used", L, 2 * c + (S_F + 1)))
                    act.wait_ge(sem["af_ready"], nth("af_ready", L, c))
                    at = V_CONV + L * (4 * KF) + 4 * c
                    act.activation(cv[:], bank(0), ACT.Identity, bias=vecs[:, bass.ds(at + 3, 1)],
                                   scale=vecs[:, bass.ds(at + 2, 1)]).then_inc(sem["cv_ready"], 1)
                    act.wait_ge(sem["conv_done"], nth("conv_done", L, c + 1))
                    act.activation(cv[:], cv[:], ACT.Gelu_apprx_tanh).then_inc(sem["gelu_ready"], 1)
                    high(L, 2 * c + (S_F + 3), 1, turn, n)
                    act.wait_ge(sem["af_ready"], nth("af_ready", L, c + 1))
                    act.activation(act_hi[:, c, :], af[:], ACT.Copy).then_inc(sem["af_hi_ready"], 1)

                act.preload_act_table(ACT.Gelu_apprx_tanh)
                with act.Fori(0, KF - 1) as c:
                    ffn_block(c, KD * P, c + (S_F // 2 + 2))
                ffn_block(KF - 1, KHALF * P, KF - 1 + S_F // 2 + 2)

                def down_pair(i, last):
                    for b in range(2):
                        for p in range(2):
                            if not (last and b == 1):
                                high(L, 4 * i + (S_D + 2 * b + p + 2), p, 2 * i + (S_D // 2 + b + 2),
                                     KHALF * P)
                        square_of(L, 2 * i + b, b, 2 * i + (KD + b + 1))

                with act.Fori(0, KD // 2 - 1) as i:
                    down_pair(i, False)
                down_pair(KD // 2 - 1, True)
                steps.end()
            act.preload_act_table_set(NLE)
            steps = Steps("act_step")
            norm(DEPTH, 1, steps)

        @block.vector
        def _(dve):
            grant(dve, "split_done", "x_new", "m_ready", "conv_done", "af_ready", "m_split", "af_split")

            def low(L, s, p, n):
                dve.wait_ge(sem["hi_ready"], nth("hi_ready", L, s + 1))
                dve.tensor_tensor(w_lo[p][:, 0:n], raw[p][:, 0:n], w_hi[p][:, 0:n].bitcast(F32),
                                  ALU.subtract).then_inc(sem["split_done"], 1)

            def low_at(L, s):
                low(L, s, s % 2, elements(s))

            def root(L, n, steps):
                dve.wait_ge(sem["y0_ready"], nth("y0_ready", L, n))
                dve.tensor_tensor(rs[:], y0[:], y0[:], ALU.mult).then_inc(sem["dve_step"], 1)
                dve.wait_ge(sem["dve_step"], steps.next(L))
                dve.scalar_tensor_tensor(rs[:], bank(6), EPS, rs[:], ALU.add, ALU.mult)\
                   .then_inc(sem["dve_step"], 1)
                dve.wait_ge(sem["dve_step"], steps.next(L))
                dve.tensor_scalar(rs[:], rs[:], -0.5, 1.5, ALU.mult, ALU.add)\
                   .then_inc(sem["dve_step"], 1)
                dve.wait_ge(sem["dve_step"], steps.next(L))
                dve.tensor_tensor(rs[:], rs[:], y0[:], ALU.mult).then_inc(sem["dve_step"], 1)
                dve.wait_ge(sem["dve_step"], steps.next(L))

            def norm(L, n, steps):
                root(L, n, steps)

                def scaled(k):
                    if k >= 2:
                        dve.wait_ge(sem["h_ready"], nth("h_ready", L, KD * (n - 1) + k - 1))
                    dve.scalar_tensor_tensor(hf[k % 2][:], x[:, k, :],
                                             vecs[:, bass.ds(V_NORM + L * (2 * KD) + ((n - 1) * KD + k), 1)],
                                             rs[:], ALU.mult, ALU.mult).then_inc(sem["hf_ready"], 1)

                scaled(0)
                for k in range(KD):
                    if k + 1 < KD:
                        scaled(k + 1)
                    dve.wait_ge(sem["h_hi_ready"], nth("h_hi_ready", L, KD * (n - 1) + k + 1))
                    dve.tensor_tensor(h_lo[:, k, :], hf[k % 2][:], h_hi[:, k, :].bitcast(F32),
                                      ALU.subtract).then_inc(sem["h_ready"], 1)

            def turn(L, s, store=None, v=None, v_bank=None):
                low_at(L, s + 2)
                if v is not None:
                    dve.wait_ge(sem["vt_ready"], nth("vt_ready", L, v + 1))
                    dve.tensor_copy(store, bank(v_bank).rearrange("p (t n) -> p t n", t=NT))\
                       .then_inc(sem["v_ready"], 1)

            def turn_b(L, c):
                if 1 <= c <= V_B:
                    turn(L, A_CHUNKS + c, bv[:, :, (c - 1) * P:c * P], V_A + c - 1, 4)
                else:
                    turn(L, A_CHUNKS + c)

            def turn_c(L, c):
                s = A_CHUNKS + B_CHUNKS + c
                if 1 <= c <= V_C:
                    turn(L, s, cvv[:, :, (c - 1) * P:c * P], V_A + V_B + c - 1, 7)
                else:
                    turn(L, s)

            def windows(L, steps):
                def biased(i):
                    r, h = divmod(i, SLOTS)
                    dve.wait_ge(sem["s_ready"], nth("s_ready", L, i + 1))
                    if i >= 2:
                        dve.wait_ge(sem["t_ready"], nth("t_ready", L, i - 1))
                    to = logits[i % 2]
                    dve.tensor_tensor(to[:, 0:SEQ], bank(2), table[:, h, 3 - r:3 - r + SEQ], ALU.add)\
                       .then_inc(sem["dve_step"], 1)
                    dve.wait_ge(sem["dve_step"], steps.next(L))
                    dve.tensor_tensor(to[:, SEQ:6 * P], bank(3, 0, 2 * P), table[:, h, EXT:TABLE],
                                      ALU.add).then_inc(sem["s_used"], 1)
                    dve.wait_ge(sem["s_used"], nth("s_used", L, i + 1))

                def maximum(i):
                    a, to = i % 4, logits[i % 2]
                    dve.reduce_max(stat[:, 0, a:a + 1], to[:], AX_X).then_inc(sem["dve_step"], 1)
                    dve.wait_ge(sem["dve_step"], steps.next(L))
                    dve.tensor_scalar(stat[:, 1, a:a + 1], stat[:, 0, a:a + 1], -1.0, None, ALU.mult)\
                       .then_inc(sem["l_ready"], 1)

                def scaled_flip(i):
                    a = i % 4
                    dve.wait_ge(sem["p_ready"], nth("p_ready", L, i + 1))
                    dve.reciprocal(stat[:, 3, a:a + 1], stat[:, 2, a:a + 1]).then_inc(sem["dve_step"], 1)
                    dve.wait_ge(sem["dve_step"], steps.next(L))
                    if i >= 2:
                        dve.wait_ge(sem["t_ready"], nth("t_ready", L, i - 1))
                    dve.tensor_scalar(diag[i % 2][:], flip, stat[:, 3, a:a + 1], None, ALU.mult)\
                       .then_inc(sem["diag_ready"], 1)

                def y_low(r):
                    dve.wait_ge(sem["ya_hi_ready"], nth("ya_hi_ready", L, r + 1))
                    dve.tensor_tensor(ya_lo[:, :, r::4], ps[:, 5, 0:2 * P].rearrange("p (c u) -> p c u", c=2),
                                      ya_hi[:, :, r::4].bitcast(F32), ALU.subtract)\
                       .then_inc(sem["ya_ready"], 1)

                dve.wait_ge(sem["table_in"], nth("table_in", L, 16 * 12))
                biased(0)
                maximum(0)
                for i in range(16):
                    if i + 1 < 16:
                        biased(i + 1)
                    scaled_flip(i)
                    if i + 1 < 16:
                        maximum(i + 1)
                    if i % SLOTS == 0 and i:
                        y_low(i // SLOTS - 1)
                    if i >= 1 and i % 4 != 1:
                        turn_b(L, 3 * ((i - 1) // 4) + (i - 2) % 4)
                turn_b(L, B_CHUNKS - 1)
                y_low(3)

            def stick_breaking(L, steps):
                turns = [(h, n) for h in range(4) for n in (3, 2, 1, 0)]

                def scaled(t):
                    n = turns[t][1]
                    dve.wait_ge(sem["z_ready"], nth("z_ready", L, t + 1))
                    if t >= 3:
                        dve.wait_ge(sem["w_ready"], nth("w_ready", L, t - 2))
                    z, b = zs[t % 3], 2 + t % 2
                    if n < 3:
                        dve.tensor_scalar(z[:, (n + 1) * P:], bank(b, (n + 1) * P), SB_SCALE, None, ALU.mult)
                    dve.scalar_tensor_tensor(z[:, n * P:(n + 1) * P], bank(b, n * P, (n + 1) * P), SB_SCALE,
                                             neg_mask, ALU.mult, ALU.add).then_inc(sem["zs_ready"], 1)

                def softplus(t):
                    n = turns[t][1]
                    dve.wait_ge(sem["e_ready"], nth("e_ready", L, t + 1))
                    dve.scalar_tensor_tensor(sp_keep[t % 2][:, n * P:], zs[t % 3][:, n * P:], 0.0,
                                             ez[t % 2][:, n * P:], ALU.max, ALU.add)\
                       .then_inc(sem["sp_ready"], 1)

                def log_weight(t):
                    n = turns[t][1]
                    z = zs[t % 3][:, n * P:]
                    dve.wait_ge(sem["sfx_ready"], nth("sfx_ready", L, t + 1))
                    dve.tensor_tensor(z, z, bank(4 + t % 2, n * P), ALU.subtract)\
                       .then_inc(sem["lw_ready"], 1)

                def accumulate(t):
                    n = turns[t][1]
                    if n == 0:
                        return
                    dve.wait_ge(sem["sp_ready"], nth("sp_ready", L, t + 1))
                    own, keep = slice(n * P, (n + 1) * P), sp_keep[t % 2]
                    if n < 3:
                        later = slice((n + 1) * P, SEQ)
                        dve.tensor_tensor(acc[n % 2][:, later], acc[(n + 1) % 2][:, later],
                                          keep[:, later], ALU.add)\
                           .then_inc(sem["dve_step"], 1)
                        dve.wait_ge(sem["dve_step"], steps.next(L))
                    dve.tensor_copy(acc[n % 2][:, own], keep[:, own]).then_inc(sem["dve_step"], 1)
                    dve.wait_ge(sem["dve_step"], steps.next(L))

                def y_low(h):
                    dve.wait_ge(sem["yb_hi_ready"], nth("yb_hi_ready", L, h + 1))
                    dve.tensor_tensor(yb_lo[:, h, :], bank(6), yb_hi[:, h, :].bitcast(F32),
                                      ALU.subtract).then_inc(sem["yb_ready"], 1)

                scaled(0)
                for t in range(16):
                    if t + 1 < 16:
                        scaled(t + 1)
                    softplus(t)
                    if t >= 1:
                        log_weight(t - 1)
                    accumulate(t)
                    if t % 4 == 2 and t > 4:
                        y_low(t // 4 - 1)
                    if t >= 1 and t % 4 != 1:
                        turn_c(L, 3 * ((t - 1) // 4) + (t - 2) % 4)
                turn_c(L, C_CHUNKS - 1)
                log_weight(15)
                y_low(3)

            def retention(L, steps):
                dve.wait_ge(late_in, 32)
                for c in range(4):
                    dve.wait_ge(sem["rx_ready"], nth("rx_ready", L, c + 1))
                    own, partner = dcy[c % 2][:, 0:SEQ], dcy[c % 2][:, SEQ:2 * SEQ]
                    dve.tensor_tensor(own, cq[:, c, :], rope[:, 0, :], ALU.mult)\
                       .then_inc(sem["dve_step"], 1)
                    dve.wait_ge(sem["dve_step"], steps.next(L))
                    dve.tensor_tensor(partner, bank(4 + c % 2), rope[:, 1, :], ALU.mult)\
                       .then_inc(sem["dve_step"], 1)
                    dve.wait_ge(sem["dve_step"], steps.next(L))
                    dve.tensor_tensor(cq[:, c, :], own, partner, ALU.add).then_inc(sem["rot_ready"], 1)
                dve.wait_ge(sem["rot_ready"], nth("rot_ready", L, 4))

                def decay_of(h):
                    if h >= 2:
                        dve.wait_ge(sem["ret_ready"], nth("ret_ready", L, h - 1))
                    for n in range(4):
                        at, w = (4 - n) * (3 - n) // 2 * P, (4 - n) * P
                        dve.wait_ge(sem["st_ready"], nth("st_ready", L, 4 * h + n + 1))
                        dve.tensor_tensor(dcy[h % 2][:, at:at + w], bank(2 + n % 2, n * P), decays[:, h, 0:w],
                                          ALU.mult).then_inc(sem["decay_ready"], 1)

                def centre(h):
                    dve.wait_ge(sem["mu_ready"], nth("mu_ready", L, h + 1))
                    dve.scalar_tensor_tensor(cen[h % 2][:], bank(7), -PER_HEAD, ret[h % 2][:], ALU.mult, ALU.add)\
                       .then_inc(sem["cen_ready"], 1)

                def finish(h):
                    dve.wait_ge(sem["cy0_ready"], nth("cy0_ready", L, h + 1))
                    if h >= 1:
                        dve.wait_ge(sem["yc_split"], nth("yc_split", L, h))
                    else:
                        dve.wait_ge(sem["swish_ready"], nth("swish_ready", L, 1))
                    dve.tensor_tensor(ct[:], cy[:], cy[:], ALU.mult).then_inc(sem["dve_step"], 1)
                    dve.wait_ge(sem["dve_step"], steps.next(L))
                    dve.scalar_tensor_tensor(ct[:], bank(1), EPS / PER_HEAD, ct[:], ALU.add, ALU.mult)\
                       .then_inc(sem["dve_step"], 1)
                    dve.wait_ge(sem["dve_step"], steps.next(L))
                    dve.tensor_scalar(ct[:], ct[:], -0.5 * PER_HEAD, 1.5, ALU.mult, ALU.add)\
                       .then_inc(sem["dve_step"], 1)
                    dve.wait_ge(sem["dve_step"], steps.next(L))
                    dve.tensor_tensor(ct[:], ct[:], cy[:], ALU.mult).then_inc(sem["dve_step"], 1)
                    dve.wait_ge(sem["dve_step"], steps.next(L))
                    dve.tensor_tensor(ct[:], ct[:], cen[h % 2][:], ALU.mult)\
                       .then_inc(sem["dve_step"], 1)
                    dve.wait_ge(sem["dve_step"], steps.next(L))
                    dve.scalar_tensor_tensor(ct[:], ct[:], vecs[:, bass.ds(V_RET + L * 4 + h, 1)],
                                             cg[:, h, :], ALU.mult, ALU.mult).then_inc(sem["yc_ready"], 1)

                def y_low(h):
                    dve.wait_ge(sem["yc_hi_ready"], nth("yc_hi_ready", L, h + 1))
                    dve.tensor_tensor(yc_lo[:, h, :], ct[:], yc_hi[:, h, :].bitcast(F32), ALU.subtract)\
                       .then_inc(sem["yc_split"], 1)

                decay_of(0)
                for h in range(4):
                    if h < 3:
                        decay_of(h + 1)
                    centre(h)
                    if h >= 1:
                        finish(h - 1)
                        y_low(h - 1)
                finish(3)
                y_low(3)

            def add_block(L, j, b, slab_end):
                dve.wait_ge(sem["slab_used"], nth("slab_used", L, slab_end))
                dve.tensor_tensor(x[:, j, :], x[:, j, :], bank(b), ALU.add).then_inc(sem["x_new"], 1)

            def add_square(L, p, n, norm):
                dve.wait_ge(sem["sq_ready"], nth("sq_ready", L, n))
                dve.wait_ge(sem["sum_added"], nth("sum_added", L, n - 1))
                dve.wait_ge(sem["sum_cleared"], nth("sum_cleared", L, norm))
                dve.tensor_tensor(sumsq[:], sumsq[:], square[p][:], ALU.add).then_inc(sem["sum_added"], 1)

            dve.memset(eps[:], EPS).then_inc(memset_done, 1)
            dve.memset(rel_ext[REL_BUCKETS:REL_BUCKETS + 1, :], MASKED).then_inc(memset_done, 1)
            for k in range(KD):
                dve.wait_ge(sem["sq_ready"], k + 1)
                if k >= 1:
                    dve.wait_ge(sem["sum_added"], k)
                    dve.tensor_tensor(sumsq[:], sumsq[:], square[k % 2][:], ALU.add)\
                       .then_inc(sem["sum_added"], 1)
                else:
                    dve.tensor_copy(sumsq[:], square[0][:]).then_inc(sem["sum_added"], 1)
            for n in range(3):
                dve.wait_ge(line_mm, n + 1)
                dve.tensor_copy(lines[:, n * SEQ:(n + 1) * SEQ], ps[0:12, n, :]).then_inc(line_copied, 1)
            dve.wait_ge(const_in, 16 * 4)
            with dve.Fori(0, DEPTH) as L:
                steps = Steps("dve_step")
                low_at(L, 0)
                low_at(L, 1)
                norm(L, 1, steps)
                for c in range(A_CHUNKS):
                    if 1 <= c <= V_A:
                        turn(L, c, av[:, (c - 1) // 2, :, (c - 1) % 2 * P:((c - 1) % 2 + 1) * P], c - 1, 2)
                    else:
                        turn(L, c)
                windows(L, steps)
                stick_breaking(L, steps)
                retention(L, steps)
                with dve.Fori(0, KD) as j:
                    steps.enter(j, 4)
                    for b in range(4):
                        low(L, 4 * j + (S_M + b + 2), b % 2, (K_PROJ if b == 1 else KD) * P)
                    dve.wait_ge(sem["slab_used"], nth("slab_used", L, 4 * j + (S_M + 4)))
                    dve.wait_ge(sem["gate_ready"], nth("gate_ready", L, 3 * j + 3))
                    dve.wait_ge(sem["m_split"], nth("m_split", L, j))
                    dve.tensor_tensor(mt[0][:], bank(1), sg[0][:], ALU.mult)\
                       .then_inc(sem["dve_step"], 1)
                    dve.wait_ge(sem["dve_step"], steps.next(L))
                    dve.tensor_tensor(mt[1][:], bank(2), sg[1][:], ALU.mult)\
                       .then_inc(sem["dve_step"], 1)
                    dve.wait_ge(sem["dve_step"], steps.next(L))
                    dve.tensor_tensor(mt[0][:], mt[0][:], mt[1][:], ALU.add)\
                       .then_inc(sem["dve_step"], 1)
                    dve.wait_ge(sem["dve_step"], steps.next(L))
                    dve.tensor_tensor(mt[1][:], bank(3), sg[2][:], ALU.mult)\
                       .then_inc(sem["dve_step"], 1)
                    dve.wait_ge(sem["dve_step"], steps.next(L))
                    dve.tensor_tensor(mt[0][:], mt[0][:], mt[1][:], ALU.add).then_inc(sem["m_ready"], 1)
                    dve.wait_ge(sem["m_hi_ready"], nth("m_hi_ready", L, j + 1))
                    dve.tensor_tensor(m_lo[:, j, :], mt[0][:], m_hi[:, j, :].bitcast(F32), ALU.subtract)\
                       .then_inc(sem["m_split"], 1)
                steps.leave(KD)
                dve.memset(sumsq[:], 0.0).then_inc(sem["sum_cleared"], 1)
                with dve.Fori(0, KD // 2) as i:
                    for p in range(2):
                        low(L, 2 * i + (S_O + p + 2), p, KD * P)
                        add_block(L, 2 * i + p, p, 2 * i + (S_O + p + 1))
                        add_square(L, p, 2 * i + (p + 1), 1)
                norm(L, 2, steps)

                def ffn_block(c, n):
                    low(L, 2 * c + (S_F + 2), 0, n)
                    dve.wait_ge(sem["cv_ready"], nth("cv_ready", L, c + 1))
                    at = V_CONV + L * (4 * KF) + 4 * c
                    dve.scalar_tensor_tensor(cv[:, 1:], bank(0, 0, SEQ - 1),
                                             vecs[:, bass.ds(at + 1, 1)], cv[:, 1:],
                                             ALU.mult, ALU.add)\
                       .then_inc(sem["dve_step"], 1)
                    dve.wait_ge(sem["dve_step"], steps.next(L))
                    dve.scalar_tensor_tensor(cv[:, 2:], bank(0, 0, SEQ - 2), vecs[:, bass.ds(at, 1)],
                                             cv[:, 2:], ALU.mult, ALU.add).then_inc(sem["conv_done"], 1)
                    low(L, 2 * c + (S_F + 3), 1, n)
                    dve.wait_ge(sem["gelu_ready"], nth("gelu_ready", L, c + 1))
                    dve.wait_ge(sem["slab_used"], nth("slab_used", L, 2 * c + (S_F + 2)))
                    dve.wait_ge(sem["af_split"], nth("af_split", L, c))
                    dve.tensor_tensor(af[:], bank(1), cv[:], ALU.mult).then_inc(sem["af_ready"], 1)
                    dve.wait_ge(sem["af_hi_ready"], nth("af_hi_ready", L, c + 1))
                    dve.tensor_tensor(act_lo[:, c, :], af[:], act_hi[:, c, :].bitcast(F32),
                                      ALU.subtract).then_inc(sem["af_split"], 1)

                with dve.Fori(0, KF - 1) as c:
                    steps.enter(c, 1)
                    ffn_block(c, KD * P)
                steps.leave(KF - 1)
                ffn_block(KF - 1, KHALF * P)
                dve.memset(sumsq[:], 0.0).then_inc(sem["sum_cleared"], 1)

                def down_pair(i, last):
                    for b in range(2):
                        for p in range(2):
                            if not (last and b == 1):
                                low(L, 4 * i + (S_D + 2 * b + p + 2), p, KHALF * P)
                        add_block(L, 2 * i + b, b, 4 * i + (S_D + 2 * b + 2))
                        add_square(L, b, 2 * i + (KD + b + 1), 2)

                with dve.Fori(0, KD // 2 - 1) as i:
                    down_pair(i, False)
                down_pair(KD // 2 - 1, True)
                steps.end()
            root(DEPTH, 1, Steps("dve_step"))
            for k in range(KD):
                at = V_NORM + 2 * DEPTH * KD + k
                dve.scalar_tensor_tensor(x[:, k, :], x[:, k, :], vecs[:, at:at + 1], rs[:],
                                         ALU.mult, ALU.mult).then_inc(out_ready, 1)


def bucket(distance):
    exact = REL_BUCKETS // 2
    n = np.maximum(distance, 0)
    large = exact + (np.log(np.maximum(n, 1) / exact) / np.log(REL_MAX_DIST / exact)
                     * (REL_BUCKETS - exact)).astype(np.int64)
    return np.where(n < exact, n, np.minimum(large, REL_BUCKETS - 1)).astype(np.int64)


def bias_lines():
    i1, i2 = np.arange(LINE1), np.arange(LINE2)
    d1, d2 = 511 - i1, 127 - i2
    parts = [(bucket(d1), (d1 >= 0) & (d1 <= 128)), (bucket(4 * d2), d2 >= 0),
             (bucket(4 * d2), (d2 >= 0) & (d2 % 4 == 0))]
    rows = np.concatenate([np.where(ok, b, REL_BUCKETS) for b, ok in parts])
    return (np.arange(REL_BUCKETS + 1)[:, None] == rows[None, :]).astype(np.float32)


def matrices():
    a, b = np.arange(P)[:, None], np.arange(P)[None, :]
    one = np.ones((P, P), np.float32)
    turn = np.where((b % HD < HD // 2) & (a == b + HD // 2), -1.0, 0.0)
    turn = np.where((b % HD >= HD // 2) & (a == b - HD // 2), 1.0, turn)
    return np.stack([one, one / D_MODEL, (a >= b) * one, (a == b) * one, turn * one,
                     np.where(a < b, 0.0, MASKED) * one, (a + b == P - 1) * one], 1).astype(np.float32)


def decay_tables():
    gamma = np.log1p(-np.exp2(-5.0 - np.arange(4, dtype=np.float64)))
    d = np.arange(SEQ)[None, :] - np.arange(P)[:, None]
    return np.stack([np.where(d >= 0, np.exp(np.maximum(d, 0) * g), 0.0) for g in gamma], 1)\
        .astype(np.float32)


def rope_tables():
    half = HD // 2
    inv = (np.float32(10000.0) ** (-np.arange(half, dtype=np.float32) / np.float32(half))).astype(np.float32)
    angle = np.arange(SEQ, dtype=np.float32)[None, :] * inv[:, None]
    angle = np.tile(angle.astype(np.float64), (P // half, 1))
    return np.stack([np.cos(angle), np.sin(angle)], 1).astype(np.float32)


def slabs(w, order=None):
    n, rows, columns = w.shape
    w = w.reshape(n, rows // P, P, columns // P, P).transpose(0, 3, 2, 1, 4)
    if order is not None:
        w = w[:, order]
    return w.reshape(n, -1, P, rows)


def halves(w):
    n, c, p, e = w.shape
    return w.reshape(n, c, p, 2, e // 2).transpose(0, 1, 3, 2, 4).reshape(n, 2 * c, p, e // 2)


def columns(v):
    return v.reshape(-1, P).T


def kernel(x, rel_bias, norm_mix_w, w_in, b_gate, ret_norm_w, w_proj_a, w_proj_b, w_proj_c,
           w_out, norm_ffn_w, w_up, w_gate, conv_w, conv_b, w_down, final_norm_w):
    import concourse.bacc as bacc
    from concourse.bass_utils import run_bass_kernel_spmd

    a = {k: np.asarray(v) for k, v in locals().items() if k not in ("bacc", "run_bass_kernel_spmd")}
    order = (list(range(12, 18)) + list(range(12)) + list(range(26, 30)) + list(range(18, 26))
             + list(range(34, 38)) + list(range(30, 34)) + list(range(38, 42)))
    gates = slabs(a["w_in"][:, :, S_M * P:]).reshape(DEPTH, 3, KD, P, KD * P).transpose(0, 2, 1, 3, 4)
    upgate = np.stack([slabs(a["w_up"]), slabs(a["w_gate"])], 2)
    norms = np.concatenate([np.stack([a["norm_mix_w"], a["norm_ffn_w"]], 1).ravel(), a["final_norm_w"]])
    conv = np.concatenate([a["conv_w"], a["conv_b"][:, None]], 1).reshape(DEPTH, 4, KF, P)
    arrays = {
        "x_t": a["x"][0].reshape(SEQ, KD, P).transpose(2, 1, 0),
        "vectors": np.concatenate([
            columns(norms), columns(a["b_gate"].reshape(DEPTH, 3, KD, P).transpose(0, 2, 1, 3)),
            columns(conv.transpose(0, 2, 1, 3)), columns(a["ret_norm_w"])], 1),
        "rel_bias": a["rel_bias"],
        "onehot": bias_lines(), "mats": matrices(), "decay": decay_tables(), "cos_sin": rope_tables(),
        "w_qkv": slabs(a["w_in"][:, :, :S_M * P], order).reshape(-1, P, KD * P),
        "w_gates": gates.reshape(-1, P, KD * P),
        "w_proj": np.concatenate([slabs(a["w_proj_a"]), slabs(a["w_proj_b"]), slabs(a["w_proj_c"])], 3)
        .reshape(-1, P, K_PROJ * P),
        "w_o": slabs(a["w_out"]).reshape(-1, P, KD * P),
        "w_upgate": upgate.reshape(-1, P, KD * P),
        "w_down": halves(slabs(a["w_down"])).reshape(-1, P, KHALF * P),
    }
    arrays = {k: np.ascontiguousarray(v) for k, v in arrays.items()}
    nc = bacc.Bacc("TRN2", target_bir_lowering=False, num_devices=1)
    args = [nc.dram_tensor(k, v.shape, F32, kind="ExternalInput").ap() for k, v in arrays.items()]
    line = nc.dram_tensor("line_dram", (12, LINE), F32, kind="Internal").ap()
    out = nc.dram_tensor("out_t", (P, KD, SEQ), F32, kind="ExternalOutput").ap()
    trunk_program(nc, *args, line, out)
    result = run_bass_kernel_spmd(nc, [arrays], core_ids=[0]).results[0]["out_t"]
    return result.transpose(2, 1, 0).reshape(1, SEQ, D_MODEL)
```

```python
from contextlib import ExitStack

import numpy as np

import concourse.bass as bass
from concourse import mybir
from concourse.alu_op_type import AluOpType as ALU

F32 = mybir.dt.float32
F32R = mybir.dt.float32r
ACT = mybir.ActivationFunctionType
AX_X = mybir.AxisListType.X

P = 128
D_MODEL, SEQ, DEPTH = 1024, 512, 2
KD = D_MODEL // P
NT = SEQ // P
GROUPS, SLOTS = 3, 4
HD = 64
D_FF = 2816
KF = D_FF // P
KHALF = KF // 2
PER_HEAD = 8.0
REL_BUCKETS, REL_MAX_DIST = 32, 2048
EPS = 1e-6
MASKED = -1e30
SB_SCALE = 128.0 ** -0.5
NLE = "natural_log_exp_and_others"

A_CHUNKS, B_CHUNKS, C_CHUNKS = 18, 12, 12
V_A, V_B, V_C = 6, 4, 4
S_M = A_CHUNKS + B_CHUNKS + C_CHUNKS
S_O = S_M + 4 * KD
S_F = S_O + KD
S_D = S_F + 2 * KF
SLABS = S_D + 2 * KD
K_PROJ = 10
SLAB_MAX = KHALF * P
GATE_BANKS = (0, 4, 5)

LINE1, LINE2 = 1024, 256
LINE = LINE1 + 2 * LINE2
EXT = SEQ + 3
TABLE = EXT + 2 * P

BANDS = [(4, 0, P, 0), (5, 0, P, P), (0, 0, 64, 256), (1, 32, 96, 320), (2, 64, P, 384), (3, 96, P, 448)]
BANDED = BANDS[-1][3] + P - 96

V_NORM, V_BGATE = 0, (2 * DEPTH + 1) * KD
V_CONV = V_BGATE + DEPTH * 3 * KD
V_RET = V_CONV + DEPTH * 4 * KF
VECS = V_RET + DEPTH * 4

DVE_STEPS, ACT_STEPS = 142, 38

COUNTS = {
    "raw_in0": (16 * (SLABS // 2), 0), "raw_in1": (16 * (SLABS // 2), 0),
    "hi_ready": (SLABS, 0), "split_done": (SLABS, 2), "slab_used": (SLABS, 2),
    "ms_ready": (2, 0), "rs_ready": (2, 0), "y0_ready": (2, 0),
    "h_hi_ready": (2 * KD, KD), "h_ready": (2 * KD, KD),
    "x_new": (2 * KD, 2), "sq_ready": (2 * KD, KD), "sum_added": (2 * KD, KD),
    "sum_cleared": (2, 0),
    "chunk_out": (S_M, 0), "vt_ready": (14, 0), "v_ready": (14, 0),
    "s_ready": (16, 0), "s_used": (16, 0), "l_ready": (16, 0), "p_ready": (16, 0), "diag_ready": (16, 0),
    "t_ready": (16, 0), "pt_ready": (16, 0), "o_ready": (16, 0),
    "ya_hi_ready": (4, 0), "ya_ready": (4, 0),
    "z_ready": (16, 0), "zs_ready": (16, 0), "e_ready": (16, 0), "sp_ready": (16, 0),
    "sfx_ready": (16, 0), "lw_ready": (16, 0), "w_ready": (16, 0),
    "yb_mm": (4, 0), "yb_hi_ready": (4, 0), "yb_ready": (4, 0),
    "rx_ready": (4, 0), "rot_ready": (4, 0),
    "st_ready": (16, 0), "decay_ready": (16, 0), "ret_ready": (4, 1), "gated_ready": (4, 0),
    "var_used": (4, 0), "table_in": (16 * 12, 0), "swish_ready": (1, 0),
    "csq_ready": (4, 0), "var_ready": (4, 0),
    "cy0_ready": (4, 0), "yc_ready": (4, 0), "yc_hi_ready": (4, 0), "yc_split": (4, 0),
    "gate_scaled": (3 * KD, 3), "gate_ready": (3 * KD, 0), "ab_done": (KD, 0), "m_ready": (KD, 1),
    "m_hi_ready": (KD, 0), "m_split": (KD, 1),
    "u_ready": (KF, 1), "cv_ready": (KF, 0), "conv_done": (KF, 0), "g_scaled": (KF, 1),
    "gelu_ready": (KF, 0), "af_ready": (KF, 1),
    "af_hi_ready": (KF, 0), "af_split": (KF, 1),
    "dve_step": (DVE_STEPS, 0), "act_step": (ACT_STEPS, 0),
}
GRANTED = {"split_done": 2, "slab_used": 2, "x_new": 2, "gate_scaled": 3, "m_ready": 1,
           "u_ready": 1, "g_scaled": 1, "af_ready": 1, "m_split": 1, "af_split": 1, "ret_ready": 1}


def trunk_program(nc, x_t, vectors, rel_bias, onehot, mats, decay, cos_sin, w_qkv, w_gates,
                  w_proj, w_o, w_upgate, w_down, line_dram, out_t):
    with ExitStack() as ctx:
        def sb(stack, name, shape, dtype=F32):
            return stack.enter_context(nc.sbuf_tensor(name, shape, dtype))

        x = sb(ctx, "x", [P, KD, SEQ])
        h_hi = sb(ctx, "h_hi", [P, KD, SEQ], F32R)
        h_lo = sb(ctx, "h_lo", [P, KD, SEQ], F32R)
        raw = [sb(ctx, f"raw{p}", [P, SLAB_MAX]) for p in range(2)]
        w_hi = [sb(ctx, f"w_hi{p}", [P, SLAB_MAX], F32R) for p in range(2)]
        w_lo = [sb(ctx, f"w_lo{p}", [P, SLAB_MAX], F32R) for p in range(2)]
        with ExitStack() as z:
            cvv = sb(z, "cvv", [P, NT, 4 * P])
        table = sb(ctx, "table", [P, SLOTS, TABLE])
        decays = sb(ctx, "decays", [P, 4, SEQ])
        rope = sb(ctx, "rope", [P, 2, SEQ])
        consts = sb(ctx, "consts", [P, 7, P])
        vecs = sb(ctx, "vecs", [P, VECS])
        stat = sb(ctx, "stat", [P, 4, 4])
        eps = sb(ctx, "eps", [P, 1])
        ones, ones_model, tri, ident, rotate, centre, flip = (
            consts[:, i, :] for i in range(7))
        with ExitStack() as z:
            square = [sb(z, f"square{p}", [P, SEQ]) for p in range(2)]
            sumsq = sb(z, "sumsq", [P, SEQ])
            y0 = sb(z, "y0", [P, SEQ])
            rs = sb(z, "rs", [P, SEQ])
        with ExitStack() as z:
            cv = sb(z, "cv", [P, SEQ])
            af = sb(z, "af", [P, SEQ])
            u = sb(z, "u", [P, SEQ])
        with ExitStack() as z:
            vs = [sb(z, f"vs{p}", [P, SEQ]) for p in range(2)]
            with ExitStack() as y:
                diag = [sb(y, f"diag{p}", [P, P]) for p in range(2)]
            acc = [sb(z, f"acc{p}", [P, SEQ]) for p in range(2)]
        ctx.enter_context(nc.sbuf_tensor("scratch", [P, 5, SEQ], F32))

        def spare(stack, name, kib):
            sb(stack, name, [P, kib * 256])

        with ExitStack() as mix:
            ya_hi, ya_lo = (sb(mix, f"ya_{n}", [P, 2, SEQ], F32R) for n in ("hi", "lo"))
            with ExitStack() as z:
                aq = sb(z, "aq", [P, 6, SEQ])
                ak = sb(z, "ak", [P, 6, SEQ])
                av = sb(z, "av", [P, GROUPS, NT, SLOTS * HD])
                logits = [sb(z, f"logits{p}", [P, 6 * P]) for p in range(2)]
                probs_t = [sb(z, f"probs_t{p}", [P, BANDED]) for p in range(2)]
                sb(z, "spare54", [P, 12 * P - 2 * BANDED])
                bv = sb(z, "bv", [P, NT, 4 * P])
                bq = sb(z, "bq", [P, 4, SEQ])
                bk = sb(z, "bk", [P, 4, SEQ])
            with ExitStack() as z:
                zs = [sb(z, f"zs{p}", [P, SEQ]) for p in range(3)]
                ez = [sb(z, f"ez{p}", [P, SEQ]) for p in range(2)]
                sp_keep = [sb(z, f"sp_keep{p}", [P, SEQ]) for p in range(2)]
                wts = sb(z, "wts", [P, 10 * P])
            with ExitStack() as z:
                dcy = [sb(z, f"dcy{p}", [P, 10 * P]) for p in range(2)]
                og = [sb(z, f"og{p}", [P, SEQ]) for p in range(2)]
                cy = [sb(z, f"cy{p}", [P, SEQ]) for p in range(2)]
                spare(z, "spare26", 1)
                yb_hi, yb_lo = (sb(z, f"yb_{n}", [P, 4, SEQ], F32R) for n in ("hi", "lo"))
                with ExitStack() as y:
                    cq = sb(y, "cq", [P, 4, SEQ])
                    csq = sb(y, "csq", [P, SEQ])
                sg = [sb(z, f"sg{p}", [P, SEQ]) for p in range(3)]
                mt = [sb(z, f"mt{p}", [P, SEQ]) for p in range(2)]
                spare(z, "spare53", 3)
                yc_hi, yc_lo = (sb(z, f"yc_{n}", [P, 4, SEQ], F32R) for n in ("hi", "lo"))
                with ExitStack() as y:
                    ct = [sb(y, f"ct{p}", [P, SEQ]) for p in range(2)]
                    spare(y, "spare76", 4)
                    cg = sb(y, "cg", [P, 4, SEQ])
                m_lo = sb(z, "m_lo", [P, KD, SEQ], F32R)
            m_hi = sb(mix, "m_hi", [P, KD, SEQ], F32R)
        with ExitStack() as ffn:
            act_hi, act_lo = (sb(ffn, f"act_{n}", [P, KF, SEQ], F32R) for n in ("hi", "lo"))
        with ExitStack() as z:
            rel_ext = sb(z, "rel_ext", [REL_BUCKETS + 1, 12])
            one_hot = sb(z, "one_hot", [REL_BUCKETS + 1, LINE])
            lines = sb(z, "lines", [12, LINE])
        ctx.enter_context(nc.sbuf_tensor("layer_area", [P, 2 * KF * SEQ], F32))

        ps = ctx.enter_context(nc.psum_tensor("ps", [P, 8, SEQ], F32))

        sem = {name: ctx.enter_context(nc.semaphore(name)) for name in COUNTS}
        raw_in = [sem["raw_in0"], sem["raw_in1"]]
        const_in = ctx.enter_context(nc.semaphore("const_in"))
        late_in = ctx.enter_context(nc.semaphore("late_in"))
        x_in = [ctx.enter_context(nc.semaphore(f"x_in{q}")) for q in range(4)]
        memset_done = ctx.enter_context(nc.semaphore("memset_done"))
        line_mm = ctx.enter_context(nc.semaphore("line_mm"))
        line_copied = ctx.enter_context(nc.semaphore("line_copied"))
        line_out = ctx.enter_context(nc.semaphore("line_out"))
        out_ready = ctx.enter_context(nc.semaphore("out_ready"))
        out_done = ctx.enter_context(nc.semaphore("out_done"))
        block = ctx.enter_context(nc.Block())

        def nth(name, L, k):
            per_layer, before = COUNTS[name]
            return L * per_layer + (k + before)

        def grant(eng, *names):
            for name in names:
                eng.sem_inc(sem[name], GRANTED[name])

        def bank(b, a=0, z=SEQ):
            return ps[:, b, a:z]

        class Steps:

            def __init__(self, name):
                self.name, self.k, self.turn = name, 0, 0

            def next(self, L):
                self.k += 1
                return nth(self.name, L, self.turn + self.k)

            def enter(self, i, per_turn):
                self.turn, self.first, self.per_turn = i * per_turn, self.k, per_turn

            def leave(self, turns):
                assert self.k - self.first == self.per_turn, (self.name, self.k - self.first)
                self.k, self.turn = self.first + turns * self.per_turn, 0

            def end(self):
                assert self.k == COUNTS[self.name][0], (self.name, self.k)

        def blocks_before(i):
            return KD + 11 * i // 2

        def ended(i):
            return range(blocks_before(i - 1) // KD if i else 0, blocks_before(i) // KD)

        def elements(s):
            if S_M <= s < S_O:
                return (K_PROJ if (s - S_M) % 4 == 3 else KD) * P
            return KHALF * P if s >= S_D else KD * P

        @block.sync
        def _(sp):
            for dst, src in ((rel_ext[0:REL_BUCKETS, :], rel_bias), (one_hot[:], onehot),
                             (vecs[:], vectors), (consts[:], mats)):
                sp.dma_start(dst, src).then_inc(const_in, 16)
            for q in range(4):
                sp.dma_start(x[:, 2 * q:2 * q + 2, :], x_t[:, 2 * q:2 * q + 2, :]).then_inc(x_in[q], 16)
            sp.dma_start(decays[:], decay).then_inc(late_in, 16)
            sp.dma_start(rope[:], cos_sin).then_inc(late_in, 16)

            def load(L, s, p, src, n):
                sp.wait_ge(sem["split_done"], nth("split_done", L, s - 1))
                sp.dma_start(raw[p][:, 0:n], src).then_inc(raw_in[p], 16)

            with sp.Fori(0, DEPTH) as L:
                with sp.Fori(0, 2) as i:
                    for p in range(2):
                        load(L, 2 * i + p, p, w_qkv[L * S_M + 2 * i + p], KD * P)
                sp.wait_ge(line_out, 16)
                sp.wait_ge(sem["ret_ready"], nth("ret_ready", L, 0))
                for h in range(SLOTS):
                    for g, at, step, n in ((0, 0, 4, EXT), (1, LINE1, 1, P), (2, LINE1 + LINE2, 1, P)):
                        to = 0 if g == 0 else EXT + (g - 1) * P
                        src = bass.AP(tensor=line_dram.tensor, offset=(SLOTS * g + h) * LINE + at,
                                      ap=[[step, P], [1, n]])
                        sp.dma_start(table[:, h, to:to + n], src).then_inc(sem["table_in"], 16)
                with sp.Fori(2, S_M // 2) as i:
                    for p in range(2):
                        load(L, 2 * i + p, p, w_qkv[L * S_M + 2 * i + p], KD * P)
                with sp.Fori(0, KD) as j:
                    for b in range(3):
                        load(L, 4 * j + (S_M + b), b % 2, w_gates[L * (3 * KD) + 3 * j + b], KD * P)
                    load(L, 4 * j + (S_M + 3), 1, w_proj[L * KD + j], K_PROJ * P)
                for first, src, n, per in ((S_O, w_o, KD // 2, KD * P), (S_F, w_upgate, KF, KD * P),
                                           (S_D, w_down, KD, KHALF * P)):
                    with sp.Fori(0, n) as i:
                        for p in range(2):
                            load(L, 2 * i + (first + p), p, src[L * (2 * n) + 2 * i + p], per)

            for p in range(2):
                load(DEPTH, p, p, w_qkv[p], KD * P)
            for k in range(KD):
                sp.wait_ge(out_ready, k + 1)
                sp.dma_start(out_t[:, k, :], x[:, k, :]).then_inc(out_done, 16)
            sp.wait_ge(out_done, 16 * KD)

        @block.gpsimd
        def _(pool):
            pool.wait_ge(line_copied, 3)
            pool.dma_start(line_dram, lines[:]).then_inc(line_out, 16)

        @block.tensor
        def _(pe):
            grant(pe, "slab_used", "ret_ready")

            def slab(L, s, p, products, split=None, done=None):
                pe.wait_ge(sem["split_done"], nth("split_done", L, s + 1))
                at = 0
                for b, blocks, first, hi, lo, starts, ends in products:
                    for k in range(blocks):
                        w = slice((at + k) * P, (at + k + 1) * P)
                        if split and b == products[-1][0]:
                            pe.wait_ge(sem[split[0]], nth(split[0], L, split[1] + k + 1))
                        for n, (a, y) in enumerate(((w_hi[p], hi), (w_hi[p], lo), (w_lo[p], hi))):
                            mm = pe.matmul(bank(b), a[:, w], y[:, first + k, :],
                                           start=starts and k == 0 and n == 0,
                                           stop=ends and k == blocks - 1 and n == 2)
                    at += blocks
                    if done and b == products[-2][0]:
                        mm.then_inc(sem[done], 1)
                mm.then_inc(sem["slab_used"], 1)

            def from_h(b):
                return [(b, KD, 0, h_hi, h_lo, True, True)]

            def mean_square(L, n):
                pe.wait_ge(sem["sum_added"], nth("sum_added", L, KD * (n - 1)))
                pe.matmul(bank(6), ones_model, sumsq[:], start=True, stop=True)\
                  .then_inc(sem["ms_ready"], 1)

            def row_block(p, b, k):
                w = slice(k * P, (k + 1) * P)
                for n, (a, y) in enumerate(((w_hi[p], h_hi), (w_hi[p], h_lo), (w_lo[p], h_hi))):
                    mm = pe.matmul(bank(b), a[:, w], y[:, k, :], start=k == 0 and n == 0,
                                   stop=k == KD - 1 and n == 2)
                return mm

            def chunk_block(L, first, c, k, v_chunks, v_before, v_bank, by=ident):
                s = first + c
                if k == 0:
                    pe.wait_ge(sem["split_done"], nth("split_done", L, s + 1))
                    if s >= 2:
                        pe.wait_ge(sem["chunk_out"], nth("chunk_out", L, s - 1))
                if s == 0:
                    pe.wait_ge(sem["h_ready"], nth("h_ready", L, k + 1 - KD))
                mm = row_block(s % 2, s % 2, k)
                if k < KD - 1:
                    return
                mm.then_inc(sem["slab_used"], 1)
                if 1 <= c <= v_chunks:
                    v = v_before + c - 1
                    pe.wait_ge(sem["chunk_out"], nth("chunk_out", L, s))
                    if v >= 1:
                        pe.wait_ge(sem["v_ready"], nth("v_ready", L, v))
                    for t in range(NT):
                        mm = pe.matmul(bank(v_bank, t * P, (t + 1) * P),
                                       vs[v % 2][:, t * P:(t + 1) * P], by, start=True, stop=True)
                    mm.then_inc(sem["vt_ready"], 1)

            def first_section(L):
                for c in range(V_A + 2):
                    for k in range(KD):
                        chunk_block(L, 0, c, k, V_A, 0, 2)
                    if c == 0:
                        mean_square(L, 1)
                with pe.Fori(0, (A_CHUNKS - V_A - 2) // 2) as i:
                    for p in range(2):
                        s = 2 * i + (V_A + 2 + p)
                        pe.wait_ge(sem["chunk_out"], nth("chunk_out", L, s - 1))
                        slab(L, s, p, from_h(p))
            def b_blocks(L, start, n):
                for a in range(start, start + n):
                    chunk_block(L, A_CHUNKS, a // KD, a % KD, V_B, V_A, 4)

            def c_blocks(L, start, n):
                for a in range(start, start + n):
                    chunk_block(L, A_CHUNKS + B_CHUNKS, a // KD, a % KD, V_C, V_A + V_B, 7, centre)

            def gate_blocks(L, start, n):
                for a in range(start, start + n):
                    b, k = divmod(a, KD)
                    if k == 0:
                        pe.wait_ge(sem["split_done"], nth("split_done", L, S_M + b + 1))
                        pe.wait_ge(sem["chunk_out"], nth("chunk_out", L, S_M - 1))
                    mm = row_block(b % 2, GATE_BANKS[b], k)
                    if k == KD - 1:
                        mm.then_inc(sem["slab_used"], 1)

            def windows(L):
                def scores(i):
                    r, h = divmod(i, SLOTS)
                    if i >= 1:
                        pe.wait_ge(sem["s_used"], nth("s_used", L, i))
                    rows = slice(HD * (h % 2), HD * (h % 2) + HD)
                    for g in range(GROUPS):
                        q = aq[rows, 2 * g + h // 2, r * P:(r + 1) * P]
                        k = ak[rows, 2 * g + h // 2, :]
                        if g == 0:
                            mm = pe.matmul(bank(2), q, k, start=True, stop=True)
                        else:
                            mm = pe.matmul(bank(3, (g - 1) * P, g * P), q,
                                           k[:, r * P:(r + 1) * P], start=True, stop=True)
                    mm.then_inc(sem["s_ready"], 1)

                b_blocks(L, 0, KD // 2)
                pe.wait_ge(sem["chunk_out"], nth("chunk_out", L, A_CHUNKS))
                pe.wait_ge(sem["v_ready"], nth("v_ready", L, V_A))
                scores(0)
                b_blocks(L, KD // 2, KD // 2)
                scores(1)
                for i in range(16):
                    r, h = divmod(i, SLOTS)
                    a = blocks_before(i)
                    pe.wait_ge(sem["diag_ready"], nth("diag_ready", L, i + 1))
                    if i >= 1:
                        pe.wait_ge(sem["pt_ready"], nth("pt_ready", L, i))
                    for kb, first, last, at in BANDS:
                        mm = pe.matmul(bank(6, at, at + last - first),
                                       logits[i % 2][:, kb * P:(kb + 1) * P],
                                       diag[i % 2][:, first:last], start=True, stop=True)
                    mm.then_inc(sem["t_ready"], 1)
                    b_blocks(L, a, 2)
                    if i + 2 < 16:
                        scores(i + 2)
                    b_blocks(L, a + 2, 2)
                    pe.wait_ge(sem["pt_ready"], nth("pt_ready", L, i + 1))
                    if h == 0 and r >= 1:
                        pe.wait_ge(sem["ya_ready"], nth("ya_ready", L, r))
                    out = h // 2 * P
                    for kb, first, last, at in BANDS:
                        g, t = (0, kb) if kb < 4 else (kb - 3, r)
                        mm = pe.matmul(ps[HD * (h % 2):HD * (h % 2) + HD, 5, out + first:out + last],
                                       av[:, g, t, h * HD:(h + 1) * HD],
                                       probs_t[i % 2][:, at:at + last - first], start=kb == 4,
                                       stop=True, skip_group_check=True)
                    mm.then_inc(sem["o_ready"], 1)
                    b_blocks(L, a + 4, blocks_before(i + 1) - a - 4)

            def stick_breaking(L):
                turns = [(h, n) for h in range(4) for n in (3, 2, 1, 0)]

                def scores(t):
                    h, n = turns[t]
                    if t >= 2:
                        pe.wait_ge(sem["zs_ready"], nth("zs_ready", L, t - 1))
                    pe.matmul(bank(2 + t % 2, n * P), bk[:, h, n * P:(n + 1) * P], bq[:, h, n * P:],
                              start=True, stop=True).then_inc(sem["z_ready"], 1)

                def output(h):
                    pe.wait_ge(sem["w_ready"], nth("w_ready", L, 4 * h + 4))
                    if h >= 1:
                        pe.wait_ge(sem["yb_ready"], nth("yb_ready", L, h))
                    for n in range(4):
                        at = (4 - n) * (3 - n) // 2 * P
                        mm = pe.matmul(bank(6, n * P), bv[:, n, h * P:(h + 1) * P],
                                       wts[:, at:at + (4 - n) * P], start=n == 0, stop=True,
                                       skip_group_check=True)
                    mm.then_inc(sem["yb_mm"], 1)

                c_blocks(L, 0, KD // 2)
                pe.wait_ge(sem["ya_ready"], nth("ya_ready", L, 4))
                pe.wait_ge(sem["chunk_out"], nth("chunk_out", L, A_CHUNKS + B_CHUNKS))
                pe.wait_ge(sem["v_ready"], nth("v_ready", L, V_A + V_B))
                scores(0)
                scores(1)
                c_blocks(L, KD // 2, KD // 2)
                for t, (h, n) in enumerate(turns):
                    a = blocks_before(t)
                    c_blocks(L, a, 3)
                    pe.wait_ge(sem["sp_ready"], nth("sp_ready", L, t + 1))
                    if t >= 2:
                        pe.wait_ge(sem["lw_ready"], nth("lw_ready", L, t - 1))
                    mm = pe.matmul(bank(4 + t % 2, n * P), tri, sp_keep[t % 2][:, n * P:],
                                   start=True, stop=True)
                    if n < 3:
                        mm = pe.matmul(bank(4 + t % 2, (n + 1) * P), ones,
                                       acc[(n + 1) % 2][:, (n + 1) * P:], start=False, stop=True,
                                       skip_group_check=True)
                    mm.then_inc(sem["sfx_ready"], 1)
                    if t + 2 < 16:
                        scores(t + 2)
                    if n == 3 and h >= 1:
                        output(h - 1)
                    c_blocks(L, a + 3, blocks_before(t + 1) - a - 3)
                gate_blocks(L, 0, 3)
                output(3)
                gate_blocks(L, 3, 2)
                pe.wait_ge(sem["yb_ready"], nth("yb_ready", L, 4))
                pe.wait_ge(sem["chunk_out"], nth("chunk_out", L, S_M))
                pe.wait_ge(sem["v_ready"], nth("v_ready", L, V_A + V_B + V_C))

            def retention(L):
                for c in range(4):
                    if c >= 2:
                        pe.wait_ge(sem["rot_ready"], nth("rot_ready", L, c - 1))
                    pe.matmul(bank(2 + c % 2), rotate, cq[:, c, :], start=True, stop=True)\
                      .then_inc(sem["rx_ready"], 1)
                    gate_blocks(L, 5 + 2 * c, 2)
                pe.wait_ge(sem["rot_ready"], nth("rot_ready", L, 4))

                def scores(h):
                    rows = slice(HD * (h % 2), HD * (h % 2) + HD)
                    for n in range(4):
                        if 4 * h + n >= 2:
                            pe.wait_ge(sem["decay_ready"], nth("decay_ready", L, 4 * h + n - 1))
                        pe.matmul(bank(2 + n % 2, n * P), cq[rows, 2 + h // 2, n * P:(n + 1) * P],
                                  cq[rows, h // 2, n * P:], start=True, stop=True)\
                          .then_inc(sem["st_ready"], 1)

                def mix(h):
                    pe.wait_ge(sem["decay_ready"], nth("decay_ready", L, 4 * h + 4))
                    if h >= 2:
                        pe.wait_ge(sem["gated_ready"], nth("gated_ready", L, h - 1))
                        pe.wait_ge(sem["csq_ready"], nth("csq_ready", L, h - 1))
                    for n in range(4):
                        at = (4 - n) * (3 - n) // 2 * P
                        mm = pe.matmul(bank(6 + h % 2, n * P), cvv[:, n, h * P:(h + 1) * P],
                                       dcy[h % 2][:, at:at + (4 - n) * P], start=n == 0, stop=True,
                                       skip_group_check=True)
                    mm.then_inc(sem["ret_ready"], 1)

                def variance(h):
                    pe.wait_ge(sem["csq_ready"], nth("csq_ready", L, h + 1))
                    if h >= 1:
                        pe.wait_ge(sem["var_used"], nth("var_used", L, h))
                    pe.matmul(bank(1), ones_model, csq[:], start=True, stop=True)\
                      .then_inc(sem["var_ready"], 1)

                scores(0)
                for h in range(4):
                    mix(h)
                    if h < 3:
                        scores(h + 1)
                    gate_blocks(L, 13 + h, 1 if h < 3 else 3)
                    variance(h)
                gate_blocks(L, 19, 5)

            pe.wait_ge(const_in, 16 * 4)
            pe.wait_ge(memset_done, 2)
            for n in range(3):
                pe.matmul(ps[0:12, n, :], rel_ext[:, :], one_hot[:, n * SEQ:(n + 1) * SEQ],
                          start=True, stop=True).then_inc(line_mm, 1)
            with pe.Fori(0, DEPTH) as L:
                first_section(L)
                windows(L)
                stick_breaking(L)
                retention(L)

                def gate(L, j, b):
                    pe.wait_ge(sem["gate_scaled"], nth("gate_scaled", L, 3 * j + (b - 2)))
                    slab(L, 4 * j + (S_M + b), b % 2, from_h(GATE_BANKS[b]))

                def branches(L, j, split=None):
                    pe.wait_ge(sem["m_ready"], nth("m_ready", L, j))
                    slab(L, 4 * j + (S_M + 3), 1,
                         [(2, 2, 0, ya_hi, ya_lo, True, True), (3, 4, 0, yb_hi, yb_lo, True, True),
                          (1, 4, 0, yc_hi, yc_lo, True, True)], split, "ab_done")

                pe.wait_ge(sem["var_used"], nth("var_used", L, 4))
                branches(L, 0, ("yc_split", 0))
                with pe.Fori(1, KD) as j:
                    for b in range(3):
                        gate(L, j, b)
                    branches(L, j)
                with pe.Fori(0, KD // 2) as i:
                    for p in range(2):
                        pe.wait_ge(sem["x_new"], nth("x_new", L, 2 * i + (p - 1)))
                        slab(L, 2 * i + (S_O + p), p, [(p, KD, 0, m_hi, m_lo, True, True)],
                             ("m_split", 0))
                slab(L, S_F, 0, from_h(0), ("h_ready", 0))
                mean_square(L, 2)
                slab(L, S_F + 1, 1, from_h(1))
                with pe.Fori(1, KF) as c:
                    pe.wait_ge(sem["u_ready"], nth("u_ready", L, c))
                    slab(L, 2 * c + S_F, 0, from_h(0))
                    pe.wait_ge(sem["g_scaled"], nth("g_scaled", L, c))
                    slab(L, 2 * c + (S_F + 1), 1, from_h(1))
                with pe.Fori(0, KD // 2) as i:
                    for b in range(2):
                        for p in range(2):
                            pe.wait_ge(sem["af_split"], nth("af_split", L, (p + 1) * KHALF))
                            if p == 0:
                                pe.wait_ge(sem["u_ready"], nth("u_ready", L, KF))
                                pe.wait_ge(sem["x_new"], nth("x_new", L, 2 * i + (KD + b - 1)))
                            slab(L, 4 * i + (S_D + 2 * b + p), p,
                                 [(b, KHALF, p * KHALF, act_hi, act_lo, p == 0, p == 1)])
            mean_square(DEPTH, 1)

        @block.scalar
        def _(act):
            def high(L, s, p, turn, n):
                act.wait_ge(sem[f"raw_in{p}"], nth(f"raw_in{p}", L, 16 * turn))
                act.wait_ge(sem["slab_used"], nth("slab_used", L, s - 1))
                act.activation(w_hi[p][:, 0:n], raw[p][:, 0:n], ACT.Copy).then_inc(sem["hi_ready"], 1)

            def high_at(L, s):
                high(L, s, s % 2, s // 2 + 1, elements(s))

            def norm(L, n, steps):
                act.wait_ge(sem["ms_ready"], nth("ms_ready", L, n))
                act.activation(y0[:], bank(6), ACT.Ln, bias=eps[:]).then_inc(sem["act_step"], 1)
                act.wait_ge(sem["act_step"], steps.next(L))
                act.activation(y0[:], y0[:], ACT.Exp, scale=-0.5).then_inc(sem["y0_ready"], 1)

            def turned(L, s, store=None, v=None, v_bank=None):
                high_at(L, s + 2)
                if v is not None:
                    act.wait_ge(sem["vt_ready"], nth("vt_ready", L, v + 1))
                    act.activation(store, bank(v_bank).rearrange("p (t n) -> p t n", t=NT), ACT.Copy)\
                       .then_inc(sem["v_ready"], 1)

            def turned_b(L, c):
                if 1 <= c <= V_B:
                    turned(L, A_CHUNKS + c, bv[:, :, (c - 1) * P:c * P], V_A + c - 1, 4)
                else:
                    turned(L, A_CHUNKS + c)

            def turned_c(L, c):
                s = A_CHUNKS + B_CHUNKS + c
                if 1 <= c <= V_C:
                    turned(L, s, cvv[:, :, (c - 1) * P:c * P], V_A + V_B + c - 1, 7)
                else:
                    turned(L, s)

            def windows(L):
                def probs(i):
                    act.wait_ge(sem["l_ready"], nth("l_ready", L, i + 1))
                    act.activation(logits[i % 2][:], logits[i % 2][:], ACT.Exp,
                                   bias=stat[:, 1, i % 4:i % 4 + 1],
                                   accum_out=stat[:, 2, i % 4:i % 4 + 1]).then_inc(sem["p_ready"], 1)

                def y_high(r):
                    act.wait_ge(sem["o_ready"], nth("o_ready", L, SLOTS * (r + 1)))
                    act.activation(ya_hi[:, :, r::4],
                                   ps[:, 5, 0:2 * P].rearrange("p (c u) -> p c u", c=2), ACT.Copy)\
                       .then_inc(sem["ya_hi_ready"], 1)

                probs(0)
                for i in range(16):
                    if i + 1 < 16:
                        probs(i + 1)
                    act.wait_ge(sem["t_ready"], nth("t_ready", L, i + 1))
                    if i >= 2:
                        act.wait_ge(sem["o_ready"], nth("o_ready", L, i - 1))
                    act.activation(probs_t[i % 2][:], bank(6, 0, BANDED), ACT.Copy)\
                       .then_inc(sem["pt_ready"], 1)
                    if i % SLOTS == 0 and i:
                        y_high(i // SLOTS - 1)
                    for c in ended(i):
                        turned_b(L, c)
                turned_b(L, B_CHUNKS - 1)
                y_high(3)

            def stick_breaking(L, steps):
                turns = [(h, n) for h in range(4) for n in (3, 2, 1, 0)]

                def log_part(t):
                    n = turns[t][1]
                    e, z = ez[t % 2][:, n * P:], zs[t % 3][:, n * P:]
                    act.wait_ge(sem["zs_ready"], nth("zs_ready", L, t + 1))
                    act.activation(e, z, ACT.Abs).then_inc(sem["act_step"], 1)
                    act.wait_ge(sem["act_step"], steps.next(L))
                    act.activation(e, e, ACT.Exp, scale=-1.0).then_inc(sem["act_step"], 1)
                    act.wait_ge(sem["act_step"], steps.next(L))
                    act.activation(e, e, ACT.Ln, bias=1.0).then_inc(sem["e_ready"], 1)

                def weights(t):
                    h, n = turns[t]
                    at = (4 - n) * (3 - n) // 2 * P
                    act.wait_ge(sem["lw_ready"], nth("lw_ready", L, t + 1))
                    if n == 3 and h >= 1:
                        act.wait_ge(sem["yb_mm"], nth("yb_mm", L, h))
                    act.activation(wts[:, at:at + (4 - n) * P], zs[t % 3][:, n * P:], ACT.Exp)\
                       .then_inc(sem["w_ready"], 1)

                def y_high(h):
                    act.wait_ge(sem["yb_mm"], nth("yb_mm", L, h + 1))
                    act.activation(yb_hi[:, h, :], bank(6), ACT.Copy)\
                       .then_inc(sem["yb_hi_ready"], 1)

                for t in range(16):
                    log_part(t)
                    if t >= 1:
                        weights(t - 1)
                    if t % 4 == 1 and t > 4:
                        y_high(t // 4 - 1)
                    for c in ended(t):
                        turned_c(L, c)
                weights(15)
                turned_c(L, C_CHUNKS - 1)
                y_high(3)

            def retention(L, steps):
                def square(h):
                    act.wait_ge(sem["ret_ready"], nth("ret_ready", L, h + 1))
                    act.activation(csq[:], bank(6 + h % 2), ACT.Square).then_inc(sem["csq_ready"], 1)

                def start_root(h):
                    act.wait_ge(sem["var_ready"], nth("var_ready", L, h + 1))
                    if h >= 2:
                        act.wait_ge(sem["yc_ready"], nth("yc_ready", L, h - 1))
                    y = cy[h % 2]
                    act.activation(y[:], bank(1), ACT.Ln, bias=eps[:], scale=PER_HEAD)\
                       .then_inc(sem["act_step"], 1)
                    act.wait_ge(sem["act_step"], steps.next(L))
                    act.activation(y[:], y[:], ACT.Exp, scale=-0.5).then_inc(sem["cy0_ready"], 1)

                def y_high(h):
                    act.wait_ge(sem["yc_ready"], nth("yc_ready", L, h + 1))
                    act.activation(yc_hi[:, h, :], ct[h % 2][:], ACT.Copy).then_inc(sem["yc_hi_ready"], 1)

                high_at(L, S_M + 2)
                for h in range(4):
                    square(h)
                    start_root(h)
                    if h >= 1:
                        y_high(h - 1)
                    if h == 2:
                        high_at(L, S_M + 3)
                y_high(3)

            def of_block(L, j, p, n, scales, slab_high):
                act.wait_ge(sem["x_new"], nth("x_new", L, n))
                act.activation(h_hi[:, j, :], x[:, j, :], ACT.Copy, scale=vecs[:, bass.ds(scales, 1)])\
                   .then_inc(sem["h_hi_ready"], 1)
                high(*slab_high)
                act.activation(square[p][:], x[:, j, :], ACT.Square).then_inc(sem["sq_ready"], 1)

            act.preload_act_table_set(NLE)
            act.wait_ge(const_in, 16 * 4)
            for k in range(KD):
                act.wait_ge(x_in[k // 2], 16)
                act.activation(h_hi[:, k, :], x[:, k, :], ACT.Copy, scale=vecs[:, V_NORM + k:V_NORM + k + 1])\
                   .then_inc(sem["h_hi_ready"], 1)
                if k >= 2:
                    act.wait_ge(sem["sum_added"], k - 1)
                act.activation(square[k % 2][:], x[:, k, :], ACT.Square).then_inc(sem["sq_ready"], 1)
                if k in (5, 7):
                    high_at(0, (k - 5) // 2)
            act.wait_ge(memset_done, 2)

            with act.Fori(0, DEPTH) as L:
                steps = Steps("act_step")
                norm(L, 1, steps)
                for c in range(A_CHUNKS):
                    if 1 <= c <= V_A:
                        turned(L, c, av[:, (c - 1) // 2, :, (c - 1) % 2 * P:((c - 1) % 2 + 1) * P], c - 1, 2)
                    else:
                        turned(L, c)
                windows(L)
                stick_breaking(L, steps)
                act.wait_ge(sem["chunk_out"], nth("chunk_out", L, S_M))
                act.activation(cg[:], cg[:], ACT.Silu).then_inc(sem["swish_ready"], 1)
                act.preload_act_table_set(NLE)
                retention(L, steps)
                def gates(j, first):
                    for b in range(4):
                        s = 4 * j + (S_M + b)
                        if not (first and b < 2):
                            high(L, s + 2, b % 2, 2 * j + (S_M // 2 + b // 2 + 2),
                                 (K_PROJ if b == 1 else KD) * P)
                        if b < 3:
                            act.wait_ge(sem["gate_scaled"], nth("gate_scaled", L, 3 * j + b + 1))
                            act.activation(sg[b][:], sg[b][:], ACT.Sigmoid,
                                           bias=vecs[:, bass.ds(V_BGATE + L * (3 * KD) + 3 * j + b, 1)])\
                               .then_inc(sem["gate_ready"], 1)
                    act.wait_ge(sem["m_ready"], nth("m_ready", L, j + 1))
                    act.activation(m_hi[:, j, :], mt[0][:], ACT.Copy).then_inc(sem["m_hi_ready"], 1)

                gates(0, True)
                with act.Fori(1, KD) as j:
                    gates(j, False)
                act.preload_act_table_set(NLE)
                with act.Fori(0, KD // 2) as i:
                    for p in range(2):
                        of_block(L, 2 * i + p, p, 2 * i + (p + 1), V_NORM + L * (2 * KD) + 2 * i + (KD + p),
                                 (L, 2 * i + (S_O + p + 2), p, i + (S_O // 2 + 2), KD * P))
                norm(L, 2, steps)

                def ffn_block(c, n, turn):
                    high(L, 2 * c + (S_F + 2), 0, turn, n)
                    act.wait_ge(sem["u_ready"], nth("u_ready", L, c + 1))
                    act.wait_ge(sem["af_ready"], nth("af_ready", L, c))
                    at = V_CONV + L * (4 * KF) + 4 * c
                    act.activation(cv[:], u[:], ACT.Identity, bias=vecs[:, bass.ds(at + 3, 1)],
                                   scale=vecs[:, bass.ds(at + 2, 1)]).then_inc(sem["cv_ready"], 1)
                    high(L, 2 * c + (S_F + 3), 1, turn, n)
                    act.wait_ge(sem["conv_done"], nth("conv_done", L, c + 1))
                    act.activation(cv[:], cv[:], ACT.Gelu_apprx_tanh).then_inc(sem["gelu_ready"], 1)
                    act.wait_ge(sem["af_ready"], nth("af_ready", L, c + 1))
                    act.activation(act_hi[:, c, :], af[:], ACT.Copy).then_inc(sem["af_hi_ready"], 1)

                act.preload_act_table(ACT.Gelu_apprx_tanh)
                with act.Fori(0, KF - 1) as c:
                    ffn_block(c, KD * P, c + (S_F // 2 + 2))
                ffn_block(KF - 1, KHALF * P, KF - 1 + S_F // 2 + 2)

                act.preload_act_table_set(NLE)

                def down_pair(i, last):
                    for b in range(2):
                        turn = 2 * i + (S_D // 2 + b + 2)
                        n = (KD if last and b == 1 else KHALF) * P
                        high(L, 4 * i + (S_D + 2 * b + 2), 0, turn, n)
                        of_block(L, 2 * i + b, b, 2 * i + (KD + b + 1),
                                 V_NORM + L * (2 * KD) + 2 * i + (2 * KD + b),
                                 (L, 4 * i + (S_D + 2 * b + 3), 1, turn, n))

                with act.Fori(0, KD // 2 - 1) as i:
                    down_pair(i, False)
                down_pair(KD // 2 - 1, True)
                steps.end()
            act.preload_act_table_set(NLE)
            steps = Steps("act_step")
            norm(DEPTH, 1, steps)

        @block.vector
        def _(dve):
            grant(dve, "split_done", "x_new", "m_ready", "u_ready", "g_scaled", "gate_scaled",
                  "af_ready", "m_split", "af_split")

            def low(L, s, p, n):
                dve.wait_ge(sem["hi_ready"], nth("hi_ready", L, s + 1))
                dve.tensor_tensor(w_lo[p][:, 0:n], raw[p][:, 0:n], w_hi[p][:, 0:n].bitcast(F32),
                                  ALU.subtract).then_inc(sem["split_done"], 1)

            def low_at(L, s):
                low(L, s, s % 2, elements(s))

            def root(L, n, steps):
                dve.wait_ge(sem["y0_ready"], nth("y0_ready", L, n))
                dve.scalar_tensor_tensor(rs[:], bank(6), EPS, y0[:], ALU.add, ALU.mult)\
                   .then_inc(sem["dve_step"], 1)
                dve.wait_ge(sem["dve_step"], steps.next(L))
                dve.scalar_tensor_tensor(rs[:], rs[:], -0.5, y0[:], ALU.mult, ALU.mult)\
                   .then_inc(sem["dve_step"], 1)
                dve.wait_ge(sem["dve_step"], steps.next(L))
                dve.scalar_tensor_tensor(rs[:], rs[:], 1.5, y0[:], ALU.add, ALU.mult)\
                   .then_inc(sem["rs_ready"], 1)

            def by_class(t):
                return t.rearrange("p (u r) -> p r u", r=4)

            def take(L, s, dst, order=0, scale=1.0, v=None):
                dve.wait_ge(sem["slab_used"], nth("slab_used", L, s + 1))
                if v is not None and v >= 2:
                    dve.wait_ge(sem["vt_ready"], nth("vt_ready", L, v - 1))
                src, by = bank(s % 2), rs[:]
                if order:
                    dst = dst.rearrange("p (r u) -> p r u", r=4)[:, :, ::order]
                    src, by = by_class(src), by_class(by)
                dve.scalar_tensor_tensor(dst, src, scale, by, ALU.mult, ALU.mult)\
                   .then_inc(sem["chunk_out"], 1)
                low_at(L, s + 2)

            def take_b(L, c):
                if c < V_B:
                    take(L, A_CHUNKS + c, vs[(V_A + c) % 2][:], v=V_A + c)
                else:
                    take(L, A_CHUNKS + c, bq[:, c - 4, :] if c < 8 else bk[:, c - 8, :],
                         scale=SB_SCALE if c < 8 else 1.0)

            def take_c(L, c):
                s = A_CHUNKS + B_CHUNKS + c
                if c < V_C:
                    take(L, s, vs[(V_A + V_B + c) % 2][:], v=V_A + V_B + c)
                elif c < 8:
                    take(L, s, cq[:, c - 4, :], scale=1.0 if c < 6 else HD ** -0.5)
                else:
                    take(L, s, cg[:, c - 8, :])

            def windows(L, steps):
                def biased(i):
                    r, h = divmod(i, SLOTS)
                    dve.wait_ge(sem["s_ready"], nth("s_ready", L, i + 1))
                    if i >= 2:
                        dve.wait_ge(sem["t_ready"], nth("t_ready", L, i - 1))
                    to = logits[i % 2]
                    dve.tensor_tensor(to[:, 0:SEQ], bank(2), table[:, h, 3 - r:3 - r + SEQ], ALU.add)\
                       .then_inc(sem["dve_step"], 1)
                    dve.wait_ge(sem["dve_step"], steps.next(L))
                    dve.tensor_tensor(to[:, SEQ:6 * P], bank(3, 0, 2 * P), table[:, h, EXT:TABLE],
                                      ALU.add).then_inc(sem["s_used"], 1)
                    dve.wait_ge(sem["s_used"], nth("s_used", L, i + 1))

                def maximum(i):
                    a, to = i % 4, logits[i % 2]
                    dve.reduce_max(stat[:, 0, a:a + 1], to[:], AX_X).then_inc(sem["dve_step"], 1)
                    dve.wait_ge(sem["dve_step"], steps.next(L))
                    dve.tensor_scalar(stat[:, 1, a:a + 1], stat[:, 0, a:a + 1], -1.0, None, ALU.mult)\
                       .then_inc(sem["l_ready"], 1)

                def scaled_flip(i):
                    a = i % 4
                    dve.wait_ge(sem["p_ready"], nth("p_ready", L, i + 1))
                    dve.reciprocal(stat[:, 3, a:a + 1], stat[:, 2, a:a + 1]).then_inc(sem["dve_step"], 1)
                    dve.wait_ge(sem["dve_step"], steps.next(L))
                    if i >= 2:
                        dve.wait_ge(sem["t_ready"], nth("t_ready", L, i - 1))
                    dve.tensor_scalar(diag[i % 2][:], flip, stat[:, 3, a:a + 1], None, ALU.mult)\
                       .then_inc(sem["diag_ready"], 1)

                def y_low(r):
                    dve.wait_ge(sem["ya_hi_ready"], nth("ya_hi_ready", L, r + 1))
                    dve.tensor_tensor(ya_lo[:, :, r::4], ps[:, 5, 0:2 * P].rearrange("p (c u) -> p c u", c=2),
                                      ya_hi[:, :, r::4].bitcast(F32), ALU.subtract)\
                       .then_inc(sem["ya_ready"], 1)

                dve.wait_ge(sem["table_in"], nth("table_in", L, 16 * 12))
                biased(0)
                maximum(0)
                for i in range(16):
                    scaled_flip(i)
                    if i + 1 < 16:
                        biased(i + 1)
                        maximum(i + 1)
                    if i % SLOTS == 0 and i:
                        y_low(i // SLOTS - 1)
                    for c in ended(i):
                        take_b(L, c)
                take_b(L, B_CHUNKS - 1)
                y_low(3)

            def stick_breaking(L, steps):
                turns = [(h, n) for h in range(4) for n in (3, 2, 1, 0)]

                def scaled(t):
                    n = turns[t][1]
                    dve.wait_ge(sem["z_ready"], nth("z_ready", L, t + 1))
                    if t >= 3:
                        dve.wait_ge(sem["w_ready"], nth("w_ready", L, t - 2))
                    z, b = zs[t % 3], 2 + t % 2
                    if n < 3:
                        dve.tensor_copy(z[:, (n + 1) * P:], bank(b, (n + 1) * P))
                    dve.scalar_tensor_tensor(z[:, n * P:(n + 1) * P], tri, MASKED,
                                             bank(b, n * P, (n + 1) * P), ALU.mult, ALU.add).then_inc(sem["zs_ready"], 1)

                def softplus(t):
                    n = turns[t][1]
                    dve.wait_ge(sem["e_ready"], nth("e_ready", L, t + 1))
                    dve.scalar_tensor_tensor(sp_keep[t % 2][:, n * P:], zs[t % 3][:, n * P:], 0.0,
                                             ez[t % 2][:, n * P:], ALU.max, ALU.add)\
                       .then_inc(sem["sp_ready"], 1)

                def log_weight(t):
                    n = turns[t][1]
                    z = zs[t % 3][:, n * P:]
                    dve.wait_ge(sem["sfx_ready"], nth("sfx_ready", L, t + 1))
                    dve.tensor_tensor(z, z, bank(4 + t % 2, n * P), ALU.subtract)\
                       .then_inc(sem["lw_ready"], 1)

                def accumulate(t):
                    n = turns[t][1]
                    if n == 0:
                        return
                    dve.wait_ge(sem["sp_ready"], nth("sp_ready", L, t + 1))
                    own, keep = slice(n * P, (n + 1) * P), sp_keep[t % 2]
                    if n < 3:
                        later = slice((n + 1) * P, SEQ)
                        dve.tensor_tensor(acc[n % 2][:, later], acc[(n + 1) % 2][:, later],
                                          keep[:, later], ALU.add)\
                           .then_inc(sem["dve_step"], 1)
                        dve.wait_ge(sem["dve_step"], steps.next(L))
                    dve.tensor_copy(acc[n % 2][:, own], keep[:, own]).then_inc(sem["dve_step"], 1)
                    dve.wait_ge(sem["dve_step"], steps.next(L))

                def y_low(h):
                    dve.wait_ge(sem["yb_hi_ready"], nth("yb_hi_ready", L, h + 1))
                    dve.tensor_tensor(yb_lo[:, h, :], bank(6), yb_hi[:, h, :].bitcast(F32),
                                      ALU.subtract).then_inc(sem["yb_ready"], 1)

                scaled(0)
                for t in range(16):
                    if t + 1 < 16:
                        scaled(t + 1)
                    softplus(t)
                    if t >= 1:
                        log_weight(t - 1)
                    accumulate(t)
                    if t % 4 == 2 and t > 4:
                        y_low(t // 4 - 1)
                    for c in ended(t):
                        take_c(L, c)
                log_weight(15)
                take_c(L, C_CHUNKS - 1)
                y_low(3)

            def retention(L, steps):
                dve.wait_ge(late_in, 32)
                for c in range(4):
                    dve.wait_ge(sem["rx_ready"], nth("rx_ready", L, c + 1))
                    own, partner = dcy[c % 2][:, 0:SEQ], dcy[c % 2][:, SEQ:2 * SEQ]
                    dve.tensor_tensor(own, cq[:, c, :], rope[:, 0, :], ALU.mult)\
                       .then_inc(sem["dve_step"], 1)
                    dve.wait_ge(sem["dve_step"], steps.next(L))
                    dve.tensor_tensor(partner, bank(2 + c % 2), rope[:, 1, :], ALU.mult)\
                       .then_inc(sem["dve_step"], 1)
                    dve.wait_ge(sem["dve_step"], steps.next(L))
                    dve.tensor_tensor(cq[:, c, :], own, partner, ALU.add).then_inc(sem["rot_ready"], 1)
                dve.wait_ge(sem["rot_ready"], nth("rot_ready", L, 4))

                def decay_of(h):
                    if h >= 2:
                        dve.wait_ge(sem["ret_ready"], nth("ret_ready", L, h - 1))
                    for n in range(4):
                        at, w = (4 - n) * (3 - n) // 2 * P, (4 - n) * P
                        dve.wait_ge(sem["st_ready"], nth("st_ready", L, 4 * h + n + 1))
                        dve.tensor_tensor(dcy[h % 2][:, at:at + w], bank(2 + n % 2, n * P), decays[:, h, 0:w],
                                          ALU.mult).then_inc(sem["decay_ready"], 1)

                def gated(h):
                    dve.wait_ge(sem["csq_ready"], nth("csq_ready", L, h + 1))
                    if h == 0:
                        dve.wait_ge(sem["swish_ready"], nth("swish_ready", L, 1))
                    dve.scalar_tensor_tensor(og[h % 2][:], bank(6 + h % 2),
                                             vecs[:, bass.ds(V_RET + L * 4 + h, 1)], cg[:, h, :],
                                             ALU.mult, ALU.mult).then_inc(sem["gated_ready"], 1)

                def finish(h):
                    c, y = ct[h % 2], cy[h % 2]
                    dve.wait_ge(sem["cy0_ready"], nth("cy0_ready", L, h + 1))
                    if h >= 2:
                        dve.wait_ge(sem["yc_split"], nth("yc_split", L, h - 1))
                    dve.scalar_tensor_tensor(c[:], bank(1), EPS / PER_HEAD, y[:], ALU.add, ALU.mult)\
                       .then_inc(sem["var_used"], 1)
                    dve.wait_ge(sem["var_used"], nth("var_used", L, h + 1))
                    dve.scalar_tensor_tensor(c[:], c[:], -0.5 * PER_HEAD, y[:], ALU.mult, ALU.mult)\
                       .then_inc(sem["dve_step"], 1)
                    dve.wait_ge(sem["dve_step"], steps.next(L))
                    dve.scalar_tensor_tensor(c[:], c[:], 1.5, y[:], ALU.add, ALU.mult)\
                       .then_inc(sem["dve_step"], 1)
                    dve.wait_ge(sem["dve_step"], steps.next(L))
                    dve.wait_ge(sem["gated_ready"], nth("gated_ready", L, h + 1))
                    dve.tensor_tensor(c[:], c[:], og[h % 2][:], ALU.mult).then_inc(sem["yc_ready"], 1)

                def y_low(h):
                    dve.wait_ge(sem["yc_hi_ready"], nth("yc_hi_ready", L, h + 1))
                    dve.tensor_tensor(yc_lo[:, h, :], ct[h % 2][:], yc_hi[:, h, :].bitcast(F32),
                                      ALU.subtract).then_inc(sem["yc_split"], 1)

                decay_of(0)
                low_at(L, S_M + 2)
                decay_of(1)
                for h in range(4):
                    gated(h)
                    if h < 2:
                        decay_of(h + 2)
                    finish(h)
                    y_low(h)
                    if h == 2:
                        low_at(L, S_M + 3)

            def add_block(L, j, b, slab_end, n, scales):
                dve.wait_ge(sem["slab_used"], nth("slab_used", L, slab_end))
                dve.tensor_tensor(x[:, j, :], x[:, j, :], bank(b), ALU.add).then_inc(sem["x_new"], 1)
                dve.wait_ge(sem["h_hi_ready"], nth("h_hi_ready", L, n))
                dve.scalar_tensor_tensor(h_lo[:, j, :], x[:, j, :], vecs[:, bass.ds(scales, 1)],
                                         h_hi[:, j, :].bitcast(F32), ALU.mult, ALU.subtract)\
                   .then_inc(sem["h_ready"], 1)

            def add_square(L, p, n, norm):
                dve.wait_ge(sem["sq_ready"], nth("sq_ready", L, n))
                dve.wait_ge(sem["sum_added"], nth("sum_added", L, n - 1))
                dve.wait_ge(sem["sum_cleared"], nth("sum_cleared", L, norm))
                dve.tensor_tensor(sumsq[:], sumsq[:], square[p][:], ALU.add).then_inc(sem["sum_added"], 1)

            dve.memset(eps[:], EPS).then_inc(memset_done, 1)
            dve.memset(rel_ext[REL_BUCKETS:REL_BUCKETS + 1, :], MASKED).then_inc(memset_done, 1)
            for n in range(3):
                dve.wait_ge(line_mm, n + 1)
                dve.tensor_copy(lines[:, n * SEQ:(n + 1) * SEQ], ps[0:12, n, :]).then_inc(line_copied, 1)
            for k in range(KD):
                dve.wait_ge(sem["h_hi_ready"], k + 1)
                dve.scalar_tensor_tensor(h_lo[:, k, :], x[:, k, :], vecs[:, V_NORM + k:V_NORM + k + 1],
                                         h_hi[:, k, :].bitcast(F32), ALU.mult, ALU.subtract)\
                   .then_inc(sem["h_ready"], 1)
                dve.wait_ge(sem["sq_ready"], k + 1)
                if k >= 1:
                    dve.wait_ge(sem["sum_added"], k)
                    dve.tensor_tensor(sumsq[:], sumsq[:], square[k % 2][:], ALU.add)\
                       .then_inc(sem["sum_added"], 1)
                else:
                    dve.tensor_copy(sumsq[:], square[0][:]).then_inc(sem["sum_added"], 1)
                if k in (5, 7):
                    low_at(0, (k - 5) // 2)
            dve.wait_ge(const_in, 16 * 4)
            with dve.Fori(0, DEPTH) as L:
                steps = Steps("dve_step")
                root(L, 1, steps)
                dve.wait_ge(sem["rs_ready"], nth("rs_ready", L, 1))
                for v in range(V_A):
                    take(L, v, vs[v % 2][:], int(v >= 2), v=v)
                dve.wait_ge(line_out, 16)
                for c in range(6):
                    take(L, V_A + c, aq[:, c, :], -1, HD ** -0.5)
                for c in range(6):
                    take(L, V_A + 6 + c, ak[:, c, :], int(c >= 2))
                windows(L, steps)
                stick_breaking(L, steps)
                retention(L, steps)

                def merged(j, first):
                    for b in range(4):
                        s = 4 * j + (S_M + b)
                        if b < 3:
                            dve.wait_ge(sem["slab_used"], nth("slab_used", L, s + 1))
                            dve.tensor_tensor(sg[b][:], bank(GATE_BANKS[b]), rs[:], ALU.mult)\
                               .then_inc(sem["gate_scaled"], 1)
                        if b < 3 and not (first and b < 2):
                            low(L, s + 2, b % 2, (K_PROJ if b == 1 else KD) * P)
                    dve.wait_ge(sem["ab_done"], nth("ab_done", L, j + 1))
                    dve.wait_ge(sem["gate_ready"], nth("gate_ready", L, 3 * j + 3))
                    dve.wait_ge(sem["m_split"], nth("m_split", L, j))
                    dve.tensor_tensor(mt[0][:], bank(2), sg[0][:], ALU.mult)\
                       .then_inc(sem["dve_step"], 1)
                    dve.wait_ge(sem["dve_step"], steps.next(L))
                    dve.tensor_tensor(mt[1][:], bank(3), sg[1][:], ALU.mult)\
                       .then_inc(sem["dve_step"], 1)
                    dve.wait_ge(sem["dve_step"], steps.next(L))
                    dve.tensor_tensor(mt[0][:], mt[0][:], mt[1][:], ALU.add)\
                       .then_inc(sem["dve_step"], 1)
                    dve.wait_ge(sem["dve_step"], steps.next(L))
                    dve.wait_ge(sem["slab_used"], nth("slab_used", L, 4 * j + (S_M + 4)))
                    dve.tensor_tensor(mt[1][:], bank(1), sg[2][:], ALU.mult)\
                       .then_inc(sem["dve_step"], 1)
                    dve.wait_ge(sem["dve_step"], steps.next(L))
                    dve.tensor_tensor(mt[0][:], mt[0][:], mt[1][:], ALU.add).then_inc(sem["m_ready"], 1)
                    low(L, 4 * j + (S_M + 5), 1, KD * P)
                    dve.wait_ge(sem["m_hi_ready"], nth("m_hi_ready", L, j + 1))
                    dve.tensor_tensor(m_lo[:, j, :], mt[0][:], m_hi[:, j, :].bitcast(F32), ALU.subtract)\
                       .then_inc(sem["m_split"], 1)

                merged(0, True)
                with dve.Fori(1, KD) as j:
                    steps.enter(j - 1, 4)
                    merged(j, False)
                steps.leave(KD - 1)
                dve.memset(sumsq[:], 0.0).then_inc(sem["sum_cleared"], 1)
                with dve.Fori(0, KD // 2) as i:
                    for p in range(2):
                        add_block(L, 2 * i + p, p, 2 * i + (S_O + p + 1), 2 * i + (p + 1),
                                  V_NORM + L * (2 * KD) + 2 * i + (KD + p))
                        low(L, 2 * i + (S_O + p + 2), p, KD * P)
                        add_square(L, p, 2 * i + (p + 1), 1)
                root(L, 2, steps)

                def ffn_block(c, n):
                    dve.wait_ge(sem["rs_ready"], nth("rs_ready", L, 2))
                    dve.wait_ge(sem["slab_used"], nth("slab_used", L, 2 * c + (S_F + 1)))
                    dve.tensor_tensor(u[:], bank(0), rs[:], ALU.mult).then_inc(sem["u_ready"], 1)
                    low(L, 2 * c + (S_F + 2), 0, n)
                    dve.wait_ge(sem["cv_ready"], nth("cv_ready", L, c + 1))
                    at = V_CONV + L * (4 * KF) + 4 * c
                    dve.scalar_tensor_tensor(cv[:, 1:], u[:, 0:SEQ - 1],
                                             vecs[:, bass.ds(at + 1, 1)], cv[:, 1:],
                                             ALU.mult, ALU.add)\
                       .then_inc(sem["dve_step"], 1)
                    dve.wait_ge(sem["dve_step"], steps.next(L))
                    dve.scalar_tensor_tensor(cv[:, 2:], u[:, 0:SEQ - 2], vecs[:, bass.ds(at, 1)],
                                             cv[:, 2:], ALU.mult, ALU.add).then_inc(sem["conv_done"], 1)
                    dve.wait_ge(sem["slab_used"], nth("slab_used", L, 2 * c + (S_F + 2)))
                    dve.wait_ge(sem["af_split"], nth("af_split", L, c))
                    dve.tensor_tensor(af[:], bank(1), rs[:], ALU.mult).then_inc(sem["g_scaled"], 1)
                    low(L, 2 * c + (S_F + 3), 1, n)
                    dve.wait_ge(sem["g_scaled"], nth("g_scaled", L, c + 1))
                    dve.wait_ge(sem["gelu_ready"], nth("gelu_ready", L, c + 1))
                    dve.tensor_tensor(af[:], af[:], cv[:], ALU.mult).then_inc(sem["af_ready"], 1)
                    dve.wait_ge(sem["af_hi_ready"], nth("af_hi_ready", L, c + 1))
                    dve.tensor_tensor(act_lo[:, c, :], af[:], act_hi[:, c, :].bitcast(F32),
                                      ALU.subtract).then_inc(sem["af_split"], 1)

                with dve.Fori(0, KF - 1) as c:
                    steps.enter(c, 1)
                    ffn_block(c, KD * P)
                steps.leave(KF - 1)
                ffn_block(KF - 1, KHALF * P)
                dve.memset(sumsq[:], 0.0).then_inc(sem["sum_cleared"], 1)

                def down_pair(i, last):
                    for b in range(2):
                        n = (KD if last and b == 1 else KHALF) * P
                        low(L, 4 * i + (S_D + 2 * b + 2), 0, n)
                        add_block(L, 2 * i + b, b, 4 * i + (S_D + 2 * b + 2), 2 * i + (KD + b + 1),
                                  V_NORM + L * (2 * KD) + 2 * i + (2 * KD + b))
                        low(L, 4 * i + (S_D + 2 * b + 3), 1, n)
                        add_square(L, b, 2 * i + (KD + b + 1), 2)

                with dve.Fori(0, KD // 2 - 1) as i:
                    down_pair(i, False)
                down_pair(KD // 2 - 1, True)
                steps.end()
            root(DEPTH, 1, Steps("dve_step"))
            dve.wait_ge(sem["rs_ready"], nth("rs_ready", DEPTH, 1))
            for k in range(KD):
                at = V_NORM + 2 * DEPTH * KD + k
                dve.scalar_tensor_tensor(x[:, k, :], x[:, k, :], vecs[:, at:at + 1], rs[:],
                                         ALU.mult, ALU.mult).then_inc(out_ready, 1)


def bucket(distance):
    exact = REL_BUCKETS // 2
    n = np.maximum(distance, 0)
    large = exact + (np.log(np.maximum(n, 1) / exact) / np.log(REL_MAX_DIST / exact)
                     * (REL_BUCKETS - exact)).astype(np.int64)
    return np.where(n < exact, n, np.minimum(large, REL_BUCKETS - 1)).astype(np.int64)


def bias_lines():
    i1, i2 = np.arange(LINE1), np.arange(LINE2)
    d1, d2 = 511 - i1, 127 - i2
    parts = [(bucket(d1), (d1 >= 0) & (d1 <= 128)), (bucket(4 * d2), d2 >= 0),
             (bucket(4 * d2), (d2 >= 0) & (d2 % 4 == 0))]
    rows = np.concatenate([np.where(ok, b, REL_BUCKETS) for b, ok in parts])
    return (np.arange(REL_BUCKETS + 1)[:, None] == rows[None, :]).astype(np.float32)


def matrices():
    a, b = np.arange(P)[:, None], np.arange(P)[None, :]
    one = np.ones((P, P), np.float32)
    turn = np.where((b % HD < HD // 2) & (a == b + HD // 2), -1.0, 0.0)
    turn = np.where((b % HD >= HD // 2) & (a == b - HD // 2), 1.0, turn)
    return np.stack([one, one / D_MODEL, (a >= b) * one, (a == b) * one, turn * one,
                     (a == b) - one / P, (a + b == P - 1) * one], 1).astype(np.float32)


def decay_tables():
    gamma = np.log1p(-np.exp2(-5.0 - np.arange(4, dtype=np.float64)))
    d = np.arange(SEQ)[None, :] - np.arange(P)[:, None]
    return np.stack([np.where(d >= 0, np.exp(np.maximum(d, 0) * g), 0.0) for g in gamma], 1)\
        .astype(np.float32)


def rope_tables():
    half = HD // 2
    inv = (np.float32(10000.0) ** (-np.arange(half, dtype=np.float32) / np.float32(half))).astype(np.float32)
    angle = np.arange(SEQ, dtype=np.float32)[None, :] * inv[:, None]
    angle = np.tile(angle.astype(np.float64), (P // half, 1))
    return np.stack([np.cos(angle), np.sin(angle)], 1).astype(np.float32)


def slabs(w, order=None):
    n, rows, columns = w.shape
    w = w.reshape(n, rows // P, P, columns // P, P).transpose(0, 3, 2, 1, 4)
    if order is not None:
        w = w[:, order]
    return w.reshape(n, -1, P, rows)


def halves(w):
    n, c, p, e = w.shape
    return w.reshape(n, c, p, 2, e // 2).transpose(0, 1, 3, 2, 4).reshape(n, 2 * c, p, e // 2)


def columns(v):
    return v.reshape(-1, P).T


def kernel(x, rel_bias, norm_mix_w, w_in, b_gate, ret_norm_w, w_proj_a, w_proj_b, w_proj_c,
           w_out, norm_ffn_w, w_up, w_gate, conv_w, conv_b, w_down, final_norm_w):
    import concourse.bacc as bacc
    from concourse.bass_utils import run_bass_kernel_spmd

    a = {k: np.asarray(v) for k, v in locals().items() if k not in ("bacc", "run_bass_kernel_spmd")}
    order = (list(range(12, 18)) + list(range(12)) + list(range(26, 30)) + list(range(18, 26))
             + list(range(34, 38)) + list(range(30, 34)) + list(range(38, 42)))
    gates = slabs(a["w_in"][:, :, S_M * P:]).reshape(DEPTH, 3, KD, P, KD * P).transpose(0, 2, 1, 3, 4)
    upgate = np.stack([slabs(a["w_up"]), slabs(a["w_gate"])], 2)
    norms = np.concatenate([np.stack([a["norm_mix_w"], a["norm_ffn_w"]], 1).ravel(), a["final_norm_w"]])
    conv = np.concatenate([a["conv_w"], a["conv_b"][:, None]], 1).reshape(DEPTH, 4, KF, P)
    arrays = {
        "x_t": a["x"][0].reshape(SEQ, KD, P).transpose(2, 1, 0),
        "vectors": np.concatenate([
            columns(norms), columns(a["b_gate"].reshape(DEPTH, 3, KD, P).transpose(0, 2, 1, 3)),
            columns(conv.transpose(0, 2, 1, 3)), columns(a["ret_norm_w"])], 1),
        "rel_bias": a["rel_bias"],
        "onehot": bias_lines(), "mats": matrices(), "decay": decay_tables(), "cos_sin": rope_tables(),
        "w_qkv": slabs(a["w_in"][:, :, :S_M * P], order).reshape(-1, P, KD * P),
        "w_gates": gates.reshape(-1, P, KD * P),
        "w_proj": np.concatenate([slabs(a["w_proj_a"]), slabs(a["w_proj_b"]), slabs(a["w_proj_c"])], 3)
        .reshape(-1, P, K_PROJ * P),
        "w_o": slabs(a["w_out"]).reshape(-1, P, KD * P),
        "w_upgate": upgate.reshape(-1, P, KD * P),
        "w_down": halves(slabs(a["w_down"])).reshape(-1, P, KHALF * P),
    }
    arrays = {k: np.ascontiguousarray(v) for k, v in arrays.items()}
    nc = bacc.Bacc("TRN2", target_bir_lowering=False, num_devices=1)
    args = [nc.dram_tensor(k, v.shape, F32, kind="ExternalInput").ap() for k, v in arrays.items()]
    line = nc.dram_tensor("line_dram", (12, LINE), F32, kind="Internal").ap()
    out = nc.dram_tensor("out_t", (P, KD, SEQ), F32, kind="ExternalOutput").ap()
    trunk_program(nc, *args, line, out)
    result = run_bass_kernel_spmd(nc, [arrays], core_ids=[0]).results[0]["out_t"]
    return result.transpose(2, 1, 0).reshape(1, SEQ, D_MODEL)
```
